# Optimizing a Trainium2 kernel written in Bass

```python
import math
import numpy as np
import jax
import jax.numpy as jnp
from jax import lax
import jax, jax.numpy as jnp

D_MODEL = 1024
BATCH = 1
SEQ = 256
DEPTH = 2

DA_HEADS = 4
DA_HEAD_DIM = 64
DA_WIDTH = DA_HEADS * 2 * DA_HEAD_DIM
Q_BLOCK = 128
ROPE_THETA = 10000.0
DN_HEADS = 4
DN_HEAD_DIM = 128
DN_WIDTH = DN_HEADS * DN_HEAD_DIM
CONV_K = 5
CHUNK = 64
D_FF = 4 * D_MODEL
EPS = 1e-6
IN_SPLITS = (DA_WIDTH, DA_WIDTH, DA_WIDTH, DN_WIDTH, DN_WIDTH, DN_WIDTH, DN_WIDTH,
             2 * DN_HEADS, 2 * DN_HEADS, 2 * D_MODEL)
IN_COLS = sum(IN_SPLITS)


def rms_norm(x, gain):
    x32 = x.astype(jnp.float32)
    y = x32 * lax.rsqrt(jnp.mean(x32 * x32, axis=-1, keepdims=True) + EPS)
    return (y * gain.astype(jnp.float32)).astype(x.dtype)

def l2_norm(x):
    x32 = x.astype(jnp.float32)
    return (x32 * lax.rsqrt(jnp.sum(x32 * x32, axis=-1, keepdims=True) + EPS)).astype(x.dtype)

def rope_tables(seq, dim, dtype):
    pos = jnp.arange(seq, dtype=jnp.float32)
    inv = 1.0 / (ROPE_THETA ** (jnp.arange(0, dim, 2, dtype=jnp.float32) / dim))
    ang = pos[:, None] * inv[None, :]
    ang = jnp.concatenate([ang, ang], axis=-1)
    return jnp.cos(ang).astype(dtype), jnp.sin(ang).astype(dtype)

def apply_rope(x, cos, sin):
    half = x.shape[-1] // 2
    rot = jnp.concatenate([-x[..., half:], x[..., :half]], axis=-1)
    return x * cos + rot * sin

def diff_attention(q, k, v, lam, lambda_init, cos, sin, qn_gain, kn_gain, subln_gain):
    B, S, H, _, d = q.shape
    q = apply_rope(rms_norm(q, qn_gain).transpose(0, 2, 3, 1, 4), cos, sin)
    k = apply_rope(rms_norm(k, kn_gain).transpose(0, 2, 3, 1, 4), cos, sin)
    v = v.transpose(0, 2, 1, 3)
    nb = S // Q_BLOCK
    qb = q.reshape(B, H, 2, nb, Q_BLOCK, d).transpose(3, 0, 1, 2, 4, 5)
    scale = d ** -0.5

    def block(qi):
        s = jnp.einsum('bhtqd,bhtkd->bhtqk', qi, k).astype(jnp.float32) * scale
        p = jax.nn.softmax(s, axis=-1)
        a = p[:, :, 0] - lam * p[:, :, 1]
        return jnp.einsum('bhqk,bhkd->bhqd', a.astype(v.dtype), v)

    o = lax.map(block, qb)
    o = o.transpose(1, 0, 3, 2, 4).reshape(B, S, H, 2 * d)
    o = rms_norm(o, subln_gain) * (1.0 - lambda_init)
    return o.reshape(B, S, H * 2 * d)

def gated_delta_rule_chunked(q, k, v, g, beta):
    out_dtype = v.dtype
    q, k, v, g, beta = [t.astype(jnp.float32) for t in (q, k, v, g, beta)]
    B, H, S, Dk = q.shape
    Dv = v.shape[-1]
    n = S // CHUNK
    q = q.reshape(B, H, n, CHUNK, Dk)
    k = k.reshape(B, H, n, CHUNK, Dk)
    v = v.reshape(B, H, n, CHUNK, Dv)
    beta = beta.reshape(B, H, n, CHUNK)
    g = jnp.cumsum(g.reshape(B, H, n, CHUNK), axis=-1)
    idx = jnp.arange(CHUNK)
    incl = idx[:, None] >= idx[None, :]
    strict = idx[:, None] > idx[None, :]
    gdiff = g[..., :, None] - g[..., None, :]
    decay = jnp.where(incl, jnp.exp(jnp.where(incl, gdiff, 0.0)), 0.0)
    kb = k * beta[..., None]
    L = jnp.where(strict, jnp.einsum('bhncd,bhnmd->bhncm', kb, k) * decay, 0.0)
    eye = jnp.eye(CHUNK, dtype=jnp.float32)
    T = lax.linalg.triangular_solve(eye + L, jnp.broadcast_to(eye, L.shape), left_side=True,
                                    lower=True, unit_diagonal=True)
    u = jnp.einsum('bhncm,bhnme->bhnce', T, v * beta[..., None])
    w = jnp.einsum('bhncm,bhnmd->bhncd', T, kb * jnp.exp(g)[..., None])
    qk = jnp.einsum('bhncd,bhnmd->bhncm', q, k) * decay
    q_dec = q * jnp.exp(g)[..., None]
    k_dec = k * jnp.exp(g[..., -1:] - g)[..., None]
    g_last = jnp.exp(g[..., -1])

    def step(state, inp):
        qd_i, kd_i, u_i, w_i, qk_i, gl_i = inp
        v_new = u_i - jnp.einsum('bhcd,bhde->bhce', w_i, state)
        o_i = jnp.einsum('bhcd,bhde->bhce', qd_i, state) + jnp.einsum('bhcm,bhme->bhce', qk_i, v_new)
        state = state * gl_i[..., None, None] + jnp.einsum('bhcd,bhce->bhde', kd_i, v_new)
        return state, o_i

    xs = (jnp.moveaxis(q_dec, 2, 0), jnp.moveaxis(k_dec, 2, 0), jnp.moveaxis(u, 2, 0),
          jnp.moveaxis(w, 2, 0), jnp.moveaxis(qk, 2, 0), jnp.moveaxis(g_last, 2, 0))
    state0 = jnp.zeros((B, H, Dk, Dv), jnp.float32)
    _, o = lax.scan(step, state0, xs)
    return jnp.moveaxis(o, 0, 2).reshape(B, H, S, Dv).astype(out_dtype)

def gated_deltanet(q, k, v, z, b, a, conv_w, A_log, dt_bias, out_gain):
    B, S, _ = q.shape
    qkv = jnp.concatenate([q, k, v], axis=-1)
    qkv = lax.conv_general_dilated(qkv, conv_w[:, None, :].astype(qkv.dtype), window_strides=(1,),
                                   padding=[(CONV_K // 2, CONV_K // 2)],
                                   dimension_numbers=('NWC', 'WIO', 'NWC'),
                                   feature_group_count=qkv.shape[-1])
    q, k, v = jnp.split(jax.nn.silu(qkv), 3, axis=-1)

    def heads(t):
        return t.reshape(B, S, DN_HEADS, DN_HEAD_DIM).transpose(0, 2, 1, 3)

    q = l2_norm(heads(q)) * (DN_HEAD_DIM ** -0.5)
    k = l2_norm(heads(k))
    v = heads(v)
    beta = jax.nn.sigmoid(b.astype(jnp.float32)).reshape(B, S, 2, DN_HEADS).transpose(2, 0, 3, 1)
    a_in = a.astype(jnp.float32).reshape(B, S, 2, DN_HEADS).transpose(2, 0, 3, 1)
    g = -jnp.exp(A_log.astype(jnp.float32))[:, None, :, None] * jax.nn.softplus(
        a_in + dt_bias.astype(jnp.float32)[:, None, :, None])
    o_fwd = gated_delta_rule_chunked(q, k, v, g[0], beta[0])
    o_bwd = jnp.flip(gated_delta_rule_chunked(jnp.flip(q, 2), jnp.flip(k, 2), jnp.flip(v, 2),
                                              jnp.flip(g[1], 2), jnp.flip(beta[1], 2)), 2)
    o = (o_fwd + o_bwd).transpose(0, 2, 1, 3)
    o = rms_norm(o, out_gain) * jax.nn.silu(z.reshape(B, S, DN_HEADS, DN_HEAD_DIM))
    return o.reshape(B, S, DN_WIDTH)

def first_inputs(seed: int = 0) -> dict:
    key = jax.random.key(seed)
    ks = jax.random.split(key, 20)
    f32 = jnp.float32

    def nrm(k, shape, scale):
        return jax.random.normal(k, shape, f32) * scale

    x = nrm(ks[0], (BATCH, SEQ, D_MODEL), 1.0)
    c = nrm(ks[1], (BATCH, D_MODEL), 1.0)
    ada_w = nrm(ks[2], (DEPTH, D_MODEL, 6 * D_MODEL), D_MODEL ** -0.5)
    ada_b = nrm(ks[3], (DEPTH, 6 * D_MODEL), 0.02)
    norm1_g = 1.0 + nrm(ks[4], (DEPTH, D_MODEL), 0.05)
    norm2_g = 1.0 + nrm(ks[5], (DEPTH, D_MODEL), 0.05)
    w_in = nrm(ks[6], (DEPTH, D_MODEL, IN_COLS), D_MODEL ** -0.5)
    dn_conv = nrm(ks[7], (DEPTH, CONV_K, 3 * DN_WIDTH), CONV_K ** -0.5)
    dn_A_log = jnp.log(jax.random.uniform(ks[8], (DEPTH, 2, DN_HEADS), f32, 1.0, 16.0))
    dt = jnp.exp(jax.random.uniform(ks[9], (DEPTH, 2, DN_HEADS), f32, math.log(1e-3), math.log(1e-1)))
    dn_dt_bias = dt + jnp.log(-jnp.expm1(-dt))
    dn_out_gain = 1.0 + nrm(ks[10], (DEPTH, DN_HEAD_DIM), 0.05)
    qk_norm_gain = 1.0 + nrm(ks[11], (DEPTH, 2, DA_HEAD_DIM), 0.05)
    diff_lambda = nrm(ks[12], (DEPTH, 4, DA_HEAD_DIM), 0.1)
    diff_subln_gain = 1.0 + nrm(ks[13], (DEPTH, 2 * DA_HEAD_DIM), 0.05)
    w_branch_a = nrm(ks[14], (DEPTH, DA_WIDTH, D_MODEL), DA_WIDTH ** -0.5)
    w_branch_b = nrm(ks[15], (DEPTH, DN_WIDTH, D_MODEL), DN_WIDTH ** -0.5)
    w_out = nrm(ks[16], (DEPTH, D_MODEL, D_MODEL), D_MODEL ** -0.5)
    w_mlp1 = nrm(ks[17], (DEPTH, D_MODEL, D_FF), D_MODEL ** -0.5)
    w_mlp2 = nrm(ks[18], (DEPTH, D_FF, D_MODEL), D_FF ** -0.5)
    return {'x': x, 'c': c, 'ada_w': ada_w, 'ada_b': ada_b, 'norm1_g': norm1_g, 'norm2_g': norm2_g,
            'w_in': w_in, 'dn_conv': dn_conv, 'dn_A_log': dn_A_log, 'dn_dt_bias': dn_dt_bias,
            'dn_out_gain': dn_out_gain, 'qk_norm_gain': qk_norm_gain, 'diff_lambda': diff_lambda,
            'diff_subln_gain': diff_subln_gain, 'w_branch_a': w_branch_a, 'w_branch_b': w_branch_b,
            'w_out': w_out, 'w_mlp1': w_mlp1, 'w_mlp2': w_mlp2}

def first_block(x, c, ada_w, ada_b, norm1_g, norm2_g, w_in, dn_conv, dn_A_log, dn_dt_bias, dn_out_gain,
              qk_norm_gain, diff_lambda, diff_subln_gain, w_branch_a, w_branch_b, w_out, w_mlp1, w_mlp2):
    B, S, D = x.shape
    cos, sin = rope_tables(S, DA_HEAD_DIM, x.dtype)
    split_points = [int(p) for p in np.cumsum(IN_SPLITS)[:-1]]
    c_act = jax.nn.silu(c)
    for l in range(DEPTH):
        mod = c_act @ ada_w[l] + ada_b[l]
        sh1, sc1, gt1, sh2, sc2, gt2 = [m[:, None, :] for m in jnp.split(mod, 6, axis=-1)]
        h = rms_norm(x, norm1_g[l]) * (1.0 + sc1) + sh1
        proj = h @ w_in[l]
        da_q, da_k, da_v, dn_q, dn_k, dn_v, dn_z, dn_b, dn_a, gates = jnp.split(proj, split_points, axis=-1)
        lambda_init = 0.8 - 0.6 * math.exp(-0.3 * l)
        lq = diff_lambda[l].astype(jnp.float32)
        lam = jnp.exp(jnp.sum(lq[0] * lq[1])) - jnp.exp(jnp.sum(lq[2] * lq[3])) + lambda_init
        y_a = diff_attention(da_q.reshape(B, S, DA_HEADS, 2, DA_HEAD_DIM),
                             da_k.reshape(B, S, DA_HEADS, 2, DA_HEAD_DIM),
                             da_v.reshape(B, S, DA_HEADS, 2 * DA_HEAD_DIM),
                             lam, lambda_init, cos, sin, qk_norm_gain[l, 0], qk_norm_gain[l, 1],
                             diff_subln_gain[l])
        y_b = gated_deltanet(dn_q, dn_k, dn_v, dn_z, dn_b, dn_a, dn_conv[l], dn_A_log[l], dn_dt_bias[l],
                             dn_out_gain[l])
        g_a, g_b = jnp.split(jax.nn.sigmoid(gates), 2, axis=-1)
        merged = g_a * (y_a @ w_branch_a[l]) + g_b * (y_b @ w_branch_b[l])
        x = x + gt1 * (merged @ w_out[l])
        h = rms_norm(x, norm2_g[l]) * (1.0 + sc2) + sh2
        x = x + gt2 * (jnp.square(jax.nn.relu(h @ w_mlp1[l])) @ w_mlp2[l])
    return x


HEAD_DIM = 64
GRID_W = 64
NA_HEADS = D_MODEL // (4 * HEAD_DIM)
NA_WIN_H = 8
NA_WIN_W = 16
MLA_HEADS = 3 * D_MODEL // (8 * HEAD_DIM)
MLA_Q_LORA = D_MODEL // 4
MLA_KV_LORA = D_MODEL // 8
MLA_NOPE = 64
MLA_ROPE = 32
MLA_V = 64
MLA_BLOCK = 128
SWA_HEADS = 3 * D_MODEL // (8 * HEAD_DIM)
SWA_KV_HEADS = 2
SWA_WINDOW = 128
SWA_BLOCK = 128
N_EXPERTS = 16
EC_CAPACITY = 2
D_EXPERT = D_MODEL
RMS_EPS = 1e-6
NEG_INF = -1e30

A_W = NA_HEADS * HEAD_DIM
B_W = MLA_HEADS * MLA_V
C_W = SWA_HEADS * HEAD_DIM
D_MIX = A_W + B_W + C_W
IN_WIDTHS = (A_W, A_W, A_W,
             MLA_Q_LORA, MLA_KV_LORA, MLA_ROPE,
             SWA_HEADS * HEAD_DIM, SWA_KV_HEADS * HEAD_DIM, SWA_KV_HEADS * HEAD_DIM)
IN_COLS_2 = sum(IN_WIDTHS)
IN_OFFSETS = tuple(int(v) for v in np.cumsum(IN_WIDTHS)[:-1])


def rms_norm_2(x, g):
    x32 = x.astype(jnp.float32)
    y = x32 * lax.rsqrt(jnp.mean(x32 * x32, axis=-1, keepdims=True) + RMS_EPS)
    return (y * g.astype(jnp.float32)).astype(x.dtype)

def rope_tables_2(seq, dim, dtype):
    inv = 1.0 / (ROPE_THETA ** (jnp.arange(0, dim, 2, dtype=jnp.float32) / dim))
    ang = jnp.arange(seq, dtype=jnp.float32)[:, None] * inv[None, :]
    return jnp.cos(ang).astype(dtype), jnp.sin(ang).astype(dtype)

def apply_rope_2(x, cos, sin):
    x1, x2 = jnp.split(x, 2, axis=-1)
    c = cos[None, :, None, :]
    s = sin[None, :, None, :]
    return jnp.concatenate([x1 * c - x2 * s, x2 * c + x1 * s], axis=-1)

def neighbourhood_attention(q, k, v, rpb):
    B, S, _ = q.shape
    rows = S // GRID_W
    wh = min(NA_WIN_H, rows)
    ww = NA_WIN_W
    shp = (B, rows, GRID_W, NA_HEADS, HEAD_DIM)
    qg, kg, vg = q.reshape(shp), k.reshape(shp), v.reshape(shp)
    cols = jnp.arange(GRID_W)
    col_start = jnp.clip(cols - ww // 2, 0, GRID_W - ww)
    col_idx = col_start[:, None] + jnp.arange(ww)[None, :]
    dc = col_idx - cols[:, None] + (NA_WIN_W - 1)
    scale = HEAD_DIM ** -0.5

    def one_row(args):
        r, q_row = args
        rs = jnp.clip(r - wh // 2, 0, rows - wh)
        k_rows = lax.dynamic_slice_in_dim(kg, rs, wh, axis=1)
        v_rows = lax.dynamic_slice_in_dim(vg, rs, wh, axis=1)
        k_win = k_rows[:, :, col_idx]
        v_win = v_rows[:, :, col_idx]
        dr = rs + jnp.arange(wh) - r + (NA_WIN_H - 1)
        bias = rpb[:, dr][:, :, dc].transpose(0, 2, 1, 3)
        s = jnp.einsum('bchd,brcjhd->bhcrj', q_row, k_win).astype(jnp.float32) * scale
        s = s + bias[None].astype(jnp.float32)
        p = jax.nn.softmax(s.reshape(B, NA_HEADS, GRID_W, wh * ww), axis=-1)
        p = p.reshape(s.shape).astype(v.dtype)
        return jnp.einsum('bhcrj,brcjhd->bchd', p, v_win)

    out = lax.map(one_row, (jnp.arange(rows), qg.swapaxes(0, 1)))
    return out.swapaxes(0, 1).reshape(B, S, NA_HEADS * HEAD_DIM)

def latent_attention(c_q, c_kv, k_rope, q_norm, w_uq, kv_norm, w_ukv, cos_r, sin_r):
    B, S, _ = c_q.shape
    q = (rms_norm_2(c_q, q_norm) @ w_uq).reshape(B, S, MLA_HEADS, MLA_NOPE + MLA_ROPE)
    q_nope = q[..., :MLA_NOPE]
    q_pe = apply_rope_2(q[..., MLA_NOPE:], cos_r, sin_r)
    kv = (rms_norm_2(c_kv, kv_norm) @ w_ukv).reshape(B, S, MLA_HEADS, MLA_NOPE + MLA_V)
    k_nope = kv[..., :MLA_NOPE]
    v = kv[..., MLA_NOPE:]
    k_pe = apply_rope_2(k_rope[:, :, None, :], cos_r, sin_r)[:, :, 0]
    nb = S // MLA_BLOCK
    scale = (MLA_NOPE + MLA_ROPE) ** -0.5

    def to_blocks(t):
        return t.reshape(B, nb, MLA_BLOCK, *t.shape[2:]).swapaxes(0, 1)

    def one_block(args):
        qn, qp = args
        s = (jnp.einsum('bqhd,bkhd->bhqk', qn, k_nope)
             + jnp.einsum('bqhd,bkd->bhqk', qp, k_pe)).astype(jnp.float32) * scale
        p = jax.nn.softmax(s, axis=-1).astype(v.dtype)
        return jnp.einsum('bhqk,bkhd->bqhd', p, v)

    o = lax.map(one_block, (to_blocks(q_nope), to_blocks(q_pe)))
    return o.swapaxes(0, 1).reshape(B, S, MLA_HEADS * MLA_V)

def window_gqa(q, k, v, sink, cos, sin):
    B, S, _ = q.shape
    G = SWA_HEADS // SWA_KV_HEADS
    q = apply_rope_2(q.reshape(B, S, SWA_HEADS, HEAD_DIM), cos, sin)
    k = apply_rope_2(k.reshape(B, S, SWA_KV_HEADS, HEAD_DIM), cos, sin)
    v = v.reshape(B, S, SWA_KV_HEADS, HEAD_DIM)
    nb = S // SWA_BLOCK
    n_side = -(-SWA_WINDOW // SWA_BLOCK)
    pad = n_side * SWA_BLOCK
    n_keys = (2 * n_side + 1) * SWA_BLOCK

    def band(t):
        tp = jnp.pad(t, ((0, 0), (pad, pad), (0, 0), (0, 0)))
        tp = tp.reshape(B, nb + 2 * n_side, SWA_BLOCK, SWA_KV_HEADS, HEAD_DIM)
        return jnp.concatenate([tp[:, i:i + nb] for i in range(2 * n_side + 1)], axis=2)

    kb, vb = band(k), band(v)
    qb = q.reshape(B, nb, SWA_BLOCK, SWA_KV_HEADS, G, HEAD_DIM)
    s = jnp.einsum('bnqkgd,bnjkd->bnkgqj', qb, kb).astype(jnp.float32) * (HEAD_DIM ** -0.5)
    blk = jnp.arange(nb)[:, None, None] * SWA_BLOCK
    qpos = blk + jnp.arange(SWA_BLOCK)[None, :, None]
    kpos = blk - pad + jnp.arange(n_keys)[None, None, :]
    valid = (jnp.abs(qpos - kpos) <= SWA_WINDOW) & (kpos >= 0) & (kpos < S)
    s = jnp.where(valid[None, :, None, None], s, NEG_INF)
    sink_logit = jnp.broadcast_to(sink.astype(jnp.float32).reshape(1, 1, SWA_KV_HEADS, G, 1, 1),
                                  s.shape[:-1] + (1,))
    p = jax.nn.softmax(jnp.concatenate([s, sink_logit], axis=-1), axis=-1)[..., :-1].astype(v.dtype)
    o = jnp.einsum('bnkgqj,bnjkd->bnqkgd', p, vb)
    return o.reshape(B, S, SWA_HEADS * HEAD_DIM)

def expert_choice_ffn(xn, w_router, w_gate, w_up, w_down):
    B, S, D = xn.shape
    cap = EC_CAPACITY * S // N_EXPERTS
    aff = jax.nn.softmax((xn @ w_router).astype(jnp.float32), axis=-1)
    g, idx = lax.top_k(aff.swapaxes(1, 2), cap)
    bidx = jnp.arange(B)[:, None, None]
    xs = xn[bidx, idx]
    hid = jax.nn.silu(jnp.einsum('becd,edf->becf', xs, w_gate)) * jnp.einsum('becd,edf->becf', xs, w_up)
    y = jnp.einsum('becf,efd->becd', hid, w_down) * g[..., None].astype(xn.dtype)
    return jnp.zeros_like(xn).at[bidx, idx].add(y)

def second_inputs(seed: int = 0) -> dict:
    key = jax.random.key(seed)
    ks = jax.random.split(key, 17)
    f32 = jnp.float32

    def nrm(k, shape, scale):
        return jax.random.normal(k, shape, f32) * scale

    def gain(k, shape):
        return 1.0 + 0.05 * jax.random.normal(k, shape, f32)

    return {
        'x': nrm(ks[0], (BATCH, SEQ, D_MODEL), 1.0),
        'attn_norm': gain(ks[1], (DEPTH, D_MODEL)),
        'w_in': nrm(ks[2], (DEPTH, D_MODEL, IN_COLS_2), D_MODEL ** -0.5),
        'na_rpb': nrm(ks[3], (DEPTH, NA_HEADS, 2 * NA_WIN_H - 1, 2 * NA_WIN_W - 1), 0.1),
        'mla_q_norm': gain(ks[4], (DEPTH, MLA_Q_LORA)),
        'mla_w_uq': nrm(ks[5], (DEPTH, MLA_Q_LORA, MLA_HEADS * (MLA_NOPE + MLA_ROPE)), MLA_Q_LORA ** -0.5),
        'mla_kv_norm': gain(ks[6], (DEPTH, MLA_KV_LORA)),
        'mla_w_ukv': nrm(ks[7], (DEPTH, MLA_KV_LORA, MLA_HEADS * (MLA_NOPE + MLA_V)), MLA_KV_LORA ** -0.5),
        'swa_sink': nrm(ks[8], (DEPTH, SWA_HEADS), 1.0),
        'group_norm': gain(ks[9], (DEPTH, D_MIX)),
        'w_out': nrm(ks[10], (DEPTH, D_MIX, D_MODEL), D_MIX ** -0.5),
        'ffn_norm': gain(ks[11], (DEPTH, D_MODEL)),
        'w_router': nrm(ks[12], (DEPTH, D_MODEL, N_EXPERTS), D_MODEL ** -0.5),
        'w_gate': nrm(ks[13], (DEPTH, N_EXPERTS, D_MODEL, D_EXPERT), D_MODEL ** -0.5),
        'w_up': nrm(ks[14], (DEPTH, N_EXPERTS, D_MODEL, D_EXPERT), D_MODEL ** -0.5),
        'w_down': nrm(ks[15], (DEPTH, N_EXPERTS, D_EXPERT, D_MODEL), D_EXPERT ** -0.5),
        'final_norm': gain(ks[16], (D_MODEL,)),
    }

def second_block(x, attn_norm, w_in, na_rpb, mla_q_norm, mla_w_uq, mla_kv_norm, mla_w_ukv, swa_sink,
              group_norm, w_out, ffn_norm, w_router, w_gate, w_up, w_down, final_norm):
    B, S, _ = x.shape
    cos, sin = rope_tables_2(S, HEAD_DIM, x.dtype)
    cos_r, sin_r = rope_tables_2(S, MLA_ROPE, x.dtype)
    h = x
    for l in range(DEPTH):
        xn = rms_norm_2(h, attn_norm[l])
        proj = xn @ w_in[l]
        a_q, a_k, a_v, b_cq, b_ckv, b_kr, c_q, c_k, c_v = jnp.split(proj, IN_OFFSETS, axis=-1)
        o_a = neighbourhood_attention(a_q, a_k, a_v, na_rpb[l])
        o_b = latent_attention(b_cq, b_ckv, b_kr, mla_q_norm[l], mla_w_uq[l],
                               mla_kv_norm[l], mla_w_ukv[l], cos_r, sin_r)
        o_c = window_gqa(c_q, c_k, c_v, swa_sink[l], cos, sin)
        gn = group_norm[l]
        o = jnp.concatenate([rms_norm_2(o_a, gn[:A_W]),
                             rms_norm_2(o_b, gn[A_W:A_W + B_W]),
                             rms_norm_2(o_c, gn[A_W + B_W:])], axis=-1)
        h = h + o @ w_out[l]
        h = h + expert_choice_ffn(rms_norm_2(h, ffn_norm[l]), w_router[l], w_gate[l], w_up[l], w_down[l])
    return rms_norm_2(h, final_norm)


def setup_inputs(seed=0):
    out = dict(first_inputs(seed))
    for name, value in second_inputs(seed + 1).items():
        if name != "x":
            out[name + "_2"] = value
    return out


def reference(
    x, c, ada_w, ada_b, norm1_g, norm2_g, w_in, dn_conv, dn_A_log, dn_dt_bias, dn_out_gain,
    qk_norm_gain, diff_lambda, diff_subln_gain, w_branch_a, w_branch_b, w_out, w_mlp1, w_mlp2,
    attn_norm_2, w_in_2, na_rpb_2, mla_q_norm_2, mla_w_uq_2, mla_kv_norm_2, mla_w_ukv_2,
    swa_sink_2, group_norm_2, w_out_2, ffn_norm_2, w_router_2, w_gate_2, w_up_2, w_down_2,
    final_norm_2,
):
    x = first_block(
        x, c, ada_w, ada_b, norm1_g, norm2_g, w_in, dn_conv, dn_A_log, dn_dt_bias, dn_out_gain,
        qk_norm_gain, diff_lambda, diff_subln_gain, w_branch_a, w_branch_b, w_out, w_mlp1,
        w_mlp2,
    )
    return second_block(
        x, attn_norm_2, w_in_2, na_rpb_2, mla_q_norm_2, mla_w_uq_2, mla_kv_norm_2, mla_w_ukv_2,
        swa_sink_2, group_norm_2, w_out_2, ffn_norm_2, w_router_2, w_gate_2, w_up_2, w_down_2,
        final_norm_2,
    )


_drawn_inputs = setup_inputs


def setup_inputs(seed=0):
    import zlib

    import numpy as np

    out = dict(_drawn_inputs(seed))
    spreads = {}
    factors = {'dn_out_gain': 3.182,
     'qk_norm_gain': 8.0,
     'diff_lambda': 8.0,
     'diff_subln_gain': 3.013,
     'na_rpb_2': 7.695,
     'mla_q_norm_2': 8.0,
     'mla_kv_norm_2': 2.67,
     'swa_sink_2': 8.0,
     'ffn_norm_2': 3.745}
    for name, (base, spread) in spreads.items():
        noise = np.random.default_rng([zlib.crc32(name.encode()), seed]).standard_normal(out[name].shape)
        drawn = base * np.exp(spread * noise) if base else spread * noise
        out[name] = jnp.asarray(drawn.astype(out[name].dtype))
    for name, factor in factors.items():
        out[name] = (out[name] * factor).astype(out[name].dtype)
    return out
```

```python
import math
from contextlib import ExitStack

import numpy as np
import concourse.bass as bass
from concourse import mybir

F32 = mybir.dt.float32
ALU = mybir.AluOpType
ACT = mybir.ActivationFunctionType
AX = mybir.AxisListType
EPS = 1e-6
NR = 4


def const_arrays():
    i = np.arange(128)
    m, c = i[:, None], i[None, :]
    same = (m // 64) == (c // 64)
    cols = {}
    cols["ident"] = (m == c)
    cols["ones"] = np.ones((128, 128))
    cols["triF"] = same & (m <= c)
    cols["triB"] = same & (m >= c)
    cols["blk"] = same
    cols["half0"] = (m < 64) & (c >= 0)
    cols["half1"] = (m >= 64) & (c >= 0)
    for s in range(6):
        b = 1 << s
        up = ((m // (2 * b)) == (c // (2 * b))) & ((m // b) % 2 == 0) & ((c // b) % 2 == 1)
        cols[f"lvF{s}"] = up
        cols[f"lvB{s}"] = up.T
    pos = np.arange(256, dtype=np.float32)

    def rope(dim):
        inv = (1.0 / (np.float32(10000.0) ** (np.arange(0, dim, 2, dtype=np.float32) / np.float32(dim)))).astype(np.float32)
        ang = pos[:, None] * inv[None, :]
        cs, sn = np.cos(ang), np.sin(ang)
        cs = np.concatenate([cs, cs], -1).reshape(2, 128, dim).transpose(1, 0, 2).reshape(128, 2 * dim)
        sn = np.concatenate([-sn, sn], -1).reshape(2, 128, dim).transpose(1, 0, 2).reshape(128, 2 * dim)
        return cs, sn
    cols["cos64"], cols["sin64"] = rope(64)
    cols["eps"] = np.full((128, 1), EPS)
    a = {k: np.asarray(v, np.float32) for k, v in cols.items()}
    two = {}
    two["triA"] = (m <= c)
    two["cos32"], two["sin32"] = rope(32)
    q, k = (i % 64)[:, None], np.arange(64)[None, :]
    st = np.clip(q - 8, 0, 48)
    win = (k >= st) & (k < st + 16)
    two["na01"] = win
    two["naneg"] = np.where(win, 0.0, -1e30)
    kk = np.arange(256)[None, :]
    two["swa"] = np.concatenate([np.where(np.abs((i + 128 * t)[:, None] - kk) <= 128, 0.0, -1e30) for t in range(2)], 1)
    two["flip"] = ((m // 64) == (c // 64)) & (m % 64 == 63 - c % 64)
    two["iota"] = np.broadcast_to(np.arange(32), (128, 32))
    b = {k: np.asarray(v, np.float32) for k, v in two.items()}

    def pack(d):
        off, o = {}, 0
        for n, v in d.items():
            off[n] = (o, v.shape[1])
            o += v.shape[1]
        return off, np.ascontiguousarray(np.concatenate(list(d.values()), 1), dtype=np.float32)
    return pack(a), pack(b)


class Queue:

    def __init__(self, nc, eng, new_sem, chained):
        self.nc, self.eng, self.new_sem, self.chained = nc, eng, new_sem, chained
        self.sem, self.n, self.seen, self.last = new_sem(), 0, {}, None

    def wait(self, toks):
        for t in toks:
            if t is None:
                continue
            if isinstance(t, list):
                self.wait(t)
                continue
            s, v = t
            if self.seen.get(id(s), 0) < v:
                self.eng.wait_ge(s, v)
                self.seen[id(s)] = v

    def __call__(self, fn, *after, inc=True):
        self.wait(after)
        if self.chained and self.last is not None:
            self.wait([self.last])
        ins = fn(self.eng)
        if not inc:
            return None
        if self.n >= 30000:
            self.sem, self.n = self.new_sem(), 0
        self.n += 1
        ins.then_inc(self.sem, 1)
        self.last = (self.sem, self.n)
        return self.last


def program(nc, a, c1off, c2off, out):
    ctx = ExitStack()
    with ctx:
        names = [0]

        def new_sem():
            names[0] += 1
            return ctx.enter_context(nc.semaphore(f"s{names[0]}"))

        def sb(name, n):
            return ctx.enter_context(nc.sbuf_tensor(name, [128, n], F32))

        P = Queue(nc, nc.tensor, new_sem, False)
        V = Queue(nc, nc.vector, new_sem, True)
        A = Queue(nc, nc.scalar, new_sem, True)
        G = Queue(nc, nc.gpsimd, new_sem, True)
        SP = Queue(nc, nc.sync, new_sem, False)

        class Landing:

            def __init__(self):
                self.sem, self.n = new_sem(), 0

            def load(self, q, dst, src, *after, slow=False):
                q.wait(after)
                self.n += 16
                q.eng.dma_start(dst, src, allow_slow_non_contiguous=slow).then_inc(self.sem, 16)
                return (self.sem, self.n)

        C1N = sum(n for _, n in c1off.values())
        C2N = sum(n for _, n in c2off.values())
        c1 = sb("c1", C1N)
        ring = sb("ring", NR * 4096)
        x = sb("x", 2048)
        xn = sb("xn", 2048)
        hT = sb("hT", 2048)
        AR = 25704
        ar = sb("ar", AR)
        par = sb("par", 3 * 128)
        rows = sb("rows", 300)
        small = sb("small", 1024)
        banks = [ctx.enter_context(nc.psum_tensor(f"pb{i}", [128, 512], F32)) for i in range(8)]

        def K(n):
            o, w = c1off[n]
            return c1[:, o:o + w]

        C2B = AR - C2N

        def K2(n):
            o, w = c2off[n]
            return ar[:, C2B + o:C2B + o + w]

        def zone(o, n):
            return ar[:, o:o + n]

        sm_at = [0]

        def S(n):
            if sm_at[0] + n > 1024:
                sm_at[0] = 0
            o = sm_at[0]
            sm_at[0] += n
            return small[:, o:o + n]

        bank_after = [None] * 8
        busy = [False] * 8
        bank_i = [0]

        def get():
            for _ in range(8):
                k = bank_i[0] % 8
                bank_i[0] += 1
                if not busy[k]:
                    busy[k] = True
                    return k
            raise RuntimeError("no bank")

        def put(k, tok):
            busy[k] = False
            bank_after[k] = tok

        def mm(o, l, r, start, stop, *after, inc=False):
            return P(lambda e: e.matmul(o, l, r, start=start, stop=stop), *after, inc=inc)

        def tr(o, i, *after, inc=False):
            n = i.shape[0]
            p0 = 0
            return P(lambda e: e.transpose(o, i, K("ident")[p0:p0 + n, 0:n]), *after, inc=inc)

        def tt(q, o, i0, i1, op, *after):
            return q(lambda e: e.tensor_tensor(o, i0, i1, op), *after)

        def ts(q, o, i, s1, s2, op0, op1, *after):
            return q(lambda e: e.tensor_scalar(o, i, s1, s2, op0, op1), *after)

        def stt(o, i0, s, i1, op0, op1, *after):
            return V(lambda e: e.scalar_tensor_tensor(out=o, in0=i0, scalar=s, in1=i1, op0=op0, op1=op1), *after)

        def act(o, i, f, *after, bias=None, scale=1.0, accum=None):
            kw = {}
            if bias is not None:
                kw["bias"] = bias
            if accum is not None:
                kw["accum_out"] = accum
            return A(lambda e: e.activation(o, i, f, scale=scale, **kw), *after)

        def copy(q, o, i, *after):
            if q is A:
                return A(lambda e: e.copy(o, i), *after)
            return q(lambda e: e.tensor_copy(o, i), *after)

        def bc(ap, shape):
            return ap.broadcast_to(shape)

        blocks = []

        def cols(w, c0, n):
            blocks.append((w.rearrange("(c p) n -> p c n", p=128)[:, :, c0:c0 + n], w.shape[0] // 128, n))

        def rws(w, k0, nk):
            blocks.append((w.rearrange("(c p) n -> p c n", p=128)[:, k0:k0 + nk, :], nk, w.shape[1]))

        for l in range(2):
            for j in range(4):
                cols(a["ada_w"][l], 512 * j, 512)
            for j in range(6):
                cols(a["w_in"][l], 512 * j, 512)
            cols(a["w_in"][l], 3584, 16)
            cols(a["w_in"][l], 3072, 512)
            for j in range(4):
                cols(a["w_in"][l], 3600 + 512 * j, 512)
            rws(a["w_branch_a"][l], 0, 4)
            rws(a["w_branch_b"][l], 0, 4)
            for j in (4, 5):
                cols(a["ada_w"][l], 512 * j, 512)
            rws(a["w_out"][l], 0, 4)
            rws(a["w_out"][l], 4, 4)
            for j in range(6, 12):
                cols(a["ada_w"][l], 512 * j, 512)
            for j in range(8):
                cols(a["w_mlp1"][l], 512 * j, 512)
            for j in range(8):
                rws(a["w_mlp2"][l], 4 * j, 4)
        for l in range(2):
            for j in range(4):
                cols(a["w_in_2"][l], 512 * j, 512 if j < 3 else 288)
            rws(a["mla_w_uq_2"][l], 0, 2)
            rws(a["mla_w_ukv_2"][l], 0, 1)
            rws(a["w_out_2"][l], 0, 4)
            rws(a["w_out_2"][l], 4, 4)
            cols(a["w_router_2"][l], 0, 16)
            for e in range(17):
                if e < 16:
                    for w in ("w_gate_2", "w_up_2"):
                        for j in range(2):
                            cols(a[w][l, e], 512 * j, 512)
                if e:
                    rws(a["w_down_2"][l, e - 1], 0, 4)
                    rws(a["w_down_2"][l, e - 1], 4, 4)

        landed = [Landing() for _ in range(NR)]
        got = {}
        used = {}

        def issue(i):
            if i >= len(blocks):
                return
            src, k, n = blocks[i]
            s = i % NR
            dst = ring[:, s * 4096:s * 4096 + k * n].rearrange("p (k n) -> p k n", k=k)
            got[i] = (dst, landed[s].load(SP, dst, src, used.get(i - NR), slow=n < 128))
        nxt = [0]
        for i in range(NR):
            issue(i)

        def take():
            i = nxt[0]
            nxt[0] += 1
            return i, got[i][0], got[i][1]

        def release(i, tok):
            used[i] = tok
            issue(i + NR)

        l_c = Landing()
        t_c = l_c.load(A, c1[:, :], a["c1"])
        l_p = Landing()
        stage = zone(0, 384)
        pd = []

        def prow(k, r0, src, n):
            pd.append(l_p.load(A, stage[r0:r0 + n, 128 * k:128 * k + 128], src))
            return 128 * k + r0

        def r128(ap):
            return ap.rearrange("(r q) -> r q", q=128)

        t_z = V(lambda e: e.memset(stage, 0.0))
        A.wait([t_z])
        pc = [{}, {}]
        for l in range(2):
            d = pc[l]
            d["n1"] = prow(l, 0, r128(a["norm1_g"][l]), 8)
            d["n2"] = prow(l, 8, r128(a["norm2_g"][l]), 8)
            d["ada_b"] = prow(l, 16, r128(a["ada_b"][l]), 48)
            d["og"] = prow(l, 64, r128(a["dn_out_gain"][l]), 1)
            d["sg"] = prow(l, 65, r128(a["diff_subln_gain"][l]), 1)
            d["cv"] = prow(l, 66, a["dn_conv"][l].rearrange("k (f q) -> (k f) q", q=128), 60)
            o = 8 + 27 * l
            d["an"] = prow(2, o, r128(a["attn_norm_2"][l]), 8)
            d["fn"] = prow(2, o + 8, r128(a["ffn_norm_2"][l]), 8)
            d["gn"] = prow(2, o + 16, r128(a["group_norm_2"][l]), 8)
            d["qn"] = prow(2, o + 24, r128(a["mla_q_norm_2"][l]), 2)
            d["kn"] = prow(2, o + 26, r128(a["mla_kv_norm_2"][l]), 1)
        p_c = prow(2, 0, a["c"].rearrange("a (r q) -> (a r) q", q=128), 8)

        def pcol(o, n=1):
            return par[:, o:o + n]

        l_x = Landing()
        xd = a["x"][0].rearrange("(t p) d -> p t d", p=128)
        x3 = x[:, :].rearrange("p (t d) -> p t d", t=2)
        t_x = l_x.load(A, x3, xd)

        l_r = Landing()
        rc = {}
        ro = [0]

        def prw(name, ap, n):
            o = ro[0]
            ro[0] += n
            rc[name] = (o, l_r.load(A, rows[:, o:o + n], ap.partition_broadcast(128)))
            return o

        k = get()
        tp = None
        for j in range(3):
            tp = tr(banks[k][:, 128 * j:128 * j + 128], stage[:, 128 * j:128 * j + 128], pd[-1], t_c, inc=True)
        t_par = copy(V, par[:, :], banks[k][:, 0:384], tp)
        put(k, t_par)
        c_act = S(8)
        sctmp = S(8)

        def sigm(q, o, i, *after):
            t = act(o, i, ACT.Exp, *after, scale=-1.0)
            ts(V, o, o, 1.0, None, ALU.add, ALU.bypass, t)
            return V(lambda e: e.reciprocal(o, o))

        t = sigm(V, sctmp, pcol(p_c, 8), t_par)
        cact = sb("cact", 8)
        t_cact = tt(V, cact[:, :], sctmp, pcol(p_c, 8), ALU.mult)

        def rsqrt(o, i, scale, *after):
            act(o, i, ACT.Ln, *after, scale=scale, bias=K("eps"))
            return act(o, o, ACT.Exp, scale=-0.5)

        xr = [None]

        def normed(*after):
            ss = S(2)
            junk = hT[:, 0:1024]
            for t in range(2):
                ta = act(junk, x3[:, t, :], ACT.Square, t_x, xr[0], *after, accum=ss[:, t:t + 1])
            r = S(2)
            ta = rsqrt(r, ss, 1.0 / 1024)
            tk = None
            for t in range(2):
                tk = ts(V, xn[:, 1024 * t:1024 * t + 1024], x3[:, t, :], r[:, t:t + 1], None, ALU.mult, ALU.bypass, ta)
            return tk

        hT3 = hT[:, :].rearrange("p (c n) -> p c n", c=8)

        def to_hT(src, sa, sbias, tk, dst=None, *after):
            dst = hT3 if dst is None else dst
            toks = []
            for cp in range(4):
                k = get()
                for j in range(2):
                    for t in range(2):
                        cc = 2 * cp + j
                        tp = tr(banks[k][:, 256 * j + 128 * t:256 * j + 128 * t + 128],
                                src[:, 1024 * t + 128 * cc:1024 * t + 128 * cc + 128], tk, t_c, bank_after[k],
                                inc=(j == 1 and t == 1))
                for j in range(2):
                    cc = 2 * cp + j
                    i = banks[k][:, 256 * j:256 * j + 256]
                    if cp % 2:
                        if sbias is None:
                            te = act(dst[:, cc, :], i, ACT.Copy, tp, *after, scale=sa(cc))
                        else:
                            te = act(dst[:, cc, :], i, ACT.Identity, tp, *after, scale=sa(cc), bias=sbias(cc))
                    else:
                        s2 = None if sbias is None else sbias(cc)
                        te = ts(V, dst[:, cc, :], i, sa(cc), s2, ALU.mult, ALU.bypass if s2 is None else ALU.add, tp, *after)
                put(k, te)
                toks.append(te)
            return toks

        def lin_tok(lhs, tl, w, tw, n, nk, evac, k0=0):
            tp = None
            for t in range(2):
                k = get()
                for c in range(nk):
                    tp = mm(banks[k][:, 0:n], lhs[:, k0 + c, 128 * t:128 * t + 128], w[:, c, 0:n], c == 0, c == nk - 1,
                            tl, tw, bank_after[k], inc=(c == nk - 1))
                put(k, evac(t, banks[k][:, 0:n], tp))
            return tp

        def lin_feat(w, tw, rhs, tr_, nk, f0, evac):
            k = get()
            tp = None
            for j in range(2):
                for c in range(nk):
                    tp = mm(banks[k][:, 256 * j:256 * j + 256], w[:, c, 128 * (f0 + j):128 * (f0 + j) + 128],
                            rhs[:, c, :], c == 0, c == nk - 1, tr_, tw, bank_after[k], inc=(c == nk - 1 and j == 1))
            put(k, evac(f0, banks[k][:, :].rearrange("p (j n) -> p j n", j=2), tp))
            return tp

        modT = sb("modT", 48)

        def ada(l, js):
            tk = None
            for j in js:
                i, w, tw = take()
                k = get()
                for f in range(4):
                    for c in range(8):
                        tp = mm(banks[k][:, f:f + 1], w[:, c, 128 * f:128 * f + 128], cact[:, c:c + 1], c == 0, c == 7,
                                tw, t_cact, bank_after[k], inc=(f == 3 and c == 7))
                release(i, tp)
                tk = tt(V, modT[:, 4 * j:4 * j + 4], banks[k][:, 0:4], pcol(pc[l]["ada_b"] + 4 * j, 4), ALU.add, tp)
                put(k, tk)
            return tk

        def spread(dst, src, tk, *after):
            dg = S(128)
            for h in range(2):
                k = get()
                for c in range(4):
                    td = ts(V, dg, K("ident"), src[:, 4 * h + c:4 * h + c + 1], None, ALU.mult, ALU.bypass, tk,
                            tk if c == 0 and h == 0 else tp)
                    tp = mm(banks[k][:, 128 * c:128 * c + 128], K("ones"), dg, True, True, td, bank_after[k], inc=True)
                te = copy(V, dst[:, 512 * h:512 * h + 512], banks[k][:, :], tp, *after)
                put(k, te)
            return te

        def interleave(*gens):
            live = list(gens)
            while live:
                for g in list(live):
                    try:
                        next(g)
                    except StopIteration:
                        live.remove(g)

        def softmax_pair(tl, kT, qT, bias, scale, sc_s, sc_e, sink):
            k = get()
            for t in range(2):
                tp = mm(banks[k][:, 256 * t:256 * t + 256], qT[:, 128 * t:128 * t + 128], kT, True, True,
                        tl, bank_after[k], inc=(t == 1))
            b3 = banks[k][:, :].rearrange("p (t n) -> p t n", t=2)
            e3 = sc_e.rearrange("p (t n) -> p t n", t=2)
            src, sc = b3, scale
            if bias is not None:
                s3 = sc_s.rearrange("p (t n) -> p t n", t=2)
                tk = stt(s3, b3, scale, bias, ALU.mult, ALU.add, tp)
                put(k, tk)
                src, sc = s3, 1.0
            mx, nm, smv = S(2), S(2), S(2)
            V(lambda e: e.tensor_reduce(mx, src, AX.X, ALU.max), tp)
            if sink is not None:
                ts(V, mx, mx, sink, None, ALU.max, ALU.bypass)
            tn = ts(V, nm, mx, -sc, None, ALU.mult, ALU.bypass)
            for t in range(2):
                te = act(e3[:, t, :], src[:, t, :], ACT.Exp, tn, tp, bias=nm[:, t:t + 1], scale=sc,
                         accum=smv[:, t:t + 1])
            if bias is None:
                put(k, te)
            if sink is not None:
                es = S(2)
                te = act(es, nm, ACT.Exp, bias=sink)
                tt(V, smv, smv, es, ALU.add, te)
            r = S(2)
            tk = V(lambda e: e.reciprocal(r, smv), te)
            return e3, r, te, tk

        def probs_T(e3, te, sc_t, q, *after):
            k = get()
            for t in range(2):
                for kt in range(2):
                    tp = tr(banks[k][:, 256 * t + 128 * kt:256 * t + 128 * kt + 128], e3[:, t, 128 * kt:128 * kt + 128],
                            te, bank_after[k], inc=(t == 1 and kt == 1))
            tk = copy(q, sc_t, banks[k][:, :], tp, *after)
            put(k, tk)
            return tk, tp

        def pv(sc_t, tk, v, dv, tv):
            k = get()
            for t in range(2):
                for kt in range(2):
                    tp = mm(banks[k][:, dv * t:dv * t + dv], sc_t[:, 256 * t + 128 * kt:256 * t + 128 * kt + 128],
                            v(kt), kt == 0, kt == 1, tk, tv, bank_after[k], inc=(t == 1 and kt == 1))
            return k, tp

        Z1, ZST, ZTOK, ZDT, ZLT, ZAT, ZG, ZZ, ZY = 0, 6144, 9264, 12336, 14384, 16432, 18480, 22576, 23600
        modw = [None, None]

        def v4(ap, *d):
            s = " ".join("abcdef"[:len(d) + 1])
            kw = {"abcdef"[i]: d[i] for i in range(len(d))}
            return ap.rearrange("p (" + s + ") -> p " + s, **kw)

        def block1(l):
            pl = pc[l]
            tm = ada(l, range(4))
            sa = S(8)
            ts(V, sa, modT[:, 8:16], 1.0, None, ALU.add, ALU.bypass)
            sa1 = sb(f"sa{l}", 8)
            tsa = tt(V, sa1[:, :], sa, pcol(pl["n1"], 8), ALU.mult)
            tk = normed()
            th = to_hT(xn, lambda c: sa1[:, c:c + 1], lambda c: modT[:, c:c + 1], tk, None, tsa, tm)

            qk = xn[:, :].rearrange("p (t n) -> p t n", t=2)
            vA = zone(ZLT, 1024).rearrange("p (t n) -> p t n", t=2)
            ev = {}

            def plain(dst, q):
                def f(t, b, tp):
                    ev[0] = copy(q, dst(t), b, tp)
                    return ev[0]
                return f
            for j in range(3):
                i, w, tw = take()
                if j < 2:
                    tp = lin_tok(hT3, th, w, tw, 512, 8, plain(lambda t: qk[:, t, 512 * j:512 * j + 512], A))
                else:
                    tp = lin_tok(hT3, th, w, tw, 512, 8, plain(lambda t: vA[:, t, :], A))
                release(i, tp)
                if j == 1:
                    tqk = ev[0]
            tvA = ev[0]

            ro[0] = 0
            if l:
                A.wait([V.last])
            prw("qkg", a["qk_norm_gain"][l].rearrange("a d -> (a d)"), 128)
            prw("al", a["dn_A_log"][l].rearrange("a d -> (a d)"), 8)
            prw("dt", a["dn_dt_bias"][l].rearrange("a d -> (a d)"), 8)
            lamd = zone(ZY, 256)
            tl_ = l_r.load(A, lamd, a["diff_lambda"][l].rearrange("a d -> (a d)").partition_broadcast(128))

            cin = zone(ZST, 3120).rearrange("p (f n) -> p f n", f=12)
            tpad = V(lambda e: e.memset(cin[:, :, 0:2], 0.0))
            tpad = V(lambda e: e.memset(cin[:, :, 258:260], 0.0))
            babs = sb(f"ba{l}", 32)
            ba = babs[:, :].rearrange("p (t n) -> p t n", t=2)
            st = {}
            zT = zone(ZZ, 1024).rearrange("p (f n) -> p f n", f=4)
            gT = zone(ZG, 4096).rearrange("p (f n) -> p f n", f=16)
            yaT = zone(ZY, 1024).rearrange("p (f n) -> p f n", f=4)
            ybT = zone(ZY + 1024, 1024).rearrange("p (f n) -> p f n", f=4)

            def proj_dn():
                for j in range(3):
                    i, w, tw = take()
                    for f in (0, 2):
                        def e(f0, b, tp, j=j):
                            q = A if f0 else V
                            st["cin", j, f0] = copy(q, cin[:, 4 * j + f0:4 * j + f0 + 2, 2:258], b, tp)
                            return st["cin", j, f0]
                        tp = lin_feat(w, tw, hT3, th, 8, f, e)
                        yield
                    release(i, tp)
                i, w, tw = take()

                def e(t, b, tp):
                    st["ba"] = copy(V, ba[:, t, :], b, tp)
                    return st["ba"]
                tp = lin_tok(hT3, th, w, tw, 16, 8, e)
                release(i, tp)
                yield

            def gates():
                for j in range(5):
                    i, w, tw = take()
                    for f in (0, 2):
                        def e(f0, b, tp, j=j):
                            dst = zT[:, f0:f0 + 2, :] if j == 0 else gT[:, 4 * (j - 1) + f0:4 * (j - 1) + f0 + 2, :]
                            if j == 0:
                                sg = v4(zone(ZY + 1024 + 512 * (f0 // 2), 512), 2)
                                te = act(sg, b, ACT.Exp, tp, scale=-1.0)
                                ts(V, sg, sg, 1.0, None, ALU.add, ALU.bypass, te)
                                V(lambda e: e.reciprocal(sg, sg))
                                return tt(V, dst, b, sg, ALU.mult)
                            te = act(dst, b, ACT.Exp, tp, scale=-1.0)
                            ts(V, dst, dst, 1.0, None, ALU.add, ALU.bypass, te)
                            V(lambda e: e.reciprocal(dst, dst))
                            return te
                        tp = lin_feat(w, tw, hT3, th, 8, f, e)
                        yield
                    release(i, tp)

            def attn_a():
                g = rows[:, 0:128]
                tr_ = rc["dt"][1]
                cg, sg = S(256), S(256)
                cg4 = v4(cg, 2, 2)
                sg4 = v4(sg, 2, 2)
                cosr = v4(K("cos64"), 2)
                sinr = v4(K("sin64"), 2)
                for t in range(2):
                    tt(V, cg4[:, t], bc(cosr[:, t:t + 1, :], [128, 2, 64]), v4(g, 2), ALU.mult, tr_, tl_, t_c)
                    for h in range(2):
                        tt(V, sg4[:, t, :, 32 * h:32 * h + 32], bc(sinr[:, t:t + 1, 32 * h:32 * h + 32], [128, 2, 32]),
                           v4(g, 2)[:, :, 32 - 32 * h:64 - 32 * h], ALU.mult)
                l4 = v4(lamd, 4)
                pr = S(128)
                p3 = v4(pr, 2)
                l2 = lamd.rearrange("p (a b d) -> p a b d", a=2, b=2)
                tt(V, p3, l2[:, :, 0, :], l2[:, :, 1, :], ALU.mult)
                sl = S(2)
                tk = V(lambda e: e.tensor_reduce(sl, p3, AX.X, ALU.add))
                tk = act(sl, sl, ACT.Exp, tk)
                lam = sb(f"lam{l}", 1)
                tt(V, lam[:, :], sl[:, 0:1], sl[:, 1:2], ALU.subtract, tk)
                li = 0.8 - 0.6 * math.exp(-0.3 * l)
                ts(V, lam[:, :], lam[:, :], li, None, ALU.add, ALU.bypass)
                sq = zone(Z1, 2048)
                t1 = zone(Z1 + 2048, 2048)
                tk = act(sq, xn[:, :], ACT.Square, tqk)
                ss = S(32)
                tk = V(lambda e: e.tensor_reduce(ss, v4(sq, 32), AX.X, ALU.add), tk)
                tk = rsqrt(ss, ss, 1.0 / 64, tk)
                q32 = v4(xn[:, :], 32)
                yield
                tt(V, q32, q32, bc(ss.unsqueeze(2), [128, 32, 64]), ALU.mult, tk, tqk)
                yield
                t14 = t1.rearrange("p (a g d) -> p a g d", a=4, g=8)
                sq4 = sq.rearrange("p (a g d) -> p a g d", a=4, g=8)
                q4 = xn[:, :].rearrange("p (a g d) -> p a g d", a=4, g=8)
                cga = cg.rearrange("p (a d) -> p a d", a=4)
                sga = sg.rearrange("p (a d) -> p a d", a=4)
                for i in range(4):
                    tt(V, t14[:, i], q4[:, i], bc(cga[:, i:i + 1, :], [128, 8, 64]), ALU.mult)
                    for h in range(2):
                        tt(V, sq4[:, i, :, 32 * h:32 * h + 32], q4[:, i, :, 32 - 32 * h:64 - 32 * h],
                           bc(sga[:, i:i + 1, 32 * h:32 * h + 32], [128, 8, 32]), ALU.mult)
                    yield
                tk = tt(V, t1, t1, sq, ALU.add)
                QT = v4(zone(ZDT, 2048), 8)
                t13 = v4(t1, 2)
                for cp in range(4):
                    k = get()
                    for j in range(2):
                        for t in range(2):
                            cc = 2 * cp + j
                            tp = tr(banks[k][:, 256 * j + 128 * t:256 * j + 128 * t + 128],
                                    t13[:, t, 128 * cc:128 * cc + 128], tk, bank_after[k], inc=(j == 1 and t == 1))
                    tq = copy(A if cp % 2 else V, QT[:, 2 * cp:2 * cp + 2, :], v4(banks[k][:, :], 2), tp)
                    put(k, tq)
                    st["qT", cp] = tq
                    yield
                tq = [st["qT", i] for i in range(4)]
                st["rope_done"] = tk
                sc = [zone(ZLT + 1024 + 512 * i, 512) for i in range(2)] + [zone(ZAT + 512 * i, 512) for i in range(4)]
                o = zone(Z1 + 4096, 1024).rearrange("p (t h d) -> p t h d", t=2, h=4)
                lastpv = [None, None]
                for h in range(4):
                    es = []
                    for c in range(2):
                        kT = QT[64 * c:64 * c + 64, 4 + h, :]
                        qT = QT[64 * c:64 * c + 64, h, :]
                        e3, r, te, tr2 = softmax_pair([tq, st.get("ptr")], kT, qT, None, 0.125, None, sc[2 * (h % 2) + c] if False else sc[c], None)
                        es.append((e3, r, te, tr2))
                        yield
                    (e0, r0, te0, _), (e1, r1, te1, _) = es
                    rl = S(2)
                    ts(V, rl, r1, lam[:, 0:1], None, ALU.mult, ALU.bypass)
                    for t in range(2):
                        ts(V, e1[:, t, :], e1[:, t, :], rl[:, t:t + 1], None, ALU.mult, ALU.bypass, te1)
                        ta = stt(e0[:, t, :], e0[:, t, :], r0[:, t:t + 1], e1[:, t, :], ALU.mult, ALU.subtract, te0)
                    yield
                    scT = sc[2 + h % 2]
                    tk, ptr = probs_T(e0, ta, scT, A, lastpv[h % 2])
                    A.wait([ptr])
                    st["ptr"] = ptr
                    yield
                    k, tp = pv(scT, tk, lambda kt: vA[:, kt, 128 * h:128 * h + 128], 128, tvA)
                    lastpv[h % 2] = tp
                    to = copy(V, o[:, :, h, :], banks[k][:, 0:256].rearrange("p (t d) -> p t d", t=2), tp)
                    put(k, to)
                    yield
                st["ya"] = head_norm(o, zone(Z1, 1024), to, pcol(pl["sg"]), 1.0 - li, None, yaT)
                yield

            def head_norm(o, tmp, to, gain, fac, mulT, dst, *after):
                o2 = o.rearrange("p t h d -> p (t h d)")
                tk = act(tmp, o2, ACT.Square, to)
                ss = S(8)
                tk = V(lambda e: e.tensor_reduce(ss, v4(tmp, 8), AX.X, ALU.add), tk)
                tk = rsqrt(ss, ss, 1.0 / 128, tk)
                o8 = v4(o2, 8)
                if fac != 1.0:
                    ts(V, ss, ss, fac, None, ALU.mult, ALU.bypass, tk)
                tk = tt(V, o8, o8, bc(ss.unsqueeze(2), [128, 8, 128]), ALU.mult, tk)
                for hp in range(2):
                    k = get()
                    for j in range(2):
                        for t in range(2):
                            tp = tr(banks[k][:, 256 * j + 128 * t:256 * j + 128 * t + 128], o[:, t, 2 * hp + j, :], tk,
                                    bank_after[k], inc=(j == 1 and t == 1))
                    b = v4(banks[k][:, :], 2)
                    if mulT is None:
                        te = ts(V, dst[:, 2 * hp:2 * hp + 2, :], b, gain, None, ALU.mult, ALU.bypass, tp, *after)
                    else:
                        te = stt(dst[:, 2 * hp:2 * hp + 2, :], b, gain, mulT[:, 2 * hp:2 * hp + 2, :], ALU.mult, ALU.mult, tp, *after)
                    put(k, te)
                return te

            interleave(attn_a(), proj_dn())

            beta = S(16)
            graw = S(16)
            gsm = S(64)
            ge = S(64)

            def delta():
                acc = v4(zone(Z1, 3072), 12)
                tmp = v4(zone(Z1 + 3072, 3072), 12)
                TOK = zone(ZTOK, 3072).rearrange("p (g t h d) -> p g t h d", g=3, t=2, h=4)
                b3 = v4(beta, 2)
                g3 = v4(graw, 2)
                tk = act(b3, ba[:, :, 0:8], ACT.Exp, st["ba"], scale=-1.0)
                ts(V, b3, b3, 1.0, None, ALU.add, ALU.bypass, tk)
                tbeta = V(lambda e: e.reciprocal(b3, b3))
                z, nz, sp, ea = v4(S(16), 2), v4(S(16), 2), v4(S(16), 2), S(8)
                dtb = rows[:, 136:144].unsqueeze(1)
                tt(V, z, ba[:, :, 8:16], bc(dtb, [128, 2, 8]), ALU.add)
                ts(V, nz, z, -1.0, None, ALU.mult, ALU.bypass)
                tk = tt(V, nz, nz, z, ALU.max)
                act(sp, nz, ACT.Exp, tk, scale=-1.0)
                tk = act(sp, sp, ACT.Ln, bias=K("ones")[:, 0:1])
                tk = act(ea, rows[:, 128:136], ACT.Exp, rc["dt"][1])
                stt(z, z, 0.0, sp, ALU.max, ALU.add, tk)
                tg = stt(g3, z, -1.0, bc(ea.unsqueeze(1), [128, 2, 8]), ALU.mult, ALU.mult)
                gb = v4(gsm, 2)
                k = get()
                for t in range(2):
                    o = 32 * t
                    for nm, lo, ro_, n in (("triF", 0, 0, 4), ("triB", 4, 4, 4), ("blk", 8, 0, 8), ("half0", 16, 0, 8), ("half1", 24, 0, 8)):
                        tp = mm(banks[k][:, o + lo:o + lo + n], K(nm), g3[:, t, ro_:ro_ + n], True, True, tg, bank_after[k],
                                inc=(t == 1 and nm == "half1"))
                tk = copy(V, gsm, banks[k][:, 0:64], tp)
                put(k, tk)
                tk = tt(V, gb[:, :, 8:16], gb[:, :, 8:16], gb[:, :, 0:8], ALU.subtract)
                tge = act(ge, gsm, ACT.Exp, tk)
                E = v4(ge, 2)
                yield
                dT = zone(ZDT, 2048).rearrange("p (i t h d) -> p i t h d", i=2, t=2, h=4)
                tdd = {}
                for i in range(2):
                    tri = K("triF" if i == 0 else "triB")
                    for t in range(2):
                        k = get()
                        for h in range(4):
                            jj = 4 * i + h
                            tp = mm(banks[k][:, 128 * h:128 * h + 128], bc(g3[:, t, jj:jj + 1], [128, 128]), tri, True, True,
                                    tg, bank_after[k], inc=(h == 3))
                        for h in range(4):
                            jj = 4 * i + h
                            tk = stt(dT[:, i, t, h, :], banks[k][:, 128 * h:128 * h + 128], gb[:, t, jj:jj + 1], tri,
                                     ALU.subtract, ALU.mult, tp, st["ya"])
                        put(k, tk)
                        te = act(dT[:, i, t], dT[:, i, t], ACT.Exp, tk)
                        tdd[i, t] = tt(V, dT[:, i, t], dT[:, i, t], bc(tri.unsqueeze(1), [128, 4, 128]), ALU.mult, te)
                        yield
                cv = pl["cv"]
                for g in range(3):
                    for f in range(4 * g, 4 * g + 4):
                        tc_ = st["cin", g, 0 if f % 4 < 2 else 2]
                        t0 = act(acc[:, f, :], cin[:, f, 0:256], ACT.Copy, tc_, tpad, st["ya"], scale=pcol(cv + f))
                        for kk in range(1, 5):
                            tk = stt(acc[:, f, :], cin[:, f, kk:kk + 256], pcol(cv + 12 * kk + f), acc[:, f, :],
                                     ALU.mult, ALU.add, t0, tc_)
                        if f % 2:
                            yield
                    ag, tg_ = acc[:, 4 * g:4 * g + 4, :], tmp[:, 4 * g:4 * g + 4, :]
                    te = act(tg_, ag, ACT.Exp, tk, scale=-1.0)
                    ts(V, tg_, tg_, 1.0, None, ALU.add, ALU.bypass, te)
                    V(lambda e: e.reciprocal(tg_, tg_))
                    tk = tt(V, ag, ag, tg_, ALU.mult)
                    yield
                    for t in range(2):
                        k = get()
                        for h in range(4):
                            tp = tr(banks[k][:, 128 * h:128 * h + 128], acc[:, 4 * g + h, 128 * t:128 * t + 128], tk,
                                    bank_after[k], inc=(h == 3))
                        st["tok", g, t] = copy(A, TOK[:, g, t], v4(banks[k][:, :], 4), tp)
                        put(k, st["tok", g, t])
                    yield
                ss = S(16)
                sq = zone(Z1 + 3072, 2048)
                tk = act(sq, zone(ZTOK, 2048), ACT.Square)
                tk = V(lambda e: e.tensor_reduce(ss, v4(sq, 16), AX.X, ALU.add), tk)
                tk = rsqrt(ss, ss, 1.0, tk)
                tk = ts(V, ss[:, 0:8], ss[:, 0:8], 128 ** -0.5, None, ALU.mult, ALU.bypass, tk)
                t16 = v4(zone(ZTOK, 2048), 16)
                tk = tt(V, t16, t16, bc(ss.unsqueeze(2), [128, 16, 128]), ALU.mult)
                yield
                kqT = v4(xn[:, :], 4)
                tkq = []
                for h in range(4):
                    k = get()
                    for g in range(2):
                        for t in range(2):
                            tp = tr(banks[k][:, 256 * g + 128 * t:256 * g + 128 * t + 128], TOK[:, 1 - g, t, h, :], tk,
                                    bank_after[k], inc=(g == 1 and t == 1))
                    te = copy(A if h % 2 else V, kqT[:, h, :], banks[k][:, :], tp)
                    put(k, te)
                    tkq.append(te)
                yield
                LT = zone(ZLT, 2048).rearrange("p (i t h d) -> p i t h d", i=2, t=2, h=4)
                AT = zone(ZAT, 2048).rearrange("p (i t h d) -> p i t h d", i=2, t=2, h=4)
                X = zone(Z1, 2048).rearrange("p (i t h d) -> p i t h d", i=2, t=2, h=4)
                XT = zone(Z1 + 2048, 2048).rearrange("p (i t h d) -> p i t h d", i=2, t=2, h=4)
                B = zone(Z1 + 4096, 2048).rearrange("p (i t h d) -> p i t h d", i=2, t=2, h=4)
                for h in range(4):
                    k = get()
                    for t in range(2):
                        kq = kqT[:, h, :].rearrange("p (g n) -> p g n", g=2)[:, :, 128 * t:128 * t + 128]
                        tp = mm(v4(banks[k][:, 256 * t:256 * t + 256], 2), kqT[:, h, 128 * t:128 * t + 128], kq, True, True,
                                tkq, bank_after[k], inc=(t == 1))
                    for t in range(2):
                        for i in range(2):
                            stt(LT[:, i, t, h, :], banks[k][:, 256 * t:256 * t + 128], b3[:, t, 4 * i + h:4 * i + h + 1],
                                dT[:, i, t, h, :], ALU.mult, ALU.mult, tp)
                            tk = tt(V, dT[:, i, t, h, :], banks[k][:, 256 * t + 128:256 * t + 256], dT[:, i, t, h, :], ALU.mult)
                    put(k, tk)
                    yield
                tLT = tk
                tqkT = tk
                grp = [(i, t) for i in range(2) for t in range(2)]

                def lv(i, s):
                    return bc(K(("lvF" if i == 0 else "lvB") + str(s)).unsqueeze(1), [128, 4, 128])
                tX, tXT, tB = {}, {}, {}
                for i, t in grp:
                    tt(V, XT[:, i, t], LT[:, i, t], lv(i, 0), ALU.mult)
                    tXT[i, t] = tt(V, XT[:, i, t], bc(K("ident").unsqueeze(1), [128, 4, 128]), XT[:, i, t], ALU.subtract)
                    k = get()
                    for h in range(4):
                        tp = tr(banks[k][:, 128 * h:128 * h + 128], XT[:, i, t, h, :], tXT[i, t], bank_after[k], inc=(h == 3))
                    tX[i, t] = copy(A, X[:, i, t], v4(banks[k][:, :], 4), tp)
                    put(k, tX[i, t])
                yield
                pB = {}
                for s in range(1, 6):
                    for i, t in grp:
                        ta = tt(G, AT[:, i, t], LT[:, i, t], lv(i, s), ALU.mult, tLT, pB.get((i, t)))
                        k = get()
                        for h in range(4):
                            tp = mm(banks[k][:, 128 * h:128 * h + 128], AT[:, i, t, h, :], X[:, i, t, h, :], True, True, ta,
                                    tX[i, t], bank_after[k], inc=(h == 3))
                        pB[i, t] = tp
                        tB[i, t] = copy(A, B[:, i, t], v4(banks[k][:, :], 4), tp)
                        put(k, tB[i, t])
                    yield
                    for i, t in grp:
                        if s < 5:
                            k = get()
                            for h in range(4):
                                tp = mm(banks[k][:, 128 * h:128 * h + 128], XT[:, i, t, h, :], B[:, i, t, h, :], True, True,
                                        tB[i, t], tXT[i, t], bank_after[k], inc=(h == 3))
                            tX[i, t] = tt(V, X[:, i, t], X[:, i, t], v4(banks[k][:, :], 4), ALU.subtract, tp)
                            put(k, tX[i, t])
                        k = get()
                        for h in range(4):
                            tp = mm(banks[k][:, 128 * h:128 * h + 128], B[:, i, t, h, :], XT[:, i, t, h, :], True, True,
                                    tB[i, t], tXT[i, t], bank_after[k], inc=(h == 3))
                        tXT[i, t] = tt(V, XT[:, i, t], XT[:, i, t], v4(banks[k][:, :], 4), ALU.subtract, tp)
                        put(k, tXT[i, t])
                    yield
                KG, KD, BU, WT = AT, LT, X, B
                ktok, vtok = TOK[:, 1], TOK[:, 2]
                tbu, twt, tkd = {}, {}, {}
                for i, t in grp:
                    egb = bc(E[:, t, 4 * i:4 * i + 4].unsqueeze(2), [128, 4, 128])
                    kdb = bc(E[:, t, 8 + 4 * i:12 + 4 * i].unsqueeze(2), [128, 4, 128])
                    tkg = tt(V, KG[:, i, t], ktok[:, t], egb, ALU.mult, tge, pB[i, t])
                    tkd[i, t] = tt(V, KD[:, i, t], ktok[:, t], kdb, ALU.mult, G.last)
                    k = get()
                    for h in range(4):
                        tp = mm(banks[k][:, 128 * h:128 * h + 128], XT[:, i, t, h, :], vtok[:, t, h, :], True, True,
                                tXT[i, t], st["tok", 2, 1], bank_after[k], inc=(h == 3))
                    tbu[i, t] = tt(V, BU[:, i, t], v4(banks[k][:, :], 4),
                                   bc(b3[:, t, 4 * i:4 * i + 4].unsqueeze(2), [128, 4, 128]), ALU.mult, tp)
                    put(k, tbu[i, t])
                    k = get()
                    for h in range(4):
                        tp = mm(banks[k][:, 128 * h:128 * h + 128], KG[:, i, t, h, :], XT[:, i, t, h, :], True, True, tkg,
                                bank_after[k], inc=(h == 3))
                    twt[i, t] = copy(A, WT[:, i, t], v4(banks[k][:, :], 4), tp)
                    put(k, twt[i, t])
                    yield
                ST = zone(ZST, 3072).rearrange("p (i s h d) -> p i s h d", i=2, s=3, h=4)
                tS = {}
                tvn = {}
                tmpd = [zone(ZAT, 512), zone(ZAT + 512, 512)]
                twm = [None, None]
                for s in range(4):
                    for i in range(2):
                        n = s if i == 0 else 3 - s
                        t, p0 = n // 2, 64 * (n % 2)
                        pp = slice(p0, p0 + 64)
                        if s:
                            k = get()
                            for h in range(4):
                                tp = mm(banks[k][pp, 128 * h:128 * h + 128], WT[:, i, t, h, pp], ST[:, i, s - 1, h, :], True, True,
                                        tS[i, s], twt[i, t], bank_after[k], inc=(h == 3))
                            tw3 = v4(tmpd[i][pp, :], 4)
                            tk = tt(V, tw3, v4(banks[k][pp, :], 4),
                                    bc(b3[pp, t, 4 * i:4 * i + 4].unsqueeze(2), [64, 4, 128]), ALU.mult, tp, twt[1, 1])
                            put(k, tk)
                            tvn[i, n] = tt(V, BU[pp, i, t], BU[pp, i, t], tw3, ALU.subtract)
                        else:
                            tvn[i, n] = tbu[i, t]
                        if s < 3:
                            k = get()
                            for h in range(4):
                                tp = mm(banks[k][:, 128 * h:128 * h + 128], KD[pp, i, t, h, :], BU[pp, i, t, h, :], True, True,
                                        tvn[i, n], tkd[i, t], bank_after[k], inc=(h == 3))
                            if s:
                                glb = bc(E[:, t, 16 + 8 * (n % 2) + 4 * i:20 + 8 * (n % 2) + 4 * i].unsqueeze(2), [128, 4, 128])
                                tt(V, ST[:, i, s], ST[:, i, s - 1], glb, ALU.mult)
                                tk = tt(V, ST[:, i, s], ST[:, i, s], v4(banks[k][:, :], 4), ALU.add, tp)
                            else:
                                tk = copy(V, ST[:, i, 0], v4(banks[k][:, :], 4), tp)
                            tS[i, s + 1] = tk
                            put(k, tk)
                    yield
                O = zone(ZTOK, 1024).rearrange("p (t h d) -> p t h d", t=2, h=4)
                t5 = zone(ZAT + 1024, 512)
                for t in range(2):
                    k = get()
                    for h in range(4):
                        for i in range(2):
                            tp = mm(banks[k][:, 128 * h:128 * h + 128], dT[:, i, t, h, :], BU[:, i, t, h, :], i == 0, i == 1,
                                    [tvn[i, 2 * t], tvn[i, 2 * t + 1]], tqkT, bank_after[k], inc=(h == 3 and i == 1))
                    to = copy(V, O[:, t], v4(banks[k][:, :], 4), tp)
                    put(k, to)
                    for i in range(2):
                        hs = [h2 for h2 in range(2) if (2 * t + h2 if i == 0 else 3 - 2 * t - h2) > 0]
                        k = get()
                        for h2 in hs:
                            n = 2 * t + h2
                            s = n if i == 0 else 3 - n
                            for h in range(4):
                                pp = slice(64 * h2, 64 * h2 + 64)
                                tp = mm(banks[k][pp, 128 * h:128 * h + 128],
                                        kqT[:, h, 256 + 128 * t + 64 * h2:256 + 128 * t + 64 * h2 + 64],
                                        ST[:, i, s - 1, h, :], True, True, tS[i, s], bank_after[k], inc=(h == 3))
                        pp = slice(64 * hs[0], 64 * hs[-1] + 64)
                        npp = 64 * len(hs)
                        tk = tt(V, v4(t5[pp, :], 4), v4(banks[k][pp, :], 4),
                                bc(E[pp, t, 4 * i:4 * i + 4].unsqueeze(2), [npp, 4, 128]), ALU.mult, tp)
                        put(k, tk)
                        to = tt(V, O[pp, t], O[pp, t], v4(t5[pp, :], 4), ALU.add)
                    yield
                st["o"] = to

            gg = gates()
            interleave(delta(), gg)
            O = zone(ZTOK, 1024).rearrange("p (t h d) -> p t h d", t=2, h=4)
            st["yb"] = head_norm(O, zone(ZTOK + 1024, 1024), st["o"], pcol(pl["og"]), 1.0, zT, ybT)

            mT = v4(zone(ZLT, 2048), 8)
            ia, wa, twa = take()
            ib, wb, twb = take()
            tmpz = zone(ZAT, 1024)
            for f in range(0, 8, 2):
                ks = []
                for w, tw, y, ty in ((wa, twa, yaT, st["ya"]), (wb, twb, ybT, st["yb"])):
                    k = get()
                    for j in range(2):
                        for c in range(4):
                            tp = mm(banks[k][:, 256 * j:256 * j + 256], w[:, c, 128 * (f + j):128 * (f + j) + 128], y[:, c, :],
                                    c == 0, c == 3, tw, ty, bank_after[k], inc=(j == 1 and c == 3))
                    ks.append((k, tp))
                t1 = v4(tmpz[:, 0:512], 2)
                tk = tt(V, t1, v4(banks[ks[0][0]][:, :], 2), gT[:, f:f + 2, :], ALU.mult, ks[0][1])
                put(ks[0][0], tk)
                t2 = v4(tmpz[:, 512:1024], 2)
                tk = tt(V, t2, v4(banks[ks[1][0]][:, :], 2), gT[:, 8 + f:10 + f, :], ALU.mult, ks[1][1])
                put(ks[1][0], tk)
                tmg = tt(V, mT[:, f:f + 2, :], t1, t2, ALU.add)
            release(ia, tp)
            release(ib, tp)
            tm = ada(l, (4, 5))
            gtB = zone(ZDT, 1024)
            tg = spread(gtB, modT[:, 16:24], tm)
            out_proj(mT, tmg, gtB)

            tm = ada(l, range(6, 12))
            sa2 = sb(f"sb{l}", 8)
            ts(V, sa2[:, :], modT[:, 32:40], 1.0, None, ALU.add, ALU.bypass)
            tsa = tt(V, sa2[:, :], sa2[:, :], pcol(pl["n2"], 8), ALU.mult)
            tg = spread(gtB, modT[:, 40:48], tm)
            tk = normed()
            th = to_hT(xn, lambda c: sa2[:, c:c + 1], lambda c: modT[:, 24 + c:25 + c], tk, None, tsa, tm)
            h1 = v4(zone(0, 8192), 32)
            for j in range(8):
                i, w, tw = take()
                for f in (0, 2):
                    def e(f0, b, tp):
                        rt = v4(zone(8192 + 512 * (f0 // 2), 512), 2)
                        te = act(rt, b, ACT.Relu, tp, th1.get(f0))
                        th1[f0] = tt(V, h1[:, 4 * j + f0:4 * j + f0 + 2, :], rt, rt, ALU.mult, te)
                        return te
                    if j == 0 and f == 0:
                        th1 = {}
                    tp = lin_feat(w, tw, hT3, th, 8, f, e)
                release(i, tp)
            acc_out(h1, list(th1.values()), 8, gtB)

        def acc_out(lhs, tl, nb, gB):
            ks = [get() for _ in range(4)]
            for b in range(nb):
                i, w, tw = take()
                for c in range(4):
                    for t in range(2):
                        for h in range(2):
                            k = ks[2 * t + h]
                            tp = mm(banks[k][:, :], lhs[:, 4 * b + c, 128 * t:128 * t + 128], w[:, c, 512 * h:512 * h + 512],
                                    b == 0 and c == 0, b == nb - 1 and c == 3, tl, tw, bank_after[k],
                                    inc=(c == 3 and t == 1 and h == 1))
                release(i, tp)
            for t in range(2):
                for h in range(2):
                    k = ks[2 * t + h]
                    xs = x3[:, t, 512 * h:512 * h + 512]
                    if gB is not None:
                        tmp = xn[:, 0:512]
                        tk = tt(V, tmp, banks[k][:, :], gB[:, 512 * h:512 * h + 512], ALU.mult, tp)
                        xr[0] = tt(V, xs, xs, tmp, ALU.add)
                    else:
                        tk = xr[0] = tt(V, xs, xs, banks[k][:, :], ALU.add, tp)
                    put(k, tk)

        def out_proj(mT, tmg, gB):
            acc_out(mT, tmg, 2, gB)

        def block2(l):
            pl = pc[l]
            tk = normed()
            th = to_hT(xn, lambda c: pcol(pl["an"] + c), None, tk)
            nab = zone(11840, 2048).rearrange("p (t h r c) -> p t h r c", t=2, h=4, r=4)
            tp_ = None
            A.wait([V.last, (P.sem, P.n)])
            raw = xn[:, :].rearrange("p (t h r c) -> p t h r c", t=2, h=4, r=4)
            for h in range(4):
                for r in range(4):
                    src = bass.AP(tensor=a["na_rpb_2"].tensor, offset=((l * 4 + h) * 15 + 7 - r) * 31 + 15 - 63,
                                  ap=[[1, 64], [31, 4], [1, 64]])
                    tb = l_b.load(A, raw[64 * (r % 2):64 * (r % 2) + 64, r // 2, h], src)
            ro[0] = 0
            prw("sink", a["swa_sink_2"][l], 6)
            P2 = zone(0, 3648).rearrange("p (t n) -> p t n", t=2)
            cc = [0]
            tpj = []
            for j in range(4):
                i, w, tw = take()
                n = 512 if j < 3 else 288

                def e(t, b, tp, j=j, n=n):
                    tpj.append(copy(A if t else V, P2[:, t, 512 * j:512 * j + n], b, tp))
                    return tpj[-1]
                tp = lin_tok(hT3, th, w, tw, n, 8, e)
                release(i, tp)
            n3 = zone(11840, 2048).rearrange("p (a c) -> p a c", a=32)
            for q in range(4):
                k = get()
                tp = mm(banks[k][:, :], K2("flip"), xn[:, 512 * q:512 * q + 512], True, True, tb, t_c2, bank_after[k], inc=True)
                tk = tt(V, n3[:, 8 * q:8 * q + 8, :], v4(banks[k][:, :], 8), bc(K2("na01").unsqueeze(1), [128, 8, 64]), ALU.mult, tp)
                put(k, tk)
            tnab = tt(V, n3, n3, bc(K2("naneg").unsqueeze(1), [128, 32, 64]), ALU.add)
            tmp = zone(16960, 1024)
            ss = S(4)
            for t in range(2):
                tk = act(tmp[:, 0:256], P2[:, t, 768:1024], ACT.Square, tpj, V.last, accum=ss[:, t:t + 1])
                tk = act(tmp[:, 0:128], P2[:, t, 1024:1152], ACT.Square, accum=ss[:, 2 + t:3 + t])
            rsqrt(ss[:, 0:2], ss[:, 0:2], 1.0 / 256)
            tk = rsqrt(ss[:, 2:4], ss[:, 2:4], 1.0 / 128)
            for t in range(2):
                ts(V, P2[:, t, 768:1024], P2[:, t, 768:1024], ss[:, t:t + 1], None, ALU.mult, ALU.bypass, tk)
                tn = ts(V, P2[:, t, 1024:1152], P2[:, t, 1024:1152], ss[:, 2 + t:3 + t], None, ALU.mult, ALU.bypass)
            cqT = v4(zone(22072, 768), 3)
            tcq = []
            for cp in range(2):
                k = get()
                for j in range(2 if cp == 0 else 1):
                    for t in range(2):
                        c0 = 768 + 128 * (2 * cp + j)
                        tp = tr(banks[k][:, 256 * j + 128 * t:256 * j + 128 * t + 128], P2[:, t, c0:c0 + 128], tn, bank_after[k],
                                inc=True)
                for j in range(2 if cp == 0 else 1):
                    g = pcol(pl["qn"] + j) if cp == 0 else pcol(pl["kn"])
                    te = ts(V, cqT[:, 2 * cp + j, :], banks[k][:, 256 * j:256 * j + 256], g, None, ALU.mult, ALU.bypass, tp)
                put(k, te)
            tcq = te
            mq = zone(3648, 1152).rearrange("p (t h d) -> p t h d", t=2, h=6)
            mk = zone(4800, 1152).rearrange("p (t h d) -> p t h d", t=2, h=6)
            mv = zone(5952, 768).rearrange("p (t h d) -> p t h d", t=2, h=6)
            i, w, tw = take()
            for t in range(2):
                for s in range(2):
                    k = get()
                    for c in range(2):
                        tp = mm(banks[k][:, 0:288], cqT[:, c, 128 * t:128 * t + 128], w[:, c, 288 * s:288 * s + 288], c == 0, c == 1,
                                tcq, tw, bank_after[k], inc=(c == 1))
                    te = copy(A, mq[:, t, 3 * s:3 * s + 3, :], v4(banks[k][:, 0:288], 3), tp)
                    put(k, te)
            release(i, tp)
            tmq = te
            i, w, tw = take()
            for t in range(2):
                for s in range(2):
                    k = get()
                    tp = mm(banks[k][:, 0:384], cqT[:, 2, 128 * t:128 * t + 128], w[:, 0, 384 * s:384 * s + 384], True, True,
                            tcq, tw, bank_after[k], inc=True)
                    b = v4(banks[k][:, 0:384], 3)
                    copy(V, mk[:, t, 3 * s:3 * s + 3, 0:64], b[:, :, 0:64], tp)
                    te = copy(V, mv[:, t, 3 * s:3 * s + 3, :], b[:, :, 64:128], tp)
                    put(k, te)
            release(i, tp)
            ta, tb_ = zone(16960, 512), zone(17472, 512)

            def rot(dst, src, n, d, cs, sn, *after):
                a_, b_ = v4(ta[:, 0:n * d], n), v4(tb_[:, 0:n * d], n)
                hd = d // 2
                tt(V, a_, src, bc(cs, [128, n, d]), ALU.mult, *after)
                for h in range(2):
                    tt(V, b_[:, :, hd * h:hd * h + hd], src[:, :, hd - hd * h:2 * hd - hd * h],
                       bc(sn[:, :, hd * h:hd * h + hd], [128, n, hd]), ALU.mult)
                return dst(a_, b_)
            c32, s32 = v4(K2("cos32"), 2), v4(K2("sin32"), 2)
            c64, s64 = v4(K("cos64"), 2), v4(K("sin64"), 2)
            cro = zone(15936, 1024).rearrange("p (t n) -> p t n", t=2)
            for t in range(2):
                rot(lambda x_, y_: tt(V, mq[:, t, :, 64:96], x_, y_, ALU.add), mq[:, t, :, 64:96], 6, 32,
                    c32[:, t:t + 1, :], s32[:, t:t + 1, :], tmq, t_c2)
                kr = P2[:, t, 1152:1184].unsqueeze(1)
                rot(lambda x_, y_: tt(V, mk[:, t, :, 64:96], bc(x_, [128, 6, 32]), bc(y_, [128, 6, 32]), ALU.add), kr, 1, 32,
                    c32[:, t:t + 1, :], s32[:, t:t + 1, :])

                def put_c(x_, y_, t=t):
                    o = cro[:, t, 0:384].rearrange("p (g v d) -> p v g d", g=3, v=2)
                    xq = x_[:, 0:6, :].rearrange("p (v g) d -> p v g d", v=2)
                    yq = y_[:, 0:6, :].rearrange("p (v g) d -> p v g d", v=2)
                    tt(V, o, xq, yq, ALU.add)
                    return tt(V, v4(cro[:, t, 384:512], 2), x_[:, 6:8, :], y_[:, 6:8, :], ALU.add)
                tk = rot(put_c, v4(P2[:, t, 1184:1696], 8), 8, 64, c64[:, t:t + 1, :], s64[:, t:t + 1, :])
            mT = zone(6720, 3072).rearrange("p (h n) -> p h n", h=6)
            cT = v4(zone(9792, 1024), 4)
            aT = v4(zone(10816, 1024), 4)
            tT = []
            n_ = [0]
            for h in range(6):
                k = get()
                for g, src in ((0, mq), (1, mk)):
                    for t in range(2):
                        tp = tr(banks[k][0:96, 256 * g + 128 * t:256 * g + 128 * t + 128], src[:, t, h, :], tk, tmq, bank_after[k],
                                inc=(g == 1 and t == 1))
                te = copy(A if h % 2 else V, mT[0:96, h, :], banks[k][0:96, :], tp)
                put(k, te)
                tT.append(te)
            for dst, src in ((aT, P2[:, :, 0:512]), (cT, cro)):
                for cp in range(2):
                    k = get()
                    for j in range(2):
                        for t in range(2):
                            c0 = 128 * (2 * cp + j)
                            tp = tr(banks[k][:, 256 * j + 128 * t:256 * j + 128 * t + 128], src[:, t, c0:c0 + 128], tk, tpj,
                                    bank_after[k], inc=(j == 1 and t == 1))
                    te = copy(A if cp % 2 else V, dst[:, 2 * cp:2 * cp + 2, :], v4(banks[k][:, :], 2), tp)
                    put(k, te)
                    tT.append(te)
            oc = zone(13888, 2048).rearrange("p (t n) -> p t n", t=2)
            swa = v4(K2("swa"), 2)
            units = []
            for h in range(4):
                pp = slice(64 * (h % 2), 64 * (h % 2) + 64)
                units.append(dict(q=aT[pp, h // 2, :], k=aT[pp, 2 + h // 2, :], bias=nab[:, :, h].rearrange("p t r c -> p t (r c)"),
                                  scale=0.125, sink=None, v=lambda kt, h=h: P2[:, kt, 512 + 64 * h:576 + 64 * h], o=64 * h))
            for h in range(6):
                units.append(dict(q=mT[0:96, h, 0:256], k=mT[0:96, h, 256:512], bias=None, scale=96 ** -0.5, sink=None,
                                  v=lambda kt, h=h: mv[:, kt, h, :], o=256 + 64 * h))
            for h in range(6):
                kv, g = h // 3, h % 3
                pp = slice(64 * kv, 64 * kv + 64)
                units.append(dict(q=cT[pp, g, :], k=cT[pp, 3, :], bias=swa, scale=0.125, sink=rows[:, h:h + 1],
                                  v=lambda kt, kv=kv: P2[:, kt, 1696 + 64 * kv:1760 + 64 * kv], o=640 + 64 * h))
            sc = [zone(19000 + 512 * i, 512) for i in range(6)]
            res = {}
            V.wait([rc["sink"][1]])
            A.wait([rc["sink"][1]])
            for s in range(len(units) + 2):
                if s < len(units):
                    u = units[s]
                    b = s % 2
                    e3, r, te, tr2 = softmax_pair([tT, res.get(("T", s - 2))], u["k"], u["q"], u["bias"], u["scale"], sc[b], sc[2 + b], u["sink"])
                    if s >= 2:
                        pass
                    res[s] = (e3, r, te, tr2)
                if 1 <= s <= len(units):
                    q = s - 1
                    e3, r, te, tr2 = res[q]
                    tk, ptr = probs_T(e3, te, sc[4 + q % 2], A, res.get(("P", q - 2)))
                    A.wait([ptr])
                    res["T", q] = ptr
                    res["tk", q] = tk
                if s >= 2:
                    q = s - 2
                    u = units[q]
                    e3, r, te, tr2 = res[q]
                    k, tp = pv(sc[4 + q % 2], res["tk", q], u["v"], 64, [te, tpj])
                    res["P", q] = tp
                    to = tt(V, oc[:, :, u["o"]:u["o"] + 64], v4(banks[k][:, 0:128], 2), bc(r.unsqueeze(2), [128, 2, 64]), ALU.mult, tp, tr2)
                    put(k, to)
            ss = S(8)
            ss3 = v4(ss[:, 0:6], 2)
            for t in range(2):
                for g, (o0, n) in enumerate(((0, 256), (256, 384), (640, 384))):
                    tk = act(tmp[:, 0:n], oc[:, t, o0:o0 + n], ACT.Square, to, accum=ss3[:, t, g:g + 1])
            rsqrt(ss3[:, :, 0:1], ss3[:, :, 0:1], 1.0 / 256)
            tk = rsqrt(ss3[:, :, 1:3], ss3[:, :, 1:3], 1.0 / 384)
            for t in range(2):
                for g, (o0, n) in enumerate(((0, 256), (256, 384), (640, 384))):
                    tk = ts(V, oc[:, t, o0:o0 + n], oc[:, t, o0:o0 + n], ss3[:, t, g:g + 1], None, ALU.mult, ALU.bypass, tk)
            th = to_hT(zone(13888, 2048), lambda c: pcol(pl["gn"] + c), None, tk)
            out_proj(hT3, th, None)

            tk = normed()
            th = to_hT(xn, lambda c: pcol(pl["fn"] + c), None, tk)
            txn = tk
            i, w, tw = take()
            k = get()
            for t in range(2):
                for c in range(8):
                    tp = mm(banks[k][:, 16 * t:16 * t + 16], hT3[:, c, 128 * t:128 * t + 128], w[:, c, :], c == 0, c == 7,
                            th, tw, bank_after[k], inc=(c == 7))
            release(i, tp)
            aff = zone(12800, 32).rearrange("p (t n) -> p t n", t=2)
            sel = zone(12832, 32).rearrange("p (t n) -> p t n", t=2)
            lg = v4(banks[k][:, 0:32], 2)
            mx, smv = S(2), S(2)
            V(lambda e: e.tensor_reduce(mx, lg, AX.X, ALU.max), tp)
            tk = tt(V, aff, lg, bc(mx.unsqueeze(2), [128, 2, 16]), ALU.subtract)
            put(k, tk)
            tk = act(aff, aff, ACT.Exp, tk)
            V(lambda e: e.tensor_reduce(smv, aff, AX.X, ALU.add), tk)
            V(lambda e: e.reciprocal(smv, smv))
            taff = tt(V, aff, aff, bc(smv.unsqueeze(2), [128, 2, 16]), ALU.mult)
            k = get()
            for t in range(2):
                tp = tr(banks[k][0:16, 128 * t:128 * t + 128], aff[:, t, :], taff, bank_after[k], inc=True)
            w0 = zone(12864, 256)[0:16, :]
            w1 = zone(13120, 256)[0:16, :]
            m8 = zone(13376, 8)[0:16, :]
            tk = copy(V, w0, banks[k][0:16, 0:256], tp)
            put(k, tk)
            ws = [w0, w1]
            for r in range(4):
                s_, d_ = ws[r % 2], ws[1 - r % 2]
                V(lambda e: e.max(m8, s_))
                V(lambda e: e.match_replace(d_, m8, s_, -1.0))
            tk = ts(V, w1, w0, 0.0, None, ALU.is_lt, ALU.bypass)
            k = get()
            for t in range(2):
                tp = tr(banks[k][:, 16 * t:16 * t + 16], w1[:, 128 * t:128 * t + 128], tk, bank_after[k], inc=True)
            tsel = copy(V, sel, v4(banks[k][:, 0:32], 2), tp)
            put(k, tsel)
            k = get()
            mm(banks[k][:, 0:16], K2("triA"), sel[:, 0, :], True, True, tsel, bank_after[k])
            mm(banks[k][:, 16:32], K("ones"), sel[:, 0, :], True, False)
            tp = mm(banks[k][:, 16:32], K2("triA"), sel[:, 1, :], False, True, inc=True)
            pm = S(32)
            pm3 = v4(pm, 2)
            tk = tt(V, pm3, v4(banks[k][:, 0:32], 2), sel, ALU.mult, tp)
            put(k, tk)
            ts(V, pm, pm, -1.0, None, ALU.add, ALU.bypass)
            Pm = zone(0, 1024).rearrange("p (t e s) -> p t e s", t=2, e=16)
            PA = zone(1024, 1024).rearrange("p (t e s) -> p t e s", t=2, e=16)
            for t in range(2):
                tt(V, Pm[:, t], bc(K2("iota").unsqueeze(1), [128, 16, 32]), bc(pm3[:, t, :].unsqueeze(2), [128, 16, 32]), ALU.is_equal)
                tPA = tt(V, PA[:, t], Pm[:, t], bc(aff[:, t, :].unsqueeze(2), [128, 16, 32]), ALU.mult)
            xs = v4(zone(3072, 4096), 8)
            txs = []
            for c in range(8):
                k = get()
                for t in range(2):
                    tp = mm(banks[k][:, :], xn[:, 1024 * t + 128 * c:1024 * t + 128 * c + 128], Pm[:, t].rearrange("p e s -> p (e s)"),
                            t == 0, t == 1, tPA, txn, bank_after[k], inc=(t == 1))
                g = pcol(pl["fn"] + c)
                if c % 2:
                    te = act(xs[:, c, :], banks[k][:, :], ACT.Copy, tp, scale=g)
                else:
                    te = ts(V, xs[:, c, :], banks[k][:, :], g, None, ALU.mult, ALU.bypass, tp)
                put(k, te)
                txs.append(te)
            PW = zone(2048, 1024).rearrange("p (g n) -> p g n", g=4)
            tpw = []
            for gp in range(2):
                k = get()
                for j in range(2):
                    for t in range(2):
                        src = PA[:, t, 4 * (2 * gp + j):4 * (2 * gp + j) + 4, :].rearrange("p e s -> p (e s)")
                        tp = tr(banks[k][:, 256 * j + 128 * t:256 * j + 128 * t + 128], src, tPA, bank_after[k], inc=(j == 1 and t == 1))
                te = copy(A, PW[:, 2 * gp:2 * gp + 2, :], v4(banks[k][:, :], 2), tp)
                put(k, te)
                tpw.append(te)
            hid = [v4(zone(7168 + 256 * b, 256), 8) for b in range(2)]
            sg = [zone(11776 + 256 * b, 256) for b in range(2)]
            Y = v4(zone(7680, 4096), 4)
            thid = {}
            tdn = {}
            tY = []
            yk = None
            for e_ in range(17):
                if e_ < 16:
                    k = get()
                    for m_ in range(2):
                        for hf in range(2):
                            i, w, tw = take()
                            for f in range(4):
                                for c in range(8):
                                    o0 = 256 * m_ + 128 * hf + 32 * f
                                    tp = mm(banks[k][:, o0:o0 + 32], w[:, c, 128 * f:128 * f + 128], xs[:, c, 32 * e_:32 * e_ + 32],
                                            c == 0, c == 7, tw, txs, bank_after[k], inc=(f == 3 and c == 7))
                            release(i, tp)
                    b = e_ % 2
                    g_, u_ = banks[k][:, 0:256], banks[k][:, 256:512]
                    s_ = sg[b]
                    te = act(s_, g_, ACT.Exp, tp, scale=-1.0)
                    ts(V, s_, s_, 1.0, None, ALU.add, ALU.bypass, te)
                    V(lambda e: e.reciprocal(s_, s_))
                    tt(V, s_, g_, s_, ALU.mult)
                    thid[e_] = tt(V, hid[b].rearrange("p c n -> p (c n)"), s_, u_, ALU.mult, tdn.get(e_ - 2))
                    put(k, thid[e_])
                if e_:
                    q = e_ - 1
                    j = q % 4
                    if j == 0:
                        yk = [get(), get()]
                    for bl in range(2):
                        i, w, tw = take()
                        for c in range(4):
                            for hf in range(2):
                                tp = mm(banks[yk[hf]][32 * j:32 * j + 32, :], hid[q % 2][:, 4 * bl + c, :], w[:, c, 512 * hf:512 * hf + 512],
                                        bl == 0 and c == 0, bl == 1 and c == 3, tw, thid[q], bank_after[yk[hf]],
                                        inc=(c == 3 and hf == 1))
                        release(i, tp)
                    tdn[q] = tp
                    if j == 3:
                        for hf in range(2):
                            te = copy(A if hf else V, Y[:, q // 4, 512 * hf:512 * hf + 512], banks[yk[hf]][:, :], tp)
                            put(yk[hf], te)
                            tY.append(te)
            for t in range(2):
                for hf in range(2):
                    k = get()
                    for g in range(4):
                        tp = mm(banks[k][:, :], PW[:, g, 128 * t:128 * t + 128], Y[:, g, 512 * hf:512 * hf + 512], g == 0, g == 3,
                                tpw, tY, bank_after[k], inc=(g == 3))
                    xs_ = x3[:, t, 512 * hf:512 * hf + 512]
                    xr[0] = tt(V, xs_, xs_, banks[k][:, :], ALU.add, tp)
                    put(k, xr[0])

        l_b = Landing()
        for l in range(2):
            block1(l)
        A.wait([V.last, (P.sem, P.n)])
        l_c2 = Landing()
        t_c2 = l_c2.load(A, ar[:, C2B:AR], a["c2"])
        for l in range(2):
            block2(l)
        fg = zone(0, 1024)
        A.wait([V.last, (P.sem, P.n)])
        tf = l_r.load(A, fg, a["final_norm_2"].partition_broadcast(128))
        tk = normed()
        l_o = Landing()
        for t in range(2):
            tk = tt(V, xn[:, 1024 * t:1024 * t + 1024], xn[:, 1024 * t:1024 * t + 1024], fg, ALU.mult, tf)
        to = l_o.load(SP, out[0].rearrange("(t p) d -> p t d", p=128), xn[:, :].rearrange("p (t d) -> p t d", t=2), tk)
        SP.wait([to])
        assert nxt[0] == len(blocks)


_INS = ['x', 'c', 'ada_w', 'ada_b', 'norm1_g', 'norm2_g', 'w_in', 'dn_conv', 'dn_A_log', 'dn_dt_bias', 'dn_out_gain',
        'qk_norm_gain', 'diff_lambda', 'diff_subln_gain', 'w_branch_a', 'w_branch_b', 'w_out', 'w_mlp1', 'w_mlp2',
        'attn_norm_2', 'w_in_2', 'na_rpb_2', 'mla_q_norm_2', 'mla_w_uq_2', 'mla_kv_norm_2', 'mla_w_ukv_2', 'swa_sink_2',
        'group_norm_2', 'w_out_2', 'ffn_norm_2', 'w_router_2', 'w_gate_2', 'w_up_2', 'w_down_2', 'final_norm_2']


def kernel(**inputs):
    import numpy as _np
    import concourse.bacc as _bacc
    from concourse import mybir as _mybir
    from concourse.bass_utils import run_bass_kernel_spmd as _run

    nc = _bacc.Bacc("TRN2", target_bir_lowering=False, num_devices=1)
    (o1, c1), (o2, c2) = const_arrays()
    arrays, aps = {}, {}
    for name in _INS:
        v = _np.ascontiguousarray(inputs[name])
        arrays[f"in_{name}_dram"] = v
        aps[name] = nc.dram_tensor(f"in_{name}_dram", v.shape, _mybir.dt.from_np(v.dtype), kind="ExternalInput").ap()
    for name, v in (("c1", c1), ("c2", c2)):
        arrays[f"in_{name}_dram"] = v
        aps[name] = nc.dram_tensor(f"in_{name}_dram", v.shape, _mybir.dt.from_np(v.dtype), kind="ExternalInput").ap()
    out = nc.dram_tensor("out_0_dram", (1, 256, 1024), F32, kind="ExternalOutput").ap()
    program(nc, aps, o1, o2, out)
    r = _run(nc, [arrays], core_ids=[0])
    return r.results[0]["out_0_dram"]
```

```python
import math
from contextlib import ExitStack

import numpy as np
import concourse.bass as bass
from concourse import mybir

F32 = mybir.dt.float32
I32 = mybir.dt.int32
ALU = mybir.AluOpType
ACT = mybir.ActivationFunctionType
AX = mybir.AxisListType
EPS = 1e-6
NR = 4


def const_arrays():
    i = np.arange(128)
    m, c = i[:, None], i[None, :]
    same = (m // 64) == (c // 64)
    cols = {}
    cols["ident"] = (m == c)
    cols["ones"] = np.ones((128, 128))
    cols["triF"] = same & (m <= c)
    cols["triB"] = same & (m >= c)
    cols["blk"] = same
    cols["half0"] = (m < 64) & (c >= 0)
    cols["half1"] = (m >= 64) & (c >= 0)
    for s in range(6):
        b = 1 << s
        up = ((m // (2 * b)) == (c // (2 * b))) & ((m // b) % 2 == 0) & ((c // b) % 2 == 1)
        cols[f"lvF{s}"] = up
        cols[f"lvB{s}"] = up.T
    pos = np.arange(256, dtype=np.float32)

    def rope(dim):
        inv = (1.0 / (np.float32(10000.0) ** (np.arange(0, dim, 2, dtype=np.float32) / np.float32(dim)))).astype(np.float32)
        ang = pos[:, None] * inv[None, :]
        cs, sn = np.cos(ang), np.sin(ang)
        cs = np.concatenate([cs, cs], -1).reshape(2, 128, dim).transpose(1, 0, 2).reshape(128, 2 * dim)
        sn = np.concatenate([-sn, sn], -1).reshape(2, 128, dim).transpose(1, 0, 2).reshape(128, 2 * dim)
        return cs, sn
    cols["cos64"], cols["sin64"] = rope(64)
    cols["eps"] = np.full((128, 1), EPS)
    a = {k: np.asarray(v, np.float32) for k, v in cols.items()}
    two = {}
    two["triA"] = (m <= c)
    two["cos32"], two["sin32"] = rope(32)
    q, k = (i % 64)[:, None], np.arange(64)[None, :]
    st = np.clip(q - 8, 0, 48)
    win = (k >= st) & (k < st + 16)
    two["na01"] = win
    two["naneg"] = np.where(win, 0.0, -1e30)
    kk = np.arange(256)[None, :]
    two["swa"] = np.concatenate([np.where(np.abs((i + 128 * t)[:, None] - kk) <= 128, 0.0, -1e30) for t in range(2)], 1)
    two["flip"] = ((m // 64) == (c // 64)) & (m % 64 == 63 - c % 64)
    two["iota"] = np.broadcast_to(np.arange(32), (128, 32))
    b = {k: np.asarray(v, np.float32) for k, v in two.items()}

    def pack(d):
        off, o = {}, 0
        for n, v in d.items():
            off[n] = (o, v.shape[1])
            o += v.shape[1]
        return off, np.ascontiguousarray(np.concatenate(list(d.values()), 1), dtype=np.float32)
    return pack(a), pack(b)


class Queue:

    def __init__(self, nc, eng, new_sem, chained):
        self.nc, self.eng, self.new_sem, self.chained = nc, eng, new_sem, chained
        self.sem, self.n, self.seen, self.last = new_sem(), 0, {}, None

    def wait(self, toks):
        for t in toks:
            if t is None:
                continue
            if isinstance(t, list):
                self.wait(t)
                continue
            s, v = t
            if self.seen.get(id(s), 0) < v:
                self.eng.wait_ge(s, v)
                self.seen[id(s)] = v

    def __call__(self, fn, *after, inc=True):
        self.wait(after)
        if self.chained and self.last is not None:
            self.wait([self.last])
        ins = fn(self.eng)
        if not inc:
            return None
        if self.n >= 30000:
            self.sem, self.n = self.new_sem(), 0
        self.n += 1
        ins.then_inc(self.sem, 1)
        self.last = (self.sem, self.n)
        return self.last


def program(nc, a, c1off, c2off, out):
    ctx = ExitStack()
    with ctx:
        names = [0]

        def new_sem():
            names[0] += 1
            return ctx.enter_context(nc.semaphore(f"s{names[0]}"))

        def sb(name, n):
            return ctx.enter_context(nc.sbuf_tensor(name, [128, n], F32))

        P = Queue(nc, nc.tensor, new_sem, False)
        V = Queue(nc, nc.vector, new_sem, True)
        A = Queue(nc, nc.scalar, new_sem, True)
        G = Queue(nc, nc.gpsimd, new_sem, True)
        SP = Queue(nc, nc.sync, new_sem, False)

        class Landing:

            def __init__(self):
                self.sem, self.n = new_sem(), 0

            def load(self, q, dst, src, *after, slow=False):
                q.wait(after)
                self.n += 16
                q.eng.dma_start(dst, src, allow_slow_non_contiguous=slow).then_inc(self.sem, 16)
                return (self.sem, self.n)

        C1N = sum(n for _, n in c1off.values())
        C2N = sum(n for _, n in c2off.values())
        c1 = sb("c1", C1N)
        ring = sb("ring", NR * 4096)
        x = sb("x", 2048)
        xn = sb("xn", 2048)
        hT = sb("hT", 2048)
        AR = 25704
        ar = sb("ar", AR)
        par = sb("par", 3 * 128)
        gper = sb("gper", 160)
        rows = sb("rows", 300)
        small = sb("small", 1024)
        banks = [ctx.enter_context(nc.psum_tensor(f"pb{i}", [128, 512], F32)) for i in range(8)]

        def K(n):
            o, w = c1off[n]
            return c1[:, o:o + w]

        C2B = AR - C2N

        def K2(n):
            o, w = c2off[n]
            return ar[:, C2B + o:C2B + o + w]

        def zone(o, n):
            return ar[:, o:o + n]

        sm_at = [0]

        def S(n):
            if sm_at[0] + n > 1024:
                sm_at[0] = 0
            o = sm_at[0]
            sm_at[0] += n
            return small[:, o:o + n]

        bank_after = [None] * 8
        busy = [False] * 8
        bank_i = [0]

        def get():
            for _ in range(8):
                k = bank_i[0] % 8
                bank_i[0] += 1
                if not busy[k]:
                    busy[k] = True
                    return k
            raise RuntimeError("no bank")

        def put(k, tok):
            busy[k] = False
            bank_after[k] = tok

        def mm(o, l, r, start, stop, *after, inc=False):
            return P(lambda e: e.matmul(o, l, r, start=start, stop=stop), *after, inc=inc)

        def tr(o, i, *after, inc=False):
            n = i.shape[0]
            p0 = 0
            return P(lambda e: e.transpose(o, i, K("ident")[p0:p0 + n, 0:n]), *after, inc=inc)

        def tt(q, o, i0, i1, op, *after):
            return q(lambda e: e.tensor_tensor(o, i0, i1, op), *after)

        def ts(q, o, i, s1, s2, op0, op1, *after):
            return q(lambda e: e.tensor_scalar(o, i, s1, s2, op0, op1), *after)

        def stt(o, i0, s, i1, op0, op1, *after):
            return V(lambda e: e.scalar_tensor_tensor(out=o, in0=i0, scalar=s, in1=i1, op0=op0, op1=op1), *after)

        def act(o, i, f, *after, bias=None, scale=1.0, accum=None):
            kw = {}
            if bias is not None:
                kw["bias"] = bias
            if accum is not None:
                kw["accum_out"] = accum
            return A(lambda e: e.activation(o, i, f, scale=scale, **kw), *after)

        def copy(q, o, i, *after):
            if q is A:
                return A(lambda e: e.copy(o, i), *after)
            return q(lambda e: e.tensor_copy(o, i), *after)

        def bc(ap, shape):
            return ap.broadcast_to(shape)

        blocks = []

        def cols(w, c0, n):
            blocks.append(([w.rearrange("(c p) n -> p c n", p=128)[:, :, c0:c0 + n]], w.shape[0] // 128, n))

        def rws(w, k0, nk):
            blocks.append(([w.rearrange("(c p) n -> p c n", p=128)[:, k0:k0 + nk, :]], nk, w.shape[1]))

        def pair(w, w2, k0):
            blocks.append(([m.rearrange("(c p) n -> p c n", p=128)[:, k0:k0 + 2, :] for m in (w, w2)], 4, w.shape[1]))

        for l in range(2):
            ad = [(lambda j=j: cols(a["ada_w"][0], 512 * j, 512)) for j in range(12)] if l == 0 else []
            for j in range(4 if l == 0 else 0):
                ad[j]()
            for j in range(6):
                cols(a["w_in"][l], 512 * j, 512)
                if l == 0 and j < 4:
                    ad[4 + 2 * j]()
                    ad[5 + 2 * j]()
            cols(a["w_in"][l], 3584, 16)
            cols(a["w_in"][l], 3072, 512)
            for j in range(4):
                cols(a["w_in"][l], 3600 + 512 * j, 512)
            rws(a["w_branch_a"][l], 0, 4)
            rws(a["w_branch_b"][l], 0, 4)
            rws(a["w_out"][l], 0, 4)
            rws(a["w_out"][l], 4, 4)
            for j in range(8):
                cols(a["w_mlp1"][l], 512 * j, 512)
                if l == 0:
                    cols(a["ada_w"][1], 512 * j, 512)
            for j in range(8):
                rws(a["w_mlp2"][l], 4 * j, 4)
                if l == 0 and j < 4:
                    cols(a["ada_w"][1], 512 * (8 + j), 512)
        for l in range(2):
            for j in range(4):
                cols(a["w_in_2"][l], 512 * j, 512 if j < 3 else 288)
            rws(a["mla_w_uq_2"][l], 0, 2)
            rws(a["mla_w_ukv_2"][l], 0, 1)
            rws(a["w_out_2"][l], 0, 4)
            rws(a["w_out_2"][l], 4, 4)
            cols(a["w_router_2"][l], 0, 16)
            for e in range(17):
                if e < 16:
                    for j in range(4):
                        pair(a["w_gate_2"][l, e], a["w_up_2"][l, e], 2 * j)
                if e:
                    rws(a["w_down_2"][l, e - 1], 0, 4)
                    rws(a["w_down_2"][l, e - 1], 4, 4)

        landed = [Landing() for _ in range(NR)]
        got = {}
        used = {}

        def issue(i):
            if i >= len(blocks):
                return
            src, k, n = blocks[i]
            s = i % NR
            dst = ring[:, s * 4096:s * 4096 + k * n].rearrange("p (k n) -> p k n", k=k)
            kk = k // len(src)
            for m_, sr in enumerate(src):
                tk = landed[s].load(SP, dst[:, kk * m_:kk * m_ + kk, :], sr, used.get(i - NR), slow=n < 128)
            got[i] = (dst, tk)
        nxt = [0]
        for i in range(NR):
            issue(i)

        def take():
            i = nxt[0]
            nxt[0] += 1
            return i, got[i][0], got[i][1]

        def release(i, tok):
            used[i] = tok
            issue(i + NR)

        l_c = Landing()
        t_c = l_c.load(A, c1[:, :], a["c1"])
        l_p = Landing()
        stage = zone(0, 384)
        pd = []

        def prow(k, r0, src, n):
            pd.append(l_p.load(A, stage[r0:r0 + n, 128 * k:128 * k + 128], src))
            return 128 * k + r0

        def r128(ap):
            return ap.rearrange("(r q) -> r q", q=128)

        t_z = V(lambda e: e.memset(stage, 0.0))
        A.wait([t_z])
        pc = [{}, {}]
        for l in range(2):
            d = pc[l]
            d["n1"] = prow(l, 0, r128(a["norm1_g"][l]), 8)
            d["n2"] = prow(l, 8, r128(a["norm2_g"][l]), 8)
            d["ada_b"] = prow(l, 16, r128(a["ada_b"][l]), 48)
            d["og"] = prow(l, 64, r128(a["dn_out_gain"][l]), 1)
            d["sg"] = prow(l, 65, r128(a["diff_subln_gain"][l]), 1)
            d["cv"] = prow(l, 66, a["dn_conv"][l].rearrange("k (f q) -> (k f) q", q=128), 60)
            o = 8 + 27 * l
            d["an"] = prow(2, o, r128(a["attn_norm_2"][l]), 8)
            d["fn"] = prow(2, o + 8, r128(a["ffn_norm_2"][l]), 8)
            d["gn"] = prow(2, o + 16, r128(a["group_norm_2"][l]), 8)
            d["qn"] = prow(2, o + 24, r128(a["mla_q_norm_2"][l]), 2)
            d["kn"] = prow(2, o + 26, r128(a["mla_kv_norm_2"][l]), 1)
        p_c = prow(2, 0, a["c"].rearrange("a (r q) -> (a r) q", q=128), 8)

        def pcol(o, n=1):
            return par[:, o:o + n]

        l_x = Landing()
        xd = a["x"][0].rearrange("(t p) d -> p t d", p=128)
        x3 = x[:, :].rearrange("p (t d) -> p t d", t=2)
        t_x = l_x.load(A, x3, xd)

        l_r = Landing()
        rc = {}
        ro = [0]

        def prw(name, ap, n):
            o = ro[0]
            ro[0] += n
            rc[name] = (o, l_r.load(A, rows[:, o:o + n], ap.partition_broadcast(128)))
            return o

        k = get()
        tp = None
        for j in range(3):
            tp = tr(banks[k][:, 128 * j:128 * j + 128], stage[:, 128 * j:128 * j + 128], pd[-1], t_c, inc=True)
        t_par = copy(V, par[:, :], banks[k][:, 0:384], tp)
        put(k, t_par)
        c_act = S(8)
        sctmp = S(8)

        t = act(sctmp, pcol(p_c, 8), ACT.Tanh, t_par, scale=0.5)
        cact = sb("cact", 8)
        ts(V, sctmp, sctmp, 0.5, 0.5, ALU.mult, ALU.add, t)
        t_cact = tt(V, cact[:, :], sctmp, pcol(p_c, 8), ALU.mult)
        for l in range(2):
            o_ = pc[l]["cv"]
            t_cact = ts(V, pcol(o_, 60), pcol(o_, 60), 0.5, None, ALU.mult, ALU.bypass)

        def rsqrt(o, i, scale, *after):
            n = 1
            for d in i.shape[1:]:
                n *= d
            v, q = S(n), S(n)
            if len(i.shape) == 3:
                v, q = v4(v, i.shape[1]), v4(q, i.shape[1])
            ts(V, v, i, scale, EPS, ALU.mult, ALU.add, *after)
            ts(V, o.bitcast(I32), v.bitcast(I32), -0.5, 1597463007.0, ALU.mult, ALU.add)
            for _ in range(3):
                tt(V, q, o, o, ALU.mult)
                stt(q, q, -0.5, v, ALU.mult, ALU.mult)
                tk = stt(o, q, 1.5, o, ALU.add, ALU.mult)
            return tk

        def v4(ap, *d):
            s = " ".join("abcdef"[:len(d) + 1])
            kw = {"abcdef"[i]: d[i] for i in range(len(d))}
            return ap.rearrange("p (" + s + ") -> p " + s, **kw)

        xr = [None]

        def normed(*after):
            ss = S(2)
            junk = hT[:, 0:1024]
            for t in range(2):
                ta = act(junk, x3[:, t, :], ACT.Square, t_x, xr[0], *after, accum=ss[:, t:t + 1])
            r = S(2)
            ta = rsqrt(r, ss, 1.0 / 1024, ta)
            tk = None
            for t in range(2):
                tk = ts(V, xn[:, 1024 * t:1024 * t + 1024], x3[:, t, :], r[:, t:t + 1], None, ALU.mult, ALU.bypass, ta)
            return tk

        hT3 = hT[:, :].rearrange("p (c n) -> p c n", c=8)

        def to_hT(src, sa, sbias, tk, dst=None, *after):
            dst = hT3 if dst is None else dst
            toks = []
            for cp in range(4):
                k = get()
                for j in range(2):
                    for t in range(2):
                        cc = 2 * cp + j
                        tp = tr(banks[k][:, 256 * j + 128 * t:256 * j + 128 * t + 128],
                                src[:, 1024 * t + 128 * cc:1024 * t + 128 * cc + 128], tk, t_c, bank_after[k],
                                inc=(j == 1 and t == 1))
                for j in range(2):
                    cc = 2 * cp + j
                    i = banks[k][:, 256 * j:256 * j + 256]
                    if cp % 2:
                        if sbias is None:
                            te = act(dst[:, cc, :], i, ACT.Copy, tp, *after, scale=sa(cc))
                        else:
                            te = act(dst[:, cc, :], i, ACT.Identity, tp, *after, scale=sa(cc), bias=sbias(cc))
                    else:
                        s2 = None if sbias is None else sbias(cc)
                        te = ts(V, dst[:, cc, :], i, sa(cc), s2, ALU.mult, ALU.bypass if s2 is None else ALU.add, tp, *after)
                put(k, te)
                toks.append(te)
            return toks

        def lin_tok(lhs, tl, w, tw, n, nk, evac, k0=0):
            tp = None
            for t in range(2):
                k = get()
                for c in range(nk):
                    tp = mm(banks[k][:, 0:n], lhs[:, k0 + c, 128 * t:128 * t + 128], w[:, c, 0:n], c == 0, c == nk - 1,
                            tl, tw, bank_after[k], inc=(c == nk - 1))
                put(k, evac(t, banks[k][:, 0:n], tp))
            return tp

        def lin_feat(w, tw, rhs, tr_, nk, f0, evac):
            k = get()
            tp = None
            for j in range(2):
                for c in range(nk):
                    tp = mm(banks[k][:, 256 * j:256 * j + 256], w[:, c, 128 * (f0 + j):128 * (f0 + j) + 128],
                            rhs[:, c, :], c == 0, c == nk - 1, tr_, tw, bank_after[k], inc=(c == nk - 1 and j == 1))
            put(k, evac(f0, banks[k][:, :].rearrange("p (j n) -> p j n", j=2), tp))
            return tp

        modT2 = [sb(f"modT{l}", 48) for l in range(2)]
        ada_at = [0]
        ada_read = [None, None]

        def ada_v(l, j, z):
            i, w, tw = take()
            b = ada_at[0] % 2
            ada_at[0] += 1
            acc = zone(z + 512 * b, 512)
            ts(V, acc, w[:, 0, :], cact[:, 0:1], None, ALU.mult, ALU.bypass, tw, t_cact, ada_read[b])
            for c in range(1, 8):
                tk = stt(acc, w[:, c, :], cact[:, c:c + 1], acc, ALU.mult, ALU.add)
            release(i, tk)
            return l, j, b, acc, tk

        def ada_pe(state):
            l, j, b, acc, tk = state
            k = get()
            for f in range(4):
                tp = mm(banks[k][:, f:f + 1], acc[:, 128 * f:128 * f + 128], K("ones")[:, 0:1], True, True, tk, t_c,
                        bank_after[k], inc=(f == 3))
            ada_read[b] = tp
            tk = tt(V, modT2[l][:, 4 * j:4 * j + 4], banks[k][:, 0:4], pcol(pc[l]["ada_b"] + 4 * j, 4), ALU.add, tp)
            put(k, tk)
            return tk

        def spread(dst, src, tk, *after):
            dg = S(128)
            for h in range(2):
                k = get()
                for c in range(4):
                    td = ts(V, dg, K("ident"), src[:, 4 * h + c:4 * h + c + 1], None, ALU.mult, ALU.bypass, tk,
                            tk if c == 0 and h == 0 else tp)
                    tp = mm(banks[k][:, 128 * c:128 * c + 128], K("ones"), dg, True, True, td, bank_after[k], inc=True)
                te = copy(V, dst[:, 512 * h:512 * h + 512], banks[k][:, :], tp, *after)
                put(k, te)
            return te

        def interleave(*gens):
            live = list(gens)
            while live:
                for g in list(live):
                    try:
                        next(g)
                    except StopIteration:
                        live.remove(g)

        def softmax_pair(tl, kT, qT, bias, scale, sc_s, sc_e, sink):
            k = get()
            for t in range(2):
                tp = mm(banks[k][:, 256 * t:256 * t + 256], qT[:, 128 * t:128 * t + 128], kT, True, True,
                        tl, bank_after[k], inc=(t == 1))
            b3 = banks[k][:, :].rearrange("p (t n) -> p t n", t=2)
            e3 = sc_e.rearrange("p (t n) -> p t n", t=2)
            src, sc = b3, scale
            if bias is not None:
                s3 = sc_s.rearrange("p (t n) -> p t n", t=2)
                tk = stt(s3, b3, scale, bias, ALU.mult, ALU.add, tp)
                put(k, tk)
                src, sc = s3, 1.0
            mx, nm, smv = S(2), S(2), S(2)
            V(lambda e: e.tensor_reduce(mx, src, AX.X, ALU.max), tp)
            if sink is not None:
                ts(V, mx, mx, sink, None, ALU.max, ALU.bypass)
            tn = ts(V, nm, mx, -sc, None, ALU.mult, ALU.bypass)
            for t in range(2):
                te = act(e3[:, t, :], src[:, t, :], ACT.Exp, tn, tp, bias=nm[:, t:t + 1], scale=sc,
                         accum=smv[:, t:t + 1])
            if bias is None:
                put(k, te)
            if sink is not None:
                es = S(2)
                te = act(es, nm, ACT.Exp, bias=sink)
                tt(V, smv, smv, es, ALU.add, te)
            r = S(2)
            tk = V(lambda e: e.reciprocal(r, smv), te)
            return e3, r, te, tk

        def probs_T(e3, te, sc_t, q, *after):
            k = get()
            for t in range(2):
                for kt in range(2):
                    tp = tr(banks[k][:, 256 * t + 128 * kt:256 * t + 128 * kt + 128], e3[:, t, 128 * kt:128 * kt + 128],
                            te, bank_after[k], inc=(t == 1 and kt == 1))
            tk = copy(q, sc_t, banks[k][:, :], tp, *after)
            put(k, tk)
            return tk, tp

        def pv(sc_t, tk, v, dv, tv):
            k = get()
            for t in range(2):
                for kt in range(2):
                    tp = mm(banks[k][:, dv * t:dv * t + dv], sc_t[:, 256 * t + 128 * kt:256 * t + 128 * kt + 128],
                            v(kt), kt == 0, kt == 1, tk, tv, bank_after[k], inc=(t == 1 and kt == 1))
            return k, tp

        Z1, ZST, ZTOK, ZDT, ZLT, ZAT, ZG, ZZ, ZY = 0, 6144, 9264, 12336, 14384, 16432, 18480, 22576, 23600
        tmod = [None]

        def block1(l):
            pl = pc[l]
            modT = modT2[l]
            if l == 0:
                ads = [ada_v(0, j, 18480) for j in range(2)]
                ads = [ada_pe(q) for q in ads] and [ada_v(0, j, 18480) for j in range(2, 4)]
                tmod[0] = [ada_pe(q) for q in ads][-1]
            tm = tmod[0]
            sa = S(8)
            ts(V, sa, modT[:, 8:16], 1.0, None, ALU.add, ALU.bypass)
            sa1 = sb(f"sa{l}", 8)
            tsa = tt(V, sa1[:, :], sa, pcol(pl["n1"], 8), ALU.mult)
            tk = normed()
            th = to_hT(xn, lambda c: sa1[:, c:c + 1], lambda c: modT[:, c:c + 1], tk, None, tsa, tm)

            qk = xn[:, :].rearrange("p (t n) -> p t n", t=2)
            vA = zone(ZLT, 1024).rearrange("p (t n) -> p t n", t=2)
            ev = {}

            def plain(dst, q):
                def f(t, b, tp):
                    ev[0] = copy(q, dst(t), b, tp)
                    return ev[0]
                return f
            ads = []
            for j in range(3):
                i, w, tw = take()
                if j < 2:
                    tp = lin_tok(hT3, th, w, tw, 512, 8, plain(lambda t: qk[:, t, 512 * j:512 * j + 512], A))
                else:
                    tp = lin_tok(hT3, th, w, tw, 512, 8, plain(lambda t: vA[:, t, :], A))
                release(i, tp)
                tevj = ev[0]
                if j == 1:
                    tqk = tevj
                for q in ads:
                    tmod[0] = ada_pe(q)
                if l == 0:
                    ads = [ada_v(0, 4 + 2 * j + q, ZZ) for q in range(2)]
            tvA = tevj

            ro[0] = 0
            if l:
                A.wait([V.last])
            prw("qkg", a["qk_norm_gain"][l].rearrange("a d -> (a d)"), 128)
            prw("al", a["dn_A_log"][l].rearrange("a d -> (a d)"), 8)
            prw("dt", a["dn_dt_bias"][l].rearrange("a d -> (a d)"), 8)
            lamd = zone(ZY, 256)
            tl_ = l_r.load(A, lamd, a["diff_lambda"][l].rearrange("a d -> (a d)").partition_broadcast(128))

            cin = zone(ZST, 3120).rearrange("p (f n) -> p f n", f=12)
            tpad = V(lambda e: e.memset(cin[:, :, 0:2], 0.0))
            tpad = V(lambda e: e.memset(cin[:, :, 258:260], 0.0))
            babs = sb(f"ba{l}", 32)
            ba = babs[:, :].rearrange("p (t n) -> p t n", t=2)
            st = {}
            zT = zone(ZZ, 1024).rearrange("p (f n) -> p f n", f=4)
            gT = zone(ZG, 4096).rearrange("p (f n) -> p f n", f=16)
            yaT = zone(ZY, 1024).rearrange("p (f n) -> p f n", f=4)
            ybT = zone(ZY + 1024, 1024).rearrange("p (f n) -> p f n", f=4)

            def proj_dn():
                pend = None
                ads2 = None
                for j in range(3):
                    i, w, tw = take()
                    for f in (0, 2):
                        def e(f0, b, tp, j=j):
                            q = A if f0 else V
                            st["cin", j, f0] = copy(q, cin[:, 4 * j + f0:4 * j + f0 + 2, 2:258], b, tp)
                            return st["cin", j, f0]
                        u = feat_steps(w, tw, f, e, i if f else None)
                        next(u)
                        yield
                        if pend is not None:
                            next(pend, None)
                        next(u)
                        pend = u
                        yield
                    if l == 0 and j < 2:
                        for q in (ads if j == 0 else ads2):
                            tmod[0] = ada_pe(q)
                        if j == 0:
                            ads2 = [ada_v(0, 10 + q, ZZ) for q in range(2)]
                next(pend, None)
                i, w, tw = take()

                def e(t, b, tp):
                    st["ba"] = copy(V, ba[:, t, :], b, tp)
                    return st["ba"]
                tp = lin_tok(hT3, th, w, tw, 16, 8, e)
                release(i, tp)
                yield
                st["proj"] = True

            def gates():
                pend = None
                for j in range(5):
                    i, w, tw = take()
                    for f in (0, 2):
                        def e(f0, b, tp, j=j):
                            dst = zT[:, f0:f0 + 2, :] if j == 0 else gT[:, 4 * (j - 1) + f0:4 * (j - 1) + f0 + 2, :]
                            te = act(dst, b, ACT.Tanh, tp, st["rope_done"], scale=0.5)
                            if j == 0:
                                te = stt(dst, dst, 1.0, b, ALU.add, ALU.mult, te)
                            st["gates"] = te
                            return te
                        u = feat_steps(w, tw, f, e, i if f else None)
                        next(u)
                        yield
                        if pend is not None:
                            next(pend, None)
                        next(u)
                        pend = u
                        yield
                next(pend, None)

            def feat_steps(w, tw, f0, evac, blk):
                k = get()
                for j in range(2):
                    for c in range(8):
                        tp = mm(banks[k][:, 256 * j:256 * j + 256], w[:, c, 128 * (f0 + j):128 * (f0 + j) + 128],
                                hT3[:, c, :], c == 0, c == 7, th, tw, bank_after[k], inc=(c == 7 and j == 1))
                    if j == 1 and blk is not None:
                        release(blk, tp)
                    yield
                put(k, evac(f0, banks[k][:, :].rearrange("p (j n) -> p j n", j=2), tp))

            def attn_a():
                g = rows[:, 0:128]
                tr_ = rc["dt"][1]
                cg, sg = zone(ZY + 256, 256), zone(ZY + 512, 256)
                cg4 = v4(cg, 2, 2)
                sg4 = v4(sg, 2, 2)
                cosr = v4(K("cos64"), 2)
                sinr = v4(K("sin64"), 2)
                for t in range(2):
                    tt(V, cg4[:, t], bc(cosr[:, t:t + 1, :], [128, 2, 64]), v4(g, 2), ALU.mult, tr_, tl_, t_c)
                    for h in range(2):
                        tt(V, sg4[:, t, :, 32 * h:32 * h + 32], bc(sinr[:, t:t + 1, 32 * h:32 * h + 32], [128, 2, 32]),
                           v4(g, 2)[:, :, 32 - 32 * h:64 - 32 * h], ALU.mult)
                l4 = v4(lamd, 4)
                pr = S(128)
                p3 = v4(pr, 2)
                l2 = lamd.rearrange("p (a b d) -> p a b d", a=2, b=2)
                tt(V, p3, l2[:, :, 0, :], l2[:, :, 1, :], ALU.mult)
                sl = S(2)
                tk = V(lambda e: e.tensor_reduce(sl, p3, AX.X, ALU.add))
                tk = act(sl, sl, ACT.Exp, tk)
                lam = sb(f"lam{l}", 1)
                tt(V, lam[:, :], sl[:, 0:1], sl[:, 1:2], ALU.subtract, tk)
                li = 0.8 - 0.6 * math.exp(-0.3 * l)
                ts(V, lam[:, :], lam[:, :], li, None, ALU.add, ALU.bypass)
                sq = zone(ZG, 2048)
                t1 = zone(ZG + 2048, 2048)
                tk = act(sq, xn[:, :], ACT.Square, tqk)
                ss = S(32)
                tk = V(lambda e: e.tensor_reduce(ss, v4(sq, 32), AX.X, ALU.add), tk)
                tk = rsqrt(ss, ss, 1.0 / 64, tk)
                q32 = v4(xn[:, :], 32)
                yield
                tt(V, q32, q32, bc(ss.unsqueeze(2), [128, 32, 64]), ALU.mult, tk, tqk)
                yield
                t14 = t1.rearrange("p (a g d) -> p a g d", a=4, g=8)
                sq4 = sq.rearrange("p (a g d) -> p a g d", a=4, g=8)
                q4 = xn[:, :].rearrange("p (a g d) -> p a g d", a=4, g=8)
                cga = cg.rearrange("p (a d) -> p a d", a=4)
                sga = sg.rearrange("p (a d) -> p a d", a=4)
                for i in range(4):
                    tt(V, t14[:, i], q4[:, i], bc(cga[:, i:i + 1, :], [128, 8, 64]), ALU.mult)
                    for h in range(2):
                        tt(V, sq4[:, i, :, 32 * h:32 * h + 32], q4[:, i, :, 32 - 32 * h:64 - 32 * h],
                           bc(sga[:, i:i + 1, 32 * h:32 * h + 32], [128, 8, 32]), ALU.mult)
                    yield
                tk = tt(V, t1, t1, sq, ALU.add)
                QT = v4(zone(ZDT, 2048), 8)
                t13 = v4(t1, 2)
                for cp in range(4):
                    k = get()
                    for j in range(2):
                        for t in range(2):
                            cc = 2 * cp + j
                            tp = tr(banks[k][:, 256 * j + 128 * t:256 * j + 128 * t + 128],
                                    t13[:, t, 128 * cc:128 * cc + 128], tk, bank_after[k], inc=(j == 1 and t == 1))
                    tq = copy(A if cp % 2 else V, QT[:, 2 * cp:2 * cp + 2, :], v4(banks[k][:, :], 2), tp)
                    put(k, tq)
                    st["qT", cp] = tq
                    yield
                tq = [st["qT", i] for i in range(4)]
                st["qTdone"] = True
                st["rope_done"] = tk
                sc = [zone(ZLT + 1024 + 512 * i, 512) for i in range(2)] + [zone(ZAT + 512 * i, 512) for i in range(4)]
                o = zone(ZY + 1024, 1024).rearrange("p (t h d) -> p t h d", t=2, h=4)
                es, ptr, lastpv, tkt = {}, {}, {}, {}

                def scores(h):
                    es[h] = []
                    for c in range(2):
                        kT = QT[64 * c:64 * c + 64, 4 + h, :]
                        qT = QT[64 * c:64 * c + 64, h, :]
                        A.wait([ptr.get(h - 2)])
                        es[h].append(softmax_pair(tq, kT, qT, None, 0.125, None, sc[2 * (h % 2) + c], None))

                def combine(h):
                    (e0, r0, te0, _), (e1, r1, te1, _) = es[h]
                    rl = S(2)
                    ts(V, rl, r1, lam[:, 0:1], None, ALU.mult, ALU.bypass)
                    for t in range(2):
                        ts(V, e1[:, t, :], e1[:, t, :], rl[:, t:t + 1], None, ALU.mult, ALU.bypass, te1)
                        ta = stt(e0[:, t, :], e0[:, t, :], r0[:, t:t + 1], e1[:, t, :], ALU.mult, ALU.subtract, te0)
                    tkt[h], ptr[h] = probs_T(e0, ta, sc[4 + h % 2], A, lastpv.get(h - 2))

                def values(h):
                    k, tp = pv(sc[4 + h % 2], tkt[h], lambda kt: vA[:, kt, 128 * h:128 * h + 128], 128, tvA)
                    lastpv[h] = tp
                    st["oa"] = copy(V, o[:, :, h, :], banks[k][:, 0:256].rearrange("p (t d) -> p t d", t=2), tp)
                    put(k, st["oa"])

                for s_ in range(6):
                    if s_ < 4:
                        scores(s_)
                        yield
                    if 1 <= s_ < 5:
                        combine(s_ - 1)
                        yield
                    if s_ >= 2:
                        values(s_ - 2)
                        yield
                st["ya"] = head_norm(o, zone(ZLT + 1024, 1024), st["oa"], pcol(pl["sg"]), 1.0 - li, None, yaT)
                yield

            def head_norm(o, tmp, to, gain, fac, mulT, dst, *after):
                o2 = o.rearrange("p t h d -> p (t h d)")
                tk = act(tmp, o2, ACT.Square, to)
                ss = S(8)
                tk = V(lambda e: e.tensor_reduce(ss, v4(tmp, 8), AX.X, ALU.add), tk)
                tk = rsqrt(ss, ss, 1.0 / 128, tk)
                o8 = v4(o2, 8)
                if fac != 1.0:
                    ts(V, ss, ss, fac, None, ALU.mult, ALU.bypass, tk)
                tk = tt(V, o8, o8, bc(ss.unsqueeze(2), [128, 8, 128]), ALU.mult, tk)
                for hp in range(2):
                    k = get()
                    for j in range(2):
                        for t in range(2):
                            tp = tr(banks[k][:, 256 * j + 128 * t:256 * j + 128 * t + 128], o[:, t, 2 * hp + j, :], tk,
                                    bank_after[k], inc=(j == 1 and t == 1))
                    b = v4(banks[k][:, :], 2)
                    if mulT is None:
                        te = ts(V, dst[:, 2 * hp:2 * hp + 2, :], b, gain, None, ALU.mult, ALU.bypass, tp, *after)
                    else:
                        te = stt(dst[:, 2 * hp:2 * hp + 2, :], b, gain, mulT[:, 2 * hp:2 * hp + 2, :], ALU.mult, ALU.mult, tp, *after)
                    put(k, te)
                return te


            beta, graw, gsm, ge = (gper[:, o_:o_ + n_] for o_, n_ in ((0, 16), (16, 16), (32, 64), (96, 64)))

            def delta():
                while "proj" not in st:
                    yield
                acc = v4(zone(Z1, 3072), 12)
                tmp = v4(zone(Z1 + 3072, 3072), 12)
                TOK = zone(ZTOK, 3072).rearrange("p (g t h d) -> p g t h d", g=3, t=2, h=4)
                b3 = v4(beta, 2)
                g3 = v4(graw, 2)
                tk = act(b3, ba[:, :, 0:8], ACT.Tanh, st["ba"], scale=0.5)
                ts(V, b3, b3, 0.5, 0.5, ALU.mult, ALU.add, tk)
                z, nz, sp, ea = v4(S(16), 2), v4(S(16), 2), v4(S(16), 2), S(8)
                dtb = rows[:, 136:144].unsqueeze(1)
                tt(V, z, ba[:, :, 8:16], bc(dtb, [128, 2, 8]), ALU.add)
                ts(V, nz, z, -1.0, None, ALU.mult, ALU.bypass)
                tk = tt(V, nz, nz, z, ALU.max)
                act(sp, nz, ACT.Exp, tk, scale=-1.0)
                tk = act(sp, sp, ACT.Ln, bias=K("ones")[:, 0:1])
                tk = act(ea, rows[:, 128:136], ACT.Exp, rc["dt"][1])
                stt(z, z, 0.0, sp, ALU.max, ALU.add, tk)
                tg = stt(g3, z, -1.0, bc(ea.unsqueeze(1), [128, 2, 8]), ALU.mult, ALU.mult)
                gb = v4(gsm, 2)
                k = get()
                for t in range(2):
                    o = 32 * t
                    for nm, lo, ro_, n in (("triF", 0, 0, 4), ("triB", 4, 4, 4), ("blk", 8, 0, 8), ("half0", 16, 0, 8), ("half1", 24, 0, 8)):
                        tp = mm(banks[k][:, o + lo:o + lo + n], K(nm), g3[:, t, ro_:ro_ + n], True, True, tg, bank_after[k],
                                inc=(t == 1 and nm == "half1"))
                tk = copy(V, gsm, banks[k][:, 0:64], tp)
                put(k, tk)
                tk = tt(V, gb[:, :, 8:16], gb[:, :, 8:16], gb[:, :, 0:8], ALU.subtract)
                tge = act(ge, gsm, ACT.Exp, tk)
                E = v4(ge, 2)
                yield
                cv = pl["cv"]
                for g in range(3):
                    for f in range(4 * g, 4 * g + 4):
                        tc_ = st["cin", g, 0 if f % 4 < 2 else 2]
                        t0 = act(acc[:, f, :], cin[:, f, 0:256], ACT.Copy, tc_, tpad, scale=pcol(cv + f))
                        for kk in range(1, 5):
                            tk = stt(acc[:, f, :], cin[:, f, kk:kk + 256], pcol(cv + 12 * kk + f), acc[:, f, :],
                                     ALU.mult, ALU.add, t0, tc_)
                        if f % 2:
                            yield
                    ag, tg_ = acc[:, 4 * g:4 * g + 4, :], tmp[:, 4 * g:4 * g + 4, :]
                    te = act(tg_, ag, ACT.Tanh, tk)
                    tk = stt(ag, tg_, 1.0, ag, ALU.add, ALU.mult, te)
                    yield
                    for t in range(2):
                        k = get()
                        for h in range(4):
                            tp = tr(banks[k][:, 128 * h:128 * h + 128], acc[:, 4 * g + h, 128 * t:128 * t + 128], tk,
                                    bank_after[k], inc=(h == 3))
                        st["tok", g, t] = copy(A, TOK[:, g, t], v4(banks[k][:, :], 4), tp)
                        put(k, st["tok", g, t])
                    yield
                ss = S(16)
                sq = zone(Z1 + 3072, 2048)
                tk = act(sq, zone(ZTOK, 2048), ACT.Square)
                tk = V(lambda e: e.tensor_reduce(ss, v4(sq, 16), AX.X, ALU.add), tk)
                tk = rsqrt(ss, ss, 1.0, tk)
                tk = ts(V, ss[:, 0:8], ss[:, 0:8], 128 ** -0.5, None, ALU.mult, ALU.bypass, tk)
                t16 = v4(zone(ZTOK, 2048), 16)
                tk = tt(V, t16, t16, bc(ss.unsqueeze(2), [128, 16, 128]), ALU.mult)
                yield
                while "qTdone" not in st:
                    yield
                kqT = v4(xn[:, :], 4)
                tkq = []
                for h in range(4):
                    k = get()
                    for g in range(2):
                        for t in range(2):
                            tp = tr(banks[k][:, 256 * g + 128 * t:256 * g + 128 * t + 128], TOK[:, 1 - g, t, h, :], tk,
                                    bank_after[k], inc=(g == 1 and t == 1))
                    te = copy(A if h % 2 else V, kqT[:, h, :], banks[k][:, :], tp)
                    put(k, te)
                    tkq.append(te)
                yield
                while "ya" not in st:
                    yield
                dT = zone(ZDT, 2048).rearrange("p (i t h d) -> p i t h d", i=2, t=2, h=4)
                tdd = {}
                for i in range(2):
                    tri = K("triF" if i == 0 else "triB")
                    for t in range(2):
                        k = get()
                        for h in range(4):
                            jj = 4 * i + h
                            tp = mm(banks[k][:, 128 * h:128 * h + 128], bc(g3[:, t, jj:jj + 1], [128, 128]), tri, True, True,
                                    tg, bank_after[k], inc=(h == 3))
                        for h in range(4):
                            jj = 4 * i + h
                            tk = stt(dT[:, i, t, h, :], banks[k][:, 128 * h:128 * h + 128], gb[:, t, jj:jj + 1], tri,
                                     ALU.subtract, ALU.mult, tp, st["ya"])
                        put(k, tk)
                        te = act(dT[:, i, t], dT[:, i, t], ACT.Exp, tk)
                        tdd[i, t] = tt(V, dT[:, i, t], dT[:, i, t], bc(tri.unsqueeze(1), [128, 4, 128]), ALU.mult, te)
                        yield
                LT = zone(ZLT, 2048).rearrange("p (i t h d) -> p i t h d", i=2, t=2, h=4)
                AT = zone(ZAT, 2048).rearrange("p (i t h d) -> p i t h d", i=2, t=2, h=4)
                X = zone(Z1, 2048).rearrange("p (i t h d) -> p i t h d", i=2, t=2, h=4)
                XT = zone(Z1 + 2048, 2048).rearrange("p (i t h d) -> p i t h d", i=2, t=2, h=4)
                B = zone(Z1 + 4096, 2048).rearrange("p (i t h d) -> p i t h d", i=2, t=2, h=4)
                for h in range(4):
                    k = get()
                    for t in range(2):
                        kq = kqT[:, h, :].rearrange("p (g n) -> p g n", g=2)[:, :, 128 * t:128 * t + 128]
                        tp = mm(v4(banks[k][:, 256 * t:256 * t + 256], 2), kqT[:, h, 128 * t:128 * t + 128], kq, True, True,
                                tkq, bank_after[k], inc=(t == 1))
                    for t in range(2):
                        for i in range(2):
                            stt(LT[:, i, t, h, :], banks[k][:, 256 * t:256 * t + 128], b3[:, t, 4 * i + h:4 * i + h + 1],
                                dT[:, i, t, h, :], ALU.mult, ALU.mult, tp)
                            tk = tt(V, dT[:, i, t, h, :], banks[k][:, 256 * t + 128:256 * t + 256], dT[:, i, t, h, :], ALU.mult)
                    put(k, tk)
                    yield
                tLT = tk
                tqkT = tk
                grp = [(i, t) for i in range(2) for t in range(2)]

                def lv(i, s):
                    return bc(K(("lvF" if i == 0 else "lvB") + str(s)).unsqueeze(1), [128, 4, 128])
                tX, tXT, tB = {}, {}, {}
                for i, t in grp:
                    tt(V, XT[:, i, t], LT[:, i, t], lv(i, 0), ALU.mult)
                    tXT[i, t] = tt(V, XT[:, i, t], bc(K("ident").unsqueeze(1), [128, 4, 128]), XT[:, i, t], ALU.subtract)
                    k = get()
                    for h in range(4):
                        tp = tr(banks[k][:, 128 * h:128 * h + 128], XT[:, i, t, h, :], tXT[i, t], bank_after[k], inc=(h == 3))
                    tX[i, t] = copy(A, X[:, i, t], v4(banks[k][:, :], 4), tp)
                    put(k, tX[i, t])
                yield
                pB = {}
                for s in range(1, 6):
                    for i, t in grp:
                        ta = tt(G, AT[:, i, t], LT[:, i, t], lv(i, s), ALU.mult, tLT, pB.get((i, t)))
                        k = get()
                        for h in range(4):
                            tp = mm(banks[k][:, 128 * h:128 * h + 128], AT[:, i, t, h, :], X[:, i, t, h, :], True, True, ta,
                                    tX[i, t], bank_after[k], inc=(h == 3))
                        pB[i, t] = tp
                        tB[i, t] = copy(A, B[:, i, t], v4(banks[k][:, :], 4), tp)
                        put(k, tB[i, t])
                    yield
                    for i, t in grp:
                        if s < 5:
                            k = get()
                            for h in range(4):
                                tp = mm(banks[k][:, 128 * h:128 * h + 128], XT[:, i, t, h, :], B[:, i, t, h, :], True, True,
                                        tB[i, t], tXT[i, t], bank_after[k], inc=(h == 3))
                            tX[i, t] = tt(V, X[:, i, t], X[:, i, t], v4(banks[k][:, :], 4), ALU.subtract, tp)
                            put(k, tX[i, t])
                        k = get()
                        for h in range(4):
                            tp = mm(banks[k][:, 128 * h:128 * h + 128], B[:, i, t, h, :], XT[:, i, t, h, :], True, True,
                                    tB[i, t], tXT[i, t], bank_after[k], inc=(h == 3))
                        tXT[i, t] = tt(V, XT[:, i, t], XT[:, i, t], v4(banks[k][:, :], 4), ALU.subtract, tp)
                        put(k, tXT[i, t])
                    yield
                KG, KD, BU, WT = AT, LT, X, B
                ktok, vtok = TOK[:, 1], TOK[:, 2]
                tbu, twt, tkd = {}, {}, {}
                for i, t in grp:
                    egb = bc(E[:, t, 4 * i:4 * i + 4].unsqueeze(2), [128, 4, 128])
                    kdb = bc(E[:, t, 8 + 4 * i:12 + 4 * i].unsqueeze(2), [128, 4, 128])
                    tkg = tt(V, KG[:, i, t], ktok[:, t], egb, ALU.mult, tge, pB[i, t])
                    tkd[i, t] = tt(V, KD[:, i, t], ktok[:, t], kdb, ALU.mult, G.last)
                    k = get()
                    for h in range(4):
                        tp = mm(banks[k][:, 128 * h:128 * h + 128], XT[:, i, t, h, :], vtok[:, t, h, :], True, True,
                                tXT[i, t], st["tok", 2, 1], bank_after[k], inc=(h == 3))
                    tbu[i, t] = tt(V, BU[:, i, t], v4(banks[k][:, :], 4),
                                   bc(b3[:, t, 4 * i:4 * i + 4].unsqueeze(2), [128, 4, 128]), ALU.mult, tp)
                    put(k, tbu[i, t])
                    k = get()
                    for h in range(4):
                        tp = mm(banks[k][:, 128 * h:128 * h + 128], KG[:, i, t, h, :], XT[:, i, t, h, :], True, True, tkg,
                                bank_after[k], inc=(h == 3))
                    twt[i, t] = copy(A, WT[:, i, t], v4(banks[k][:, :], 4), tp)
                    put(k, twt[i, t])
                    yield
                ST = zone(ZST, 3072).rearrange("p (i s h d) -> p i s h d", i=2, s=3, h=4)
                tS = {}
                tvn = {}
                tmpd = [zone(ZAT, 512), zone(ZAT + 512, 512)]
                twm = [None, None]
                for s in range(4):
                    for i in range(2):
                        n = s if i == 0 else 3 - s
                        t, p0 = n // 2, 64 * (n % 2)
                        pp = slice(p0, p0 + 64)
                        if s:
                            k = get()
                            for h in range(4):
                                tp = mm(banks[k][pp, 128 * h:128 * h + 128], WT[:, i, t, h, pp], ST[:, i, s - 1, h, :], True, True,
                                        tS[i, s], twt[i, t], bank_after[k], inc=(h == 3))
                            tw3 = v4(tmpd[i][pp, :], 4)
                            tk = tt(V, tw3, v4(banks[k][pp, :], 4),
                                    bc(b3[pp, t, 4 * i:4 * i + 4].unsqueeze(2), [64, 4, 128]), ALU.mult, tp, twt[1, 1])
                            put(k, tk)
                            tvn[i, n] = tt(V, BU[pp, i, t], BU[pp, i, t], tw3, ALU.subtract)
                        else:
                            tvn[i, n] = tbu[i, t]
                        if s < 3:
                            k = get()
                            for h in range(4):
                                tp = mm(banks[k][:, 128 * h:128 * h + 128], KD[pp, i, t, h, :], BU[pp, i, t, h, :], True, True,
                                        tvn[i, n], tkd[i, t], bank_after[k], inc=(h == 3))
                            if s:
                                glb = bc(E[:, t, 16 + 8 * (n % 2) + 4 * i:20 + 8 * (n % 2) + 4 * i].unsqueeze(2), [128, 4, 128])
                                tt(V, ST[:, i, s], ST[:, i, s - 1], glb, ALU.mult)
                                tk = tt(V, ST[:, i, s], ST[:, i, s], v4(banks[k][:, :], 4), ALU.add, tp)
                            else:
                                tk = copy(V, ST[:, i, 0], v4(banks[k][:, :], 4), tp)
                            tS[i, s + 1] = tk
                            put(k, tk)
                    yield
                O = zone(ZTOK, 1024).rearrange("p (t h d) -> p t h d", t=2, h=4)
                t5 = zone(ZAT + 1024, 512)
                for t in range(2):
                    k = get()
                    for h in range(4):
                        for i in range(2):
                            tp = mm(banks[k][:, 128 * h:128 * h + 128], dT[:, i, t, h, :], BU[:, i, t, h, :], i == 0, i == 1,
                                    [tvn[i, 2 * t], tvn[i, 2 * t + 1]], tqkT, bank_after[k], inc=(h == 3 and i == 1))
                    to = copy(V, O[:, t], v4(banks[k][:, :], 4), tp)
                    put(k, to)
                    for i in range(2):
                        hs = [h2 for h2 in range(2) if (2 * t + h2 if i == 0 else 3 - 2 * t - h2) > 0]
                        k = get()
                        for h2 in hs:
                            n = 2 * t + h2
                            s = n if i == 0 else 3 - n
                            for h in range(4):
                                pp = slice(64 * h2, 64 * h2 + 64)
                                tp = mm(banks[k][pp, 128 * h:128 * h + 128],
                                        kqT[:, h, 256 + 128 * t + 64 * h2:256 + 128 * t + 64 * h2 + 64],
                                        ST[:, i, s - 1, h, :], True, True, tS[i, s], bank_after[k], inc=(h == 3))
                        pp = slice(64 * hs[0], 64 * hs[-1] + 64)
                        npp = 64 * len(hs)
                        tk = tt(V, v4(t5[pp, :], 4), v4(banks[k][pp, :], 4),
                                bc(E[pp, t, 4 * i:4 * i + 4].unsqueeze(2), [npp, 4, 128]), ALU.mult, tp)
                        put(k, tk)
                        to = tt(V, O[pp, t], O[pp, t], v4(t5[pp, :], 4), ALU.add)
                    yield
                st["o"] = to

            def filler():
                yield from proj_dn()
                yield from gates()
            interleave(attn_a(), delta(), filler())
            O = zone(ZTOK, 1024).rearrange("p (t h d) -> p t h d", t=2, h=4)
            st["yb"] = head_norm(O, zone(ZTOK + 1024, 1024), st["o"], pcol(pl["og"]), 0.5, zT, ybT, st["gates"])

            mT = v4(zone(ZLT, 2048), 8)
            ia, wa, twa = take()
            ib, wb, twb = take()
            tmpz = zone(ZAT, 1024)
            for f in range(0, 8, 2):
                ks = []
                for w, tw, y, ty in ((wa, twa, yaT, st["ya"]), (wb, twb, ybT, st["yb"])):
                    k = get()
                    for j in range(2):
                        for c in range(4):
                            tp = mm(banks[k][:, 256 * j:256 * j + 256], w[:, c, 128 * (f + j):128 * (f + j) + 128], y[:, c, :],
                                    c == 0, c == 3, tw, ty, bank_after[k], inc=(j == 1 and c == 3))
                    ks.append((k, tp))
                t1 = v4(tmpz[:, 0:512], 2)
                tk = stt(t1, gT[:, f:f + 2, :], 1.0, v4(banks[ks[0][0]][:, :], 2), ALU.add, ALU.mult, ks[0][1], st["gates"])
                put(ks[0][0], tk)
                t2 = v4(tmpz[:, 512:1024], 2)
                tk = stt(t2, gT[:, 8 + f:10 + f, :], 1.0, v4(banks[ks[1][0]][:, :], 2), ALU.add, ALU.mult, ks[1][1])
                put(ks[1][0], tk)
                tmg = tt(V, mT[:, f:f + 2, :], t1, t2, ALU.add)
            release(ia, tp)
            release(ib, tp)
            tm = tmod[0]
            gtB = zone(ZDT, 1024)
            gt1 = S(8)
            tm = ts(V, gt1, modT[:, 16:24], 0.5, None, ALU.mult, ALU.bypass, tm)
            tg = spread(gtB, gt1, tm)
            out_proj(mT, tmg, gtB)

            sa2 = sb(f"sb{l}", 8)
            ts(V, sa2[:, :], modT[:, 32:40], 1.0, None, ALU.add, ALU.bypass)
            tsa = tt(V, sa2[:, :], sa2[:, :], pcol(pl["n2"], 8), ALU.mult)
            tg = spread(gtB, modT[:, 40:48], tm)
            tk = normed()
            th = to_hT(xn, lambda c: sa2[:, c:c + 1], lambda c: modT[:, 24 + c:25 + c], tk, None, tsa, tm)
            h1 = v4(zone(0, 8192), 32)
            ads = []
            for j in range(8):
                i, w, tw = take()
                for f in (0, 2):
                    def e(f0, b, tp):
                        rt = v4(zone(8192 + 512 * (f0 // 2), 512), 2)
                        te = act(rt, b, ACT.Relu, tp, th1.get(f0))
                        th1[f0] = tt(V, h1[:, 4 * j + f0:4 * j + f0 + 2, :], rt, rt, ALU.mult, te)
                        return te
                    if j == 0 and f == 0:
                        th1 = {}
                    tp = lin_feat(w, tw, hT3, th, 8, f, e)
                release(i, tp)
                for q in ads:
                    ada_pe(q)
                ads = [ada_v(1, j, 14384)] if l == 0 else []

            def more(b):
                nonlocal ads
                for q in ads:
                    tmod[0] = ada_pe(q)
                ads = [ada_v(1, 8 + b, 14384)] if l == 0 and b < 4 else []
            acc_out(h1, list(th1.values()), 8, gtB, more)

        def acc_out(lhs, tl, nb, gB, hook=None):
            ks = [get() for _ in range(4)]
            for b in range(nb):
                i, w, tw = take()
                for c in range(4):
                    for t in range(2):
                        for h in range(2):
                            k = ks[2 * t + h]
                            tp = mm(banks[k][:, :], lhs[:, 4 * b + c, 128 * t:128 * t + 128], w[:, c, 512 * h:512 * h + 512],
                                    b == 0 and c == 0, b == nb - 1 and c == 3, tl, tw, bank_after[k],
                                    inc=(c == 3 and t == 1 and h == 1))
                release(i, tp)
                if hook is not None:
                    hook(b)
            for t in range(2):
                for h in range(2):
                    k = ks[2 * t + h]
                    xs = x3[:, t, 512 * h:512 * h + 512]
                    if gB is not None:
                        tmp = xn[:, 0:512]
                        tk = tt(V, tmp, banks[k][:, :], gB[:, 512 * h:512 * h + 512], ALU.mult, tp)
                        xr[0] = tt(V, xs, xs, tmp, ALU.add)
                    else:
                        tk = xr[0] = tt(V, xs, xs, banks[k][:, :], ALU.add, tp)
                    put(k, tk)

        def out_proj(mT, tmg, gB):
            acc_out(mT, tmg, 2, gB)

        def block2(l):
            pl = pc[l]
            tk = normed()
            th = to_hT(xn, lambda c: pcol(pl["an"] + c), None, tk)
            nab = zone(11840, 2048).rearrange("p (t h r c) -> p t h r c", t=2, h=4, r=4)
            tp_ = None
            A.wait([V.last, (P.sem, P.n)])
            raw = xn[:, :].rearrange("p (t h r c) -> p t h r c", t=2, h=4, r=4)
            for h in range(4):
                for r in range(4):
                    src = bass.AP(tensor=a["na_rpb_2"].tensor, offset=((l * 4 + h) * 15 + 7 - r) * 31 + 15 - 63,
                                  ap=[[1, 64], [31, 4], [1, 64]])
                    tb = l_b.load(A, raw[64 * (r % 2):64 * (r % 2) + 64, r // 2, h], src)
            ro[0] = 0
            prw("sink", a["swa_sink_2"][l], 6)
            P2 = zone(0, 3648).rearrange("p (t n) -> p t n", t=2)
            cc = [0]
            tpj = []
            for j in range(4):
                i, w, tw = take()
                n = 512 if j < 3 else 288

                def e(t, b, tp, j=j, n=n):
                    tpj.append(copy(A if t else V, P2[:, t, 512 * j:512 * j + n], b, tp))
                    return tpj[-1]
                tp = lin_tok(hT3, th, w, tw, n, 8, e)
                release(i, tp)
            n3 = zone(11840, 2048).rearrange("p (a c) -> p a c", a=32)
            for q in range(4):
                k = get()
                tp = mm(banks[k][:, :], K2("flip"), xn[:, 512 * q:512 * q + 512], True, True, tb, t_c2, bank_after[k], inc=True)
                tk = tt(V, n3[:, 8 * q:8 * q + 8, :], v4(banks[k][:, :], 8), bc(K2("na01").unsqueeze(1), [128, 8, 64]), ALU.mult, tp)
                put(k, tk)
            tnab = tt(V, n3, n3, bc(K2("naneg").unsqueeze(1), [128, 32, 64]), ALU.add)
            tmp = zone(16960, 1024)
            ss = S(4)
            for t in range(2):
                tk = act(tmp[:, 0:256], P2[:, t, 768:1024], ACT.Square, tpj, V.last, accum=ss[:, t:t + 1])
                tk = act(tmp[:, 0:128], P2[:, t, 1024:1152], ACT.Square, accum=ss[:, 2 + t:3 + t])
            rsqrt(ss[:, 0:2], ss[:, 0:2], 1.0 / 256, tk)
            tk = rsqrt(ss[:, 2:4], ss[:, 2:4], 1.0 / 128)
            for t in range(2):
                ts(V, P2[:, t, 768:1024], P2[:, t, 768:1024], ss[:, t:t + 1], None, ALU.mult, ALU.bypass, tk)
                tn = ts(V, P2[:, t, 1024:1152], P2[:, t, 1024:1152], ss[:, 2 + t:3 + t], None, ALU.mult, ALU.bypass)
            cqT = v4(zone(22072, 768), 3)
            tcq = []
            for cp in range(2):
                k = get()
                for j in range(2 if cp == 0 else 1):
                    for t in range(2):
                        c0 = 768 + 128 * (2 * cp + j)
                        tp = tr(banks[k][:, 256 * j + 128 * t:256 * j + 128 * t + 128], P2[:, t, c0:c0 + 128], tn, bank_after[k],
                                inc=True)
                for j in range(2 if cp == 0 else 1):
                    g = pcol(pl["qn"] + j) if cp == 0 else pcol(pl["kn"])
                    te = ts(V, cqT[:, 2 * cp + j, :], banks[k][:, 256 * j:256 * j + 256], g, None, ALU.mult, ALU.bypass, tp)
                put(k, te)
            tcq = te
            mq = zone(3648, 1152).rearrange("p (t h d) -> p t h d", t=2, h=6)
            mk = zone(4800, 1152).rearrange("p (t h d) -> p t h d", t=2, h=6)
            mv = zone(5952, 768).rearrange("p (t h d) -> p t h d", t=2, h=6)
            i, w, tw = take()
            for t in range(2):
                for s in range(2):
                    k = get()
                    for c in range(2):
                        tp = mm(banks[k][:, 0:288], cqT[:, c, 128 * t:128 * t + 128], w[:, c, 288 * s:288 * s + 288], c == 0, c == 1,
                                tcq, tw, bank_after[k], inc=(c == 1))
                    te = copy(A, mq[:, t, 3 * s:3 * s + 3, :], v4(banks[k][:, 0:288], 3), tp)
                    put(k, te)
            release(i, tp)
            tmq = te
            i, w, tw = take()
            for t in range(2):
                for s in range(2):
                    k = get()
                    tp = mm(banks[k][:, 0:384], cqT[:, 2, 128 * t:128 * t + 128], w[:, 0, 384 * s:384 * s + 384], True, True,
                            tcq, tw, bank_after[k], inc=True)
                    b = v4(banks[k][:, 0:384], 3)
                    copy(V, mk[:, t, 3 * s:3 * s + 3, 0:64], b[:, :, 0:64], tp)
                    te = copy(V, mv[:, t, 3 * s:3 * s + 3, :], b[:, :, 64:128], tp)
                    put(k, te)
            release(i, tp)
            ta, tb_ = zone(16960, 512), zone(17472, 512)

            def rot(dst, src, n, d, cs, sn, *after):
                a_, b_ = v4(ta[:, 0:n * d], n), v4(tb_[:, 0:n * d], n)
                hd = d // 2
                tt(V, a_, src, bc(cs, [128, n, d]), ALU.mult, *after)
                for h in range(2):
                    tt(V, b_[:, :, hd * h:hd * h + hd], src[:, :, hd - hd * h:2 * hd - hd * h],
                       bc(sn[:, :, hd * h:hd * h + hd], [128, n, hd]), ALU.mult)
                return dst(a_, b_)
            c32, s32 = v4(K2("cos32"), 2), v4(K2("sin32"), 2)
            c64, s64 = v4(K("cos64"), 2), v4(K("sin64"), 2)
            cro = zone(15936, 1024).rearrange("p (t n) -> p t n", t=2)
            for t in range(2):
                rot(lambda x_, y_: tt(V, mq[:, t, :, 64:96], x_, y_, ALU.add), mq[:, t, :, 64:96], 6, 32,
                    c32[:, t:t + 1, :], s32[:, t:t + 1, :], tmq, t_c2)
                kr = P2[:, t, 1152:1184].unsqueeze(1)
                rot(lambda x_, y_: tt(V, mk[:, t, :, 64:96], bc(x_, [128, 6, 32]), bc(y_, [128, 6, 32]), ALU.add), kr, 1, 32,
                    c32[:, t:t + 1, :], s32[:, t:t + 1, :])

                def put_c(x_, y_, t=t):
                    o = cro[:, t, 0:384].rearrange("p (g v d) -> p v g d", g=3, v=2)
                    xq = x_[:, 0:6, :].rearrange("p (v g) d -> p v g d", v=2)
                    yq = y_[:, 0:6, :].rearrange("p (v g) d -> p v g d", v=2)
                    tt(V, o, xq, yq, ALU.add)
                    return tt(V, v4(cro[:, t, 384:512], 2), x_[:, 6:8, :], y_[:, 6:8, :], ALU.add)
                tk = rot(put_c, v4(P2[:, t, 1184:1696], 8), 8, 64, c64[:, t:t + 1, :], s64[:, t:t + 1, :])
            mT = zone(6720, 3072).rearrange("p (h n) -> p h n", h=6)
            cT = v4(zone(9792, 1024), 4)
            aT = v4(zone(10816, 1024), 4)
            tT = []
            n_ = [0]
            for h in range(6):
                k = get()
                for g, src in ((0, mq), (1, mk)):
                    for t in range(2):
                        tp = tr(banks[k][0:96, 256 * g + 128 * t:256 * g + 128 * t + 128], src[:, t, h, :], tk, tmq, bank_after[k],
                                inc=(g == 1 and t == 1))
                te = copy(A if h % 2 else V, mT[0:96, h, :], banks[k][0:96, :], tp)
                put(k, te)
                tT.append(te)
            for dst, src in ((aT, P2[:, :, 0:512]), (cT, cro)):
                for cp in range(2):
                    k = get()
                    for j in range(2):
                        for t in range(2):
                            c0 = 128 * (2 * cp + j)
                            tp = tr(banks[k][:, 256 * j + 128 * t:256 * j + 128 * t + 128], src[:, t, c0:c0 + 128], tk, tpj,
                                    bank_after[k], inc=(j == 1 and t == 1))
                    te = copy(A if cp % 2 else V, dst[:, 2 * cp:2 * cp + 2, :], v4(banks[k][:, :], 2), tp)
                    put(k, te)
                    tT.append(te)
            oc = zone(13888, 2048).rearrange("p (t n) -> p t n", t=2)
            swa = v4(K2("swa"), 2)
            units = []
            for h in range(4):
                pp = slice(64 * (h % 2), 64 * (h % 2) + 64)
                units.append(dict(q=aT[pp, h // 2, :], k=aT[pp, 2 + h // 2, :], bias=nab[:, :, h].rearrange("p t r c -> p t (r c)"),
                                  scale=0.125, sink=None, v=lambda kt, h=h: P2[:, kt, 512 + 64 * h:576 + 64 * h], o=64 * h))
            for h in range(6):
                units.append(dict(q=mT[0:96, h, 0:256], k=mT[0:96, h, 256:512], bias=None, scale=96 ** -0.5, sink=None,
                                  v=lambda kt, h=h: mv[:, kt, h, :], o=256 + 64 * h))
            for h in range(6):
                kv, g = h // 3, h % 3
                pp = slice(64 * kv, 64 * kv + 64)
                units.append(dict(q=cT[pp, g, :], k=cT[pp, 3, :], bias=swa, scale=0.125, sink=rows[:, h:h + 1],
                                  v=lambda kt, kv=kv: P2[:, kt, 1696 + 64 * kv:1760 + 64 * kv], o=640 + 64 * h))
            sc = [zone(19000 + 512 * i, 512) for i in range(6)]
            res = {}
            V.wait([rc["sink"][1]])
            A.wait([rc["sink"][1]])
            for s in range(len(units) + 2):
                if s < len(units):
                    u = units[s]
                    b = s % 2
                    e3, r, te, tr2 = softmax_pair([tT, res.get(("T", s - 2))], u["k"], u["q"], u["bias"], u["scale"], sc[b], sc[2 + b], u["sink"])
                    if s >= 2:
                        pass
                    res[s] = (e3, r, te, tr2)
                if 1 <= s <= len(units):
                    q = s - 1
                    e3, r, te, tr2 = res[q]
                    tk, ptr = probs_T(e3, te, sc[4 + q % 2], A, res.get(("P", q - 2)))
                    A.wait([ptr])
                    res["T", q] = ptr
                    res["tk", q] = tk
                if s >= 2:
                    q = s - 2
                    u = units[q]
                    e3, r, te, tr2 = res[q]
                    k, tp = pv(sc[4 + q % 2], res["tk", q], u["v"], 64, [te, tpj])
                    res["P", q] = tp
                    to = tt(V, oc[:, :, u["o"]:u["o"] + 64], v4(banks[k][:, 0:128], 2), bc(r.unsqueeze(2), [128, 2, 64]), ALU.mult, tp, tr2)
                    put(k, to)
            ss = S(8)
            ss3 = v4(ss[:, 0:6], 2)
            for t in range(2):
                for g, (o0, n) in enumerate(((0, 256), (256, 384), (640, 384))):
                    tk = act(tmp[:, 0:n], oc[:, t, o0:o0 + n], ACT.Square, to, accum=ss3[:, t, g:g + 1])
            rsqrt(ss3[:, :, 0:1], ss3[:, :, 0:1], 1.0 / 256, tk)
            tk = rsqrt(ss3[:, :, 1:3], ss3[:, :, 1:3], 1.0 / 384)
            for t in range(2):
                for g, (o0, n) in enumerate(((0, 256), (256, 384), (640, 384))):
                    tk = ts(V, oc[:, t, o0:o0 + n], oc[:, t, o0:o0 + n], ss3[:, t, g:g + 1], None, ALU.mult, ALU.bypass, tk)
            th = to_hT(zone(13888, 2048), lambda c: pcol(pl["gn"] + c), None, tk)
            out_proj(hT3, th, None)

            tk = normed()
            th = to_hT(xn, lambda c: pcol(pl["fn"] + c), None, tk)
            txn = tk
            i, w, tw = take()
            k = get()
            for t in range(2):
                for c in range(8):
                    tp = mm(banks[k][:, 16 * t:16 * t + 16], hT3[:, c, 128 * t:128 * t + 128], w[:, c, :], c == 0, c == 7,
                            th, tw, bank_after[k], inc=(c == 7))
            release(i, tp)
            aff = zone(17408, 32).rearrange("p (t n) -> p t n", t=2)
            sel = zone(17440, 32).rearrange("p (t n) -> p t n", t=2)
            lg = v4(banks[k][:, 0:32], 2)
            mx, smv = S(2), S(2)
            V(lambda e: e.tensor_reduce(mx, lg, AX.X, ALU.max), tp)
            tk = tt(V, aff, lg, bc(mx.unsqueeze(2), [128, 2, 16]), ALU.subtract)
            put(k, tk)
            tk = act(aff, aff, ACT.Exp, tk)
            V(lambda e: e.tensor_reduce(smv, aff, AX.X, ALU.add), tk)
            V(lambda e: e.reciprocal(smv, smv))
            taff = tt(V, aff, aff, bc(smv.unsqueeze(2), [128, 2, 16]), ALU.mult)
            k = get()
            for t in range(2):
                tp = tr(banks[k][0:16, 128 * t:128 * t + 128], aff[:, t, :], taff, bank_after[k], inc=True)
            w0 = zone(17472, 256)[0:16, :]
            w1 = zone(17728, 256)[0:16, :]
            m8 = zone(17984, 8)[0:16, :]
            tk = copy(V, w0, banks[k][0:16, 0:256], tp)
            put(k, tk)
            ws = [w0, w1]
            for r in range(4):
                s_, d_ = ws[r % 2], ws[1 - r % 2]
                V(lambda e: e.max(m8, s_))
                V(lambda e: e.match_replace(d_, m8, s_, -1.0))
            tk = ts(V, w1, w0, 0.0, None, ALU.is_lt, ALU.bypass)
            k = get()
            for t in range(2):
                tp = tr(banks[k][:, 16 * t:16 * t + 16], w1[:, 128 * t:128 * t + 128], tk, bank_after[k], inc=True)
            tsel = copy(V, sel, v4(banks[k][:, 0:32], 2), tp)
            put(k, tsel)
            k = get()
            mm(banks[k][:, 0:16], K2("triA"), sel[:, 0, :], True, True, tsel, bank_after[k])
            mm(banks[k][:, 16:32], K("ones"), sel[:, 0, :], True, False)
            tp = mm(banks[k][:, 16:32], K2("triA"), sel[:, 1, :], False, True, inc=True)
            pm = S(32)
            pm3 = v4(pm, 2)
            tk = tt(V, pm3, v4(banks[k][:, 0:32], 2), sel, ALU.mult, tp)
            put(k, tk)
            ts(V, pm, pm, -1.0, None, ALU.add, ALU.bypass)
            Pm = zone(0, 1024).rearrange("p (t e s) -> p t e s", t=2, e=16)
            PA = zone(1024, 4096).rearrange("p (t e r s) -> p t e r s", t=2, e=16, r=4)
            for t in range(2):
                tt(V, Pm[:, t], bc(K2("iota").unsqueeze(1), [128, 16, 32]), bc(pm3[:, t, :].unsqueeze(2), [128, 16, 32]), ALU.is_equal)
                for r in range(4):
                    tPA = tt(V, PA[:, t, :, r, :], Pm[:, t], bc(aff[:, t, :].unsqueeze(2), [128, 16, 32]), ALU.mult)
            xs = v4(zone(9216, 4096), 8)
            txs = []
            for c in range(8):
                k = get()
                for t in range(2):
                    tp = mm(banks[k][:, :], xn[:, 1024 * t + 128 * c:1024 * t + 128 * c + 128], Pm[:, t].rearrange("p e s -> p (e s)"),
                            t == 0, t == 1, tPA, txn, bank_after[k], inc=(t == 1))
                g = pcol(pl["fn"] + c)
                if c % 2:
                    te = act(xs[:, c, :], banks[k][:, :], ACT.Copy, tp, scale=g)
                else:
                    te = ts(V, xs[:, c, :], banks[k][:, :], g, None, ALU.mult, ALU.bypass, tp)
                put(k, te)
                txs.append(te)
            PW = zone(5120, 4096).rearrange("p (g n) -> p g n", g=16)
            tpw = []
            for gp in range(8):
                k = get()
                for j in range(2):
                    for t in range(2):
                        src = PA[:, t, 2 * gp + j].rearrange("p r s -> p (r s)")
                        tp = tr(banks[k][:, 256 * j + 128 * t:256 * j + 128 * t + 128], src, tPA, bank_after[k], inc=(j == 1 and t == 1))
                te = copy(A if gp % 2 else V, PW[:, 2 * gp:2 * gp + 2, :], v4(banks[k][:, :], 2), tp)
                put(k, te)
                tpw.append(te)
            hid = [zone(13312 + 256 * b, 256).rearrange("p (c b s) -> p c b s", c=4, b=2) for b in range(2)]
            sg = [zone(13824 + 256 * b, 256).rearrange("p (c s) -> p c s", c=4) for b in range(2)]
            gs = [zone(14336 + 512 * b, 512) for b in range(2)]
            Ys = [v4(zone(15360 + 1024 * b, 1024), 2) for b in range(2)]
            thid, tdn, ttr, tY, tsc = {}, {}, {}, {}, {}
            acc4 = [[get(), get()], [get(), get()]]

            def gate_up(e_):
                k = get()
                for s_ in range(4):
                    i, w, tw = take()
                    for c2 in range(2):
                        for q in range(4):
                            tp = mm(banks[k][32 * q:32 * q + 32, :], xs[:, 2 * s_ + c2, 32 * e_:32 * e_ + 32],
                                    w[:, 2 * (q // 2) + c2, 512 * (q % 2):512 * (q % 2) + 512], s_ == 0 and c2 == 0,
                                    s_ == 3 and c2 == 1, tw, txs, bank_after[k], inc=(c2 == 1 and q == 3))
                    release(i, tp)
                tk = copy(A, gs[e_ % 2], banks[k][:, :], tp, ttr.get(e_ - 2))
                put(k, tk)
                return tk

            def hidden(e_, tk):
                k = get()
                for c in range(4):
                    tp = tr(banks[k][:, 128 * c:128 * c + 128], gs[e_ % 2][:, 128 * c:128 * c + 128], tk, bank_after[k], inc=(c == 3))
                ttr[e_] = tp
                b4 = v4(banks[k][:, :], 4)
                g_, u_, s_ = b4[:, :, 0:64], b4[:, :, 64:128], sg[e_ % 2]
                te = act(s_, g_, ACT.Tanh, tp, scale=0.5)
                stt(s_, s_, 1.0, g_, ALU.add, ALU.mult, te)
                thid[e_] = stt(hid[e_ % 2].rearrange("p c b s -> p c (b s)"), s_, 0.5, u_, ALU.mult, ALU.mult, tdn.get(e_ - 2))
                put(k, thid[e_])

            def down(q):
                yk = [get(), get()]
                for b in range(2):
                    i, w, tw = take()
                    for hf in range(2):
                        for j in range(4):
                            tp = mm(banks[yk[hf]][32 * j:32 * j + 32, :], hid[q % 2][:, j, b, :], w[:, j, 512 * hf:512 * hf + 512],
                                    b == 0, b == 1, tw, thid[q], bank_after[yk[hf]], inc=(hf == 1 and j == 3))
                    release(i, tp)
                tdn[q] = tp
                tY[q] = []
                for hf in range(2):
                    te = copy(A if hf else V, Ys[q % 2][:, hf, :], banks[yk[hf]][:, :], tp, tsc.get(q - 2))
                    put(yk[hf], te)
                    tY[q].append(te)

            def scatter(q):
                for t in range(2):
                    for hf in range(2):
                        k = acc4[t][hf]
                        tp = mm(banks[k][:, :], PW[:, q, 128 * t:128 * t + 128], Ys[q % 2][:, hf, :], q == 0, q == 15,
                                tpw, tY[q], bank_after[k], inc=(t == 1 and hf == 1))
                tsc[q] = tp

            for s_ in range(18):
                if s_ < 16:
                    tk = gate_up(s_)
                if 2 <= s_:
                    scatter(s_ - 2)
                if 1 <= s_ <= 16:
                    down(s_ - 1)
                if s_ < 16:
                    hidden(s_, tk)
            for t in range(2):
                for hf in range(2):
                    k = acc4[t][hf]
                    xs_ = x3[:, t, 512 * hf:512 * hf + 512]
                    xr[0] = tt(V, xs_, xs_, banks[k][:, :], ALU.add, tsc[15])
                    put(k, xr[0])

        l_b = Landing()
        for l in range(2):
            block1(l)
        A.wait([V.last, (P.sem, P.n)])
        l_c2 = Landing()
        t_c2 = l_c2.load(A, ar[:, C2B:AR], a["c2"])
        for l in range(2):
            block2(l)
        fg = zone(0, 1024)
        A.wait([V.last, (P.sem, P.n)])
        tf = l_r.load(A, fg, a["final_norm_2"].partition_broadcast(128))
        tk = normed()
        l_o = Landing()
        for t in range(2):
            tk = tt(V, xn[:, 1024 * t:1024 * t + 1024], xn[:, 1024 * t:1024 * t + 1024], fg, ALU.mult, tf)
        to = l_o.load(SP, out[0].rearrange("(t p) d -> p t d", p=128), xn[:, :].rearrange("p (t d) -> p t d", t=2), tk)
        SP.wait([to])
        assert nxt[0] == len(blocks)


_INS = ['x', 'c', 'ada_w', 'ada_b', 'norm1_g', 'norm2_g', 'w_in', 'dn_conv', 'dn_A_log', 'dn_dt_bias', 'dn_out_gain',
        'qk_norm_gain', 'diff_lambda', 'diff_subln_gain', 'w_branch_a', 'w_branch_b', 'w_out', 'w_mlp1', 'w_mlp2',
        'attn_norm_2', 'w_in_2', 'na_rpb_2', 'mla_q_norm_2', 'mla_w_uq_2', 'mla_kv_norm_2', 'mla_w_ukv_2', 'swa_sink_2',
        'group_norm_2', 'w_out_2', 'ffn_norm_2', 'w_router_2', 'w_gate_2', 'w_up_2', 'w_down_2', 'final_norm_2']


def kernel(**inputs):
    import numpy as _np
    import concourse.bacc as _bacc
    from concourse import mybir as _mybir
    from concourse.bass_utils import run_bass_kernel_spmd as _run

    nc = _bacc.Bacc("TRN2", target_bir_lowering=False, num_devices=1)
    (o1, c1), (o2, c2) = const_arrays()
    arrays, aps = {}, {}
    for name in _INS:
        v = _np.ascontiguousarray(inputs[name])
        arrays[f"in_{name}_dram"] = v
        aps[name] = nc.dram_tensor(f"in_{name}_dram", v.shape, _mybir.dt.from_np(v.dtype), kind="ExternalInput").ap()
    for name, v in (("c1", c1), ("c2", c2)):
        arrays[f"in_{name}_dram"] = v
        aps[name] = nc.dram_tensor(f"in_{name}_dram", v.shape, _mybir.dt.from_np(v.dtype), kind="ExternalInput").ap()
    out = nc.dram_tensor("out_0_dram", (1, 256, 1024), F32, kind="ExternalOutput").ap()
    program(nc, aps, o1, o2, out)
    r = _run(nc, [arrays], core_ids=[0])
    return r.results[0]["out_0_dram"]
```

```python
import math
from contextlib import ExitStack

import numpy as np
import concourse.bass as bass
from concourse import mybir

F32 = mybir.dt.float32
F32R = mybir.dt.float32r
I32 = mybir.dt.int32
ALU = mybir.AluOpType
ACT = mybir.ActivationFunctionType
AX = mybir.AxisListType
EPS = 1e-6
NR = 4


def const_arrays():
    i = np.arange(128)
    m, c = i[:, None], i[None, :]
    same = (m // 64) == (c // 64)
    cols = {}
    cols["ident"] = (m == c)
    cols["ones"] = np.ones((128, 128))
    cols["triF"] = same & (m <= c)
    cols["triB"] = same & (m >= c)
    cols["blk"] = same
    cols["half0"] = (m < 64) & (c >= 0)
    cols["half1"] = (m >= 64) & (c >= 0)
    for s in range(6):
        b = 1 << s
        up = ((m // (2 * b)) == (c // (2 * b))) & ((m // b) % 2 == 0) & ((c // b) % 2 == 1)
        cols[f"lvF{s}"] = up
        cols[f"lvB{s}"] = up.T
    pos = np.arange(256, dtype=np.float32)

    def rope(dim):
        inv = (1.0 / (np.float32(10000.0) ** (np.arange(0, dim, 2, dtype=np.float32) / np.float32(dim)))).astype(np.float32)
        ang = pos[:, None] * inv[None, :]
        cs, sn = np.cos(ang), np.sin(ang)
        cs = np.concatenate([cs, cs], -1).reshape(2, 128, dim).transpose(1, 0, 2).reshape(128, 2 * dim)
        sn = np.concatenate([-sn, sn], -1).reshape(2, 128, dim).transpose(1, 0, 2).reshape(128, 2 * dim)
        return cs, sn
    cols["cos64"], cols["sin64"] = rope(64)
    cols["eps"] = np.full((128, 1), EPS)
    a = {k: np.asarray(v, np.float32) for k, v in cols.items()}
    two = {}
    two["triA"] = (m <= c)
    two["cos32"], two["sin32"] = rope(32)
    q, k = (i % 64)[:, None], np.arange(64)[None, :]
    st = np.clip(q - 8, 0, 48)
    win = (k >= st) & (k < st + 16)
    two["na01"] = win
    two["naneg"] = np.where(win, 0.0, -1e30)
    kk = np.arange(256)[None, :]
    two["swa"] = np.concatenate([np.where(np.abs((i + 128 * t)[:, None] - kk) <= 128, 0.0, -1e30) for t in range(2)], 1)
    two["flip"] = ((m // 64) == (c // 64)) & (m % 64 == 63 - c % 64)
    two["iota"] = np.broadcast_to(np.arange(32), (128, 32))
    b = {k: np.asarray(v, np.float32) for k, v in two.items()}

    def pack(d):
        off, o = {}, 0
        for n, v in d.items():
            off[n] = (o, v.shape[1])
            o += v.shape[1]
        return off, np.ascontiguousarray(np.concatenate(list(d.values()), 1), dtype=np.float32)
    return pack(a), pack(b)


class Queue:

    def __init__(self, nc, eng, new_sem, chained):
        self.nc, self.eng, self.new_sem, self.chained = nc, eng, new_sem, chained
        self.sem, self.n, self.seen, self.last = new_sem(), 0, {}, None

    def wait(self, toks):
        for t in toks:
            if t is None:
                continue
            if isinstance(t, list):
                self.wait(t)
                continue
            s, v = t
            if self.seen.get(id(s), 0) < v:
                self.eng.wait_ge(s, v)
                self.seen[id(s)] = v

    def __call__(self, fn, *after, inc=True):
        self.wait(after)
        if self.chained and self.last is not None:
            self.wait([self.last])
        ins = fn(self.eng)
        if not inc:
            return None
        if self.n >= 30000:
            self.sem, self.n = self.new_sem(), 0
        self.n += 1
        ins.then_inc(self.sem, 1)
        self.last = (self.sem, self.n)
        return self.last


def program(nc, a, c1off, c2off, out):
    ctx = ExitStack()
    with ctx:
        names = [0]

        def new_sem():
            names[0] += 1
            return ctx.enter_context(nc.semaphore(f"s{names[0]}"))

        def v4(ap, *d):
            s = " ".join("abcdef"[:len(d) + 1])
            kw = {"abcdef"[i]: d[i] for i in range(len(d))}
            return ap.rearrange("p (" + s + ") -> p " + s, **kw)

        def sb(name, n):
            return ctx.enter_context(nc.sbuf_tensor(name, [128, n], F32))

        P = Queue(nc, nc.tensor, new_sem, False)
        V = Queue(nc, nc.vector, new_sem, True)
        A = Queue(nc, nc.scalar, new_sem, True)
        G = Queue(nc, nc.gpsimd, new_sem, True)
        SP = Queue(nc, nc.sync, new_sem, False)

        class Landing:

            def __init__(self):
                self.sem, self.n = new_sem(), 0

            def load(self, q, dst, src, *after, slow=False):
                q.wait(after)
                self.n += 16
                q.eng.dma_start(dst, src, allow_slow_non_contiguous=slow).then_inc(self.sem, 16)
                return (self.sem, self.n)

        C1N = sum(n for _, n in c1off.values())
        C2N = sum(n for _, n in c2off.values())
        c1 = sb("c1", C1N)
        ring = sb("ring", NR * 4096)
        x = sb("x", 2048)
        xn = sb("xn", 2048)
        par = sb("par", 3 * 128)
        gper = sb("gper", 160)
        rows = sb("rows", 300)
        small = sb("small", 1024)
        modT2 = [sb(f"modT{l}", 48) for l in range(2)]
        sas = [sb(f"sa{l}", 8) for l in range(2)]
        sbs = [sb(f"sb{l}", 8) for l in range(2)]
        lams = [sb(f"lam{l}", 1) for l in range(2)]
        bas = [sb(f"ba{l}", 32) for l in range(2)]
        cact = sb("cact", 8)
        sq4 = sb("sq4", 4)
        rstd = sb("rstd", 2)
        AR = 25704
        toph = ctx.enter_context(ExitStack())
        top = ctx.enter_context(ExitStack())
        hT = ar = hT3 = c2t = None
        made = [0]

        def arena():
            nonlocal hT, ar, hT3
            top.close()
            made[0] += 1
            if hT is None:
                hT = toph.enter_context(nc.sbuf_tensor(f"hT{made[0]}", [128, 2048], F32))
                hT3 = hT[:, :].rearrange("p (c n) -> p c n", c=8)
            ar = top.enter_context(nc.sbuf_tensor(f"ar{made[0]}", [128, AR], F32))

        def split_mem(l):
            nonlocal hT
            top.close()
            toph.close()
            hT = None

            def r(name, n):
                return top.enter_context(nc.sbuf_tensor(f"{name}{l}", [128, n], F32R))
            h = [v4(r(f"hs{i}", 2048)[:, :], 8) for i in range(2)]
            h1 = [v4(r(f"h1s{i}", 8192)[:, :], 32) for i in range(2)]
            ws = [[r(f"ws{b}_{i}", 1024)[:, :] for i in range(2)] for b in range(3)]
            aux = top.enter_context(nc.sbuf_tensor(f"aux{l}", [128, 1024], F32))[:, :]
            return h, h1, ws, aux
        def split_proj(m):
            top.close()
            top.enter_context(nc.sbuf_tensor(f"below{m}", [128, 3648], F32))

            def r(name, n):
                return top.enter_context(nc.sbuf_tensor(f"{name}{m}", [128, n], F32R))
            h = [v4(r(f"hp{i}", 2048)[:, :], 8) for i in range(2)]
            ws = [[r(f"wp{b}_{i}", 1024)[:, :] for i in range(2)] for b in range(2)]
            top.close()
            return h, ws
        arena()
        banks = [ctx.enter_context(nc.psum_tensor(f"pb{i}", [128, 512], F32)) for i in range(8)]

        def K(n):
            o, w = c1off[n]
            return c1[:, o:o + w]

        C2B = AR - C2N

        def K2(n):
            o, w = c2off[n]
            return c2t[:, C2B + o:C2B + o + w]

        def zone(o, n):
            return ar[:, o:o + n]

        sm_at = [0]

        def S(n):
            if sm_at[0] + n > 1024:
                sm_at[0] = 0
            o = sm_at[0]
            sm_at[0] += n
            return small[:, o:o + n]

        bank_after = [None] * 8
        busy = [False] * 8
        bank_i = [0]

        def get():
            for _ in range(8):
                k = bank_i[0] % 8
                bank_i[0] += 1
                if not busy[k]:
                    busy[k] = True
                    return k
            raise RuntimeError("no bank")

        def put(k, tok):
            busy[k] = False
            bank_after[k] = tok

        def mm(o, l, r, start, stop, *after, inc=False):
            return P(lambda e: e.matmul(o, l, r, start=start, stop=stop), *after, inc=inc)

        def tr(o, i, *after, inc=False):
            n = i.shape[0]
            p0 = 0
            return P(lambda e: e.transpose(o, i, K("ident")[p0:p0 + n, 0:n]), *after, inc=inc)

        def tt(q, o, i0, i1, op, *after):
            return q(lambda e: e.tensor_tensor(o, i0, i1, op), *after)

        def ts(q, o, i, s1, s2, op0, op1, *after):
            return q(lambda e: e.tensor_scalar(o, i, s1, s2, op0, op1), *after)

        def stt(o, i0, s, i1, op0, op1, *after):
            return V(lambda e: e.scalar_tensor_tensor(out=o, in0=i0, scalar=s, in1=i1, op0=op0, op1=op1), *after)

        def act(o, i, f, *after, bias=None, scale=1.0, accum=None):
            kw = {}
            if bias is not None:
                kw["bias"] = bias
            if accum is not None:
                kw["accum_out"] = accum
            return A(lambda e: e.activation(o, i, f, scale=scale, **kw), *after)

        def copy(q, o, i, *after):
            if q is A:
                return A(lambda e: e.copy(o, i), *after)
            return q(lambda e: e.tensor_copy(o, i), *after)

        def bc(ap, shape):
            return ap.broadcast_to(shape)

        blocks = []
        first_expert, last_expert = [], []

        def cols(w, c0, n):
            blocks.append(([w.rearrange("(c p) n -> p c n", p=128)[:, :, c0:c0 + n]], w.shape[0] // 128, n))

        def rws(w, k0, nk):
            blocks.append(([w.rearrange("(c p) n -> p c n", p=128)[:, k0:k0 + nk, :]], nk, w.shape[1]))

        def pair(w, w2, k0):
            blocks.append(([m.rearrange("(c p) n -> p c n", p=128)[:, k0:k0 + 2, :] for m in (w, w2)], 4, w.shape[1]))

        for l in range(2):
            ad = [(lambda j=j: cols(a["ada_w"][0], 512 * j, 512)) for j in range(12)] if l == 0 else []
            for j in range(4 if l == 0 else 0):
                ad[j]()
            for j in range(6):
                cols(a["w_in"][l], 512 * j, 512)
                if l == 0 and j < 4:
                    ad[4 + 2 * j]()
                    ad[5 + 2 * j]()
            cols(a["w_in"][l], 3584, 16)
            cols(a["w_in"][l], 3072, 512)
            for j in range(4):
                cols(a["w_in"][l], 3600 + 512 * j, 512)
            rws(a["w_branch_a"][l], 0, 4)
            rws(a["w_branch_b"][l], 0, 4)
            rws(a["w_out"][l], 0, 4)
            rws(a["w_out"][l], 4, 4)
            for j in range(8):
                cols(a["w_mlp1"][l], 512 * j, 512)
                if l == 0:
                    cols(a["ada_w"][1], 512 * j, 512)
            for j in range(8):
                rws(a["w_mlp2"][l], 4 * j, 4)
                if l == 0 and j < 4:
                    cols(a["ada_w"][1], 512 * (8 + j), 512)
        for l in range(2):
            for j in (1, 2, 3, 0):
                cols(a["w_in_2"][l], 512 * j, 512 if j < 3 else 288)
            rws(a["mla_w_uq_2"][l], 0, 2)
            rws(a["mla_w_ukv_2"][l], 0, 1)
            rws(a["w_out_2"][l], 0, 4)
            rws(a["w_out_2"][l], 4, 4)
            cols(a["w_router_2"][l], 0, 16)
            first_expert.append(len(blocks))
            for e in range(17):
                if e < 16:
                    for j in range(4):
                        pair(a["w_gate_2"][l, e], a["w_up_2"][l, e], 2 * j)
                if e:
                    rws(a["w_down_2"][l, e - 1], 0, 4)
                    rws(a["w_down_2"][l, e - 1], 4, 4)
            last_expert.append(len(blocks))

        landed = [Landing() for _ in range(NR + 1)]
        place = []
        line = [(q, None) for q in range(NR)]
        for i in range(len(blocks)):
            for m_, f_ in enumerate(first_expert):
                if i == f_ + 3:
                    line.insert(0, (NR, ("more", m_)))
            if line[0][0] == NR and not any(f_ <= i < e_ for f_, e_ in zip(first_expert, last_expert)):
                line.pop(0)
            place.append(line.pop(0))
            line.append((place[-1][0], i))
        got = {}
        used = {}
        at = [0]

        def issue():
            while at[0] < len(blocks):
                i = at[0]
                s, before = place[i]
                if before is not None and before not in used:
                    return
                src, k, n = blocks[i]
                mem = ring[:, s * 4096:s * 4096 + k * n] if s < NR else c2t[:, 18432:18432 + k * n]
                dst = mem.rearrange("p (k n) -> p k n", k=k)
                kk = k // len(src)
                for m_, sr in enumerate(src):
                    tk = landed[s].load(SP, dst[:, kk * m_:kk * m_ + kk, :], sr, used.get(before), slow=n < 128)
                got[i] = (dst, tk)
                at[0] += 1
                if i == 0:
                    return
        nxt = [0]
        issue()

        def take():
            i = nxt[0]
            nxt[0] += 1
            return i, got[i][0], got[i][1]

        def release(i, tok):
            used[i] = tok
            issue()

        l_c = Landing()
        t_c = l_c.load(A, c1[:, :], a["c1"])
        l_p = Landing()
        stage = zone(0, 384)
        pd = []

        def prow(k, r0, src, n):
            pd.append(l_p.load(A, stage[r0:r0 + n, 128 * k:128 * k + 128], src))
            return 128 * k + r0

        def r128(ap):
            return ap.rearrange("(r q) -> r q", q=128)

        t_z = V(lambda e: e.memset(stage, 0.0))
        A.wait([t_z])
        pc = [{}, {}]
        for l in range(2):
            d = pc[l]
            d["n1"] = prow(l, 0, r128(a["norm1_g"][l]), 8)
            d["n2"] = prow(l, 8, r128(a["norm2_g"][l]), 8)
            d["ada_b"] = prow(l, 16, r128(a["ada_b"][l]), 48)
            d["og"] = prow(l, 64, r128(a["dn_out_gain"][l]), 1)
            d["sg"] = prow(l, 65, r128(a["diff_subln_gain"][l]), 1)
            d["cv"] = prow(l, 66, a["dn_conv"][l].rearrange("k (f q) -> (k f) q", q=128), 60)
            o = 8 + 27 * l
            d["an"] = prow(2, o, r128(a["attn_norm_2"][l]), 8)
            d["fn"] = prow(2, o + 8, r128(a["ffn_norm_2"][l]), 8)
            d["gn"] = prow(2, o + 16, r128(a["group_norm_2"][l]), 8)
            d["qn"] = prow(2, o + 24, r128(a["mla_q_norm_2"][l]), 2)
            d["kn"] = prow(2, o + 26, r128(a["mla_kv_norm_2"][l]), 1)
        p_c = prow(2, 0, a["c"].rearrange("a (r q) -> (a r) q", q=128), 8)

        def pcol(o, n=1):
            return par[:, o:o + n]

        l_x = Landing()
        xd = a["x"][0].rearrange("(t p) d -> p t d", p=128)
        x3 = x[:, :].rearrange("p (t d) -> p t d", t=2)
        t_x = l_x.load(A, x3, xd)

        l_r = Landing()
        rc = {}
        ro = [0]

        def prw(name, ap, n):
            o = ro[0]
            ro[0] += n
            rc[name] = (o, l_r.load(A, rows[:, o:o + n], ap.partition_broadcast(128)))
            return o

        SP.wait([pd[-1], t_c])
        issue()

        k = get()
        tp = None
        for j in range(3):
            tp = tr(banks[k][:, 128 * j:128 * j + 128], stage[:, 128 * j:128 * j + 128], pd[-1], t_c, inc=True)
        t_par = copy(V, par[:, :], banks[k][:, 0:384], tp)
        put(k, t_par)
        c_act = S(8)
        sctmp = S(8)

        t = act(sctmp, pcol(p_c, 8), ACT.Tanh, t_par, scale=0.5)
        ts(V, sctmp, sctmp, 0.5, 0.5, ALU.mult, ALU.add, t)
        t_cact = tt(V, cact[:, :], sctmp, pcol(p_c, 8), ALU.mult)
        for l in range(2):
            o_ = pc[l]["cv"]
            t_cact = ts(V, pcol(o_, 60), pcol(o_, 60), 0.5, None, ALU.mult, ALU.bypass)

        def rsqrt(o, i, scale, *after):
            n = 1
            for d in i.shape[1:]:
                n *= d
            v, q = S(n), S(n)
            if len(i.shape) == 3:
                v, q = v4(v, i.shape[1]), v4(q, i.shape[1])
            ts(V, v, i, scale, EPS, ALU.mult, ALU.add, *after)
            ts(V, o.bitcast(I32), v.bitcast(I32), -0.5, 1597463007.0, ALU.mult, ALU.add)
            for _ in range(3):
                tt(V, q, o, o, ALU.mult)
                stt(q, q, -0.5, v, ALU.mult, ALU.mult)
                tk = stt(o, q, 1.5, o, ALU.add, ALU.mult)
            return tk

        xr = [None]
        xsq = [None]

        def norm_r():
            ss = S(2)
            s4 = v4(sq4[:, :], 2)
            tt(V, ss, s4[:, :, 0], s4[:, :, 1], ALU.add, xsq[0])
            return rsqrt(rstd[:, :], ss, 1.0 / 1024)

        def normed():
            tk = norm_r()
            for t in range(2):
                tk = ts(V, xn[:, 1024 * t:1024 * t + 1024], x3[:, t, :], rstd[:, t:t + 1], None, ALU.mult, ALU.bypass, tk)
            return tk

        def norm_diag(D):
            norm_r()
            for t in range(2):
                tk = ts(V, D[:, 128 * t:128 * t + 128], K("ident"), rstd[:, t:t + 1], None, ALU.mult, ALU.bypass, t_c)
            return tk

        def turn(cp, D, tk):
            k = get()
            for j in range(2):
                for t in range(2):
                    cc = 2 * cp + j
                    tp = mm(banks[k][:, 256 * j + 128 * t:256 * j + 128 * t + 128], x3[:, t, 128 * cc:128 * cc + 128],
                            D[:, 128 * t:128 * t + 128], True, True, tk, bank_after[k], inc=(j == 1 and t == 1))
            return k, tp

        def x_hT(D, sa, sbias, *after, each=None):
            td = norm_diag(D)
            if each is not None:
                each(-1, None)
            toks = []
            for cp in range(4):
                k, tp = turn(cp, D, td)
                for j in range(2):
                    cc = 2 * cp + j
                    i = banks[k][:, 256 * j:256 * j + 256]
                    if cp % 2:
                        if sbias is None:
                            te = act(hT3[:, cc, :], i, ACT.Copy, tp, *after, scale=sa(cc))
                        else:
                            te = act(hT3[:, cc, :], i, ACT.Identity, tp, *after, scale=sa(cc), bias=sbias(cc))
                    else:
                        s2 = None if sbias is None else sbias(cc)
                        te = ts(V, hT3[:, cc, :], i, sa(cc), s2, ALU.mult, ALU.bypass if s2 is None else ALU.add, tp, *after)
                put(k, te)
                toks.append(te)
                if each is not None and cp:
                    each(cp - 1, toks[cp - 1])
            if each is not None:
                each(3, toks[3])
            return toks

        def part(tl, c):
            return tl[c // 2] if isinstance(tl, list) and len(tl) == 4 else tl

        def to_hT(src, sa, sbias, tk, dst=None, *after):
            dst = hT3 if dst is None else dst
            toks = []
            for cp in range(4):
                k = get()
                for j in range(2):
                    for t in range(2):
                        cc = 2 * cp + j
                        tp = tr(banks[k][:, 256 * j + 128 * t:256 * j + 128 * t + 128],
                                src[:, 1024 * t + 128 * cc:1024 * t + 128 * cc + 128], tk, t_c, bank_after[k],
                                inc=(j == 1 and t == 1))
                for j in range(2):
                    cc = 2 * cp + j
                    i = banks[k][:, 256 * j:256 * j + 256]
                    if cp % 2:
                        if sbias is None:
                            te = act(dst[:, cc, :], i, ACT.Copy, tp, *after, scale=sa(cc))
                        else:
                            te = act(dst[:, cc, :], i, ACT.Identity, tp, *after, scale=sa(cc), bias=sbias(cc))
                    else:
                        s2 = None if sbias is None else sbias(cc)
                        te = ts(V, dst[:, cc, :], i, sa(cc), s2, ALU.mult, ALU.bypass if s2 is None else ALU.add, tp, *after)
                put(k, te)
                toks.append(te)
            return toks

        def lin_tok(lhs, tl, w, tw, n, nk, evac, k0=0):
            tp = None
            for t in range(2):
                k = get()
                for c in range(nk):
                    tp = mm(banks[k][:, 0:n], lhs[:, k0 + c, 128 * t:128 * t + 128], w[:, c, 0:n], c == 0, c == nk - 1,
                            part(tl, c), tw, bank_after[k], inc=(c == nk - 1))
                put(k, evac(t, banks[k][:, 0:n], tp))
            return tp

        def lin3(m, turned, ns, evac, ahead=None):
            hs, ws = split_proj(m)
            A.wait([V.last, (P.sem, P.n)])
            V.wait([A.last, (P.sem, P.n)])
            thi, tlo = [], []

            def parts(cp, te):
                if cp < 0:
                    return split(0)
                d = slice(2 * cp, 2 * cp + 2)
                thi.append(copy(A, hs[0][:, d, :], hT3[:, d, :], te))
                tlo.append(tt(V, hs[1][:, d, :], hT3[:, d, :], hs[0][:, d, :], ALU.subtract, thi[-1], te))
            cut, free, held = {}, {}, [None]

            def split(g):
                if g >= 4 * len(ns):
                    return
                if g % 4 == 0:
                    if g and ahead is not None:
                        ahead(g // 4)
                    held[0] = take()
                i, w, tw = held[0]
                n, q = ns[g // 4], g % 4
                hi, lo = [v4(z[:, 0:2 * n], 2) for z in ws[g % 2]]
                ta = copy(A, hi, w[:, 2 * q:2 * q + 2, :], tw, free.get(g - 2))
                tv = tt(V, lo, w[:, 2 * q:2 * q + 2, :], hi, ALU.subtract, ta)
                cut[g] = (hi, lo, tv)
                if q == 3:
                    release(i, tv)
            th = turned(parts)
            split(1)
            for g in range(4 * len(ns)):
                n, q = ns[g // 4], g % 4
                if q == 0:
                    ks = [get(), get()]
                hi, lo, tv = cut[g]
                for t in range(2):
                    u = 0
                    for wp, hp, tl in ((hi, 0, thi), (lo, 0, thi), (hi, 1, tlo)):
                        for c2 in range(2):
                            tp = mm(banks[ks[t]][:, 0:n], hs[hp][:, 2 * q + c2, 128 * t:128 * t + 128], wp[:, c2, :],
                                    q == 0 and u == 0, q == 3 and u == 5, tv, tl[q], bank_after[ks[t]], inc=(t == 1 and u == 5))
                            u += 1
                free[g] = tp
                split(g + 2)
                if q == 3:
                    for t in range(2):
                        put(ks[t], evac(g // 4, t, banks[ks[t]][:, 0:n], tp))
            V.wait([tp])
            A.wait([tp])
            return th

        def lin_feat(w, tw, rhs, tr_, nk, f0, evac):
            k = get()
            tp = None
            for j in range(2):
                for c in range(nk):
                    tp = mm(banks[k][:, 256 * j:256 * j + 256], w[:, c, 128 * (f0 + j):128 * (f0 + j) + 128],
                            rhs[:, c, :], c == 0, c == nk - 1, tr_, tw, bank_after[k], inc=(c == nk - 1 and j == 1))
            put(k, evac(f0, banks[k][:, :].rearrange("p (j n) -> p j n", j=2), tp))
            return tp

        ada_at = [0]
        ada_read = [None, None]

        def ada_v(l, j, room):
            i, w, tw = take()
            b = ada_at[0] % 2
            ada_at[0] += 1
            k = get()
            for c in range(8):
                q = 32 * (c % 4)
                tp = mm(banks[k][q:q + 32, :], bc(cact[:, c:c + 1], [128, 32]), w[:, c, :], c < 4, c >= 4, tw, t_cact,
                        bank_after[k], inc=(c == 7))
            release(i, tp)
            acc = room[:, 512 * b:512 * b + 512]
            tk = act(acc, banks[k][:, :], ACT.Copy, tp, ada_read[b], scale=1.0 / 32)
            put(k, tk)
            return l, j, b, acc, tk

        def ada_pe(state):
            l, j, b, acc, tk = state
            k = get()
            for f in range(4):
                tp = mm(banks[k][:, f:f + 1], acc[:, 128 * f:128 * f + 128], K("ones")[:, 0:1], True, True, tk, t_c,
                        bank_after[k], inc=(f == 3))
            ada_read[b] = tp
            tk = tt(V, modT2[l][:, 4 * j:4 * j + 4], banks[k][:, 0:4], pcol(pc[l]["ada_b"] + 4 * j, 4), ALU.add, tp)
            put(k, tk)
            return tk

        def diags(dg, src, *after):
            return tt(V, v4(dg, 8), bc(K("ident").unsqueeze(1), [128, 8, 128]), bc(src.unsqueeze(2), [128, 8, 128]),
                      ALU.mult, *after)

        def spread(dst, dg, tk, *after):
            for h in range(2):
                k = get()
                tp = mm(banks[k][:, :], K("ones"), dg[:, 512 * h:512 * h + 512], True, True, tk, bank_after[k], inc=True)
                te = copy(A if h else V, dst[:, 512 * h:512 * h + 512], banks[k][:, :], tp, *after)
                put(k, te)
                after = after + (te,)
            return te

        def interleave(filler, *gens):
            live = list(gens)
            while live:
                for g in list(live):
                    try:
                        n = next(g)
                    except StopIteration:
                        live.remove(g)
                        continue
                    for _ in range(n or 0):
                        next(filler, None)

        def softmax_pair(tl, kT, qT, bias, scale, sc_s, sc_e, sink):
            k = get()
            for t in range(2):
                tp = mm(banks[k][:, 256 * t:256 * t + 256], qT[:, 128 * t:128 * t + 128], kT, True, True,
                        tl, bank_after[k], inc=(t == 1))
            b3 = banks[k][:, :].rearrange("p (t n) -> p t n", t=2)
            e3 = sc_e.rearrange("p (t n) -> p t n", t=2)
            src, sc = b3, scale
            if bias is not None:
                s3 = sc_s.rearrange("p (t n) -> p t n", t=2)
                tk = stt(s3, b3, scale, bias, ALU.mult, ALU.add, tp)
                put(k, tk)
                src, sc = s3, 1.0
            mx, nm, smv = S(2), S(2), S(2)
            V(lambda e: e.tensor_reduce(mx, src, AX.X, ALU.max), tp)
            if sink is not None:
                ts(V, mx, mx, sink, None, ALU.max, ALU.bypass)
            tn = ts(V, nm, mx, -sc, None, ALU.mult, ALU.bypass)
            for t in range(2):
                te = act(e3[:, t, :], src[:, t, :], ACT.Exp, tn, tp, bias=nm[:, t:t + 1], scale=sc,
                         accum=smv[:, t:t + 1])
            if bias is None:
                put(k, te)
            if sink is not None:
                es = S(2)
                te = act(es, nm, ACT.Exp, bias=sink)
                tt(V, smv, smv, es, ALU.add, te)
            r = S(2)
            tk = V(lambda e: e.reciprocal(r, smv), te)
            return e3, r, te, tk

        def probs_T(e3, te, sc_t, q, *after):
            k = get()
            for t in range(2):
                for kt in range(2):
                    tp = tr(banks[k][:, 256 * t + 128 * kt:256 * t + 128 * kt + 128], e3[:, t, 128 * kt:128 * kt + 128],
                            te, bank_after[k], inc=(t == 1 and kt == 1))
            tk = copy(q, sc_t, banks[k][:, :], tp, *after)
            put(k, tk)
            return tk, tp

        def pv(sc_t, tk, v, dv, tv):
            k = get()
            for t in range(2):
                for kt in range(2):
                    tp = mm(banks[k][:, dv * t:dv * t + dv], sc_t[:, 256 * t + 128 * kt:256 * t + 128 * kt + 128],
                            v(kt), kt == 0, kt == 1, tk, tv, bank_after[k], inc=(t == 1 and kt == 1))
            return k, tp

        Z1, ZST, ZTOK, ZDT, ZLT, ZAT, ZG, ZZ, ZY = 0, 6144, 9264, 12336, 14384, 16432, 18480, 22576, 23600
        tmod = [None]
        N = dict(si=1, fr=1, fine=1, held=2, rope=9, sc=1, co=1, va=0, hn=1, g=1, kq=3, dT=0, LT=0, X=4, scan=1)

        def block1(l):
            pl = pc[l]
            modT = modT2[l]
            if l == 0:
                ads = [ada_v(0, j, zone(18480, 1024)) for j in range(2)]
                ads = [ada_pe(q) for q in ads] and [ada_v(0, j, zone(18480, 1024)) for j in range(2, 4)]
                tmod[0] = [ada_pe(q) for q in ads][-1]
            tm = tmod[0]
            sa = S(8)
            ts(V, sa, modT[:, 8:16], 1.0, None, ALU.add, ALU.bypass)
            sa1 = sas[l]
            tsa = tt(V, sa1[:, :], sa, pcol(pl["n1"], 8), ALU.mult)

            qk = xn[:, :].rearrange("p (t n) -> p t n", t=2)
            vA = zone(ZLT, 1024).rearrange("p (t n) -> p t n", t=2)
            ev = {}

            def plain(dst, q):
                def f(t, b, tp):
                    ev[0] = copy(q, dst(t), b, tp)
                    return ev[0]
                return f
            ads = []

            def ev3(j, t, b, tp):
                ev[j] = copy(A, qk[:, t, 512 * j:512 * j + 512] if j < 2 else vA[:, t, :], b, tp)
                return ev[j]

            def ahead(j):
                nonlocal ads
                for q in ads:
                    tmod[0] = ada_pe(q)
                if l == 0:
                    ads = [ada_v(0, 4 + 2 * (j - 1) + q, zone(ZZ, 1024)) for q in range(2)]
            def turned(each):
                return x_hT(xn[:, 0:256], lambda c: sa1[:, c:c + 1], lambda c: modT[:, c:c + 1], tsa, tm, each=each)
            th = lin3(f"a{l}", turned, [512, 512, 512], ev3, ahead)
            ahead(3)
            tqk, tevj = ev[1], ev[2]
            tvA = tevj

            ro[0] = 0
            if l:
                A.wait([V.last])
            prw("qkg", a["qk_norm_gain"][l].rearrange("a d -> (a d)"), 128)
            prw("al", a["dn_A_log"][l].rearrange("a d -> (a d)"), 8)
            prw("dt", a["dn_dt_bias"][l].rearrange("a d -> (a d)"), 8)
            lamd = zone(ZY, 256)
            tl_ = l_r.load(A, lamd, a["diff_lambda"][l].rearrange("a d -> (a d)").partition_broadcast(128))

            cin = zone(ZST, 3120).rearrange("p (f n) -> p f n", f=12)
            tpad = V(lambda e: e.memset(cin[:, :, 0:2], 0.0))
            tpad = V(lambda e: e.memset(cin[:, :, 258:260], 0.0))
            babs = bas[l]
            ba = babs[:, :].rearrange("p (t n) -> p t n", t=2)
            st = {}
            zT = zone(ZZ, 1024).rearrange("p (f n) -> p f n", f=4)
            gT = zone(ZG, 4096).rearrange("p (f n) -> p f n", f=16)
            yaT = zone(ZY, 1024).rearrange("p (f n) -> p f n", f=4)
            ybT = zone(ZY + 1024, 1024).rearrange("p (f n) -> p f n", f=4)

            def proj_dn():
                pend = None
                ads2 = None
                for j in range(3):
                    i, w, tw = take()
                    for f in (0, 2):
                        def e(f0, b, tp, j=j):
                            q = A if f0 else V
                            st["cin", j, f0] = copy(q, cin[:, 4 * j + f0:4 * j + f0 + 2, 2:258], b, tp)
                            return st["cin", j, f0]
                        u = feat_steps(w, tw, f, e, i if f else None)
                        next(u)
                        yield
                        if pend is not None:
                            next(pend, None)
                        next(u)
                        pend = u
                        yield
                    if l == 0 and j < 2:
                        for q in (ads if j == 0 else ads2):
                            tmod[0] = ada_pe(q)
                        if j == 0:
                            ads2 = [ada_v(0, 10 + q, zone(ZZ, 1024)) for q in range(2)]
                next(pend, None)
                i, w, tw = take()

                def e(t, b, tp):
                    st["ba"] = copy(V, ba[:, t, :], b, tp)
                    return st["ba"]
                tp = lin_tok(hT3, th, w, tw, 16, 8, e)
                release(i, tp)
                yield
                st["proj"] = True

            def gates():
                pend = None
                for j in range(5):
                    i, w, tw = take()
                    for f in (0, 2):
                        def e(f0, b, tp, j=j):
                            dst = zT[:, f0:f0 + 2, :] if j == 0 else gT[:, 4 * (j - 1) + f0:4 * (j - 1) + f0 + 2, :]
                            te = act(dst, b, ACT.Tanh, tp, st["rope_done"], scale=0.5)
                            if j == 0:
                                te = stt(dst, dst, 1.0, b, ALU.add, ALU.mult, te)
                            st["gates"] = te
                            return te
                        u = feat_steps(w, tw, f, e, i if f else None)
                        next(u)
                        yield
                        if pend is not None:
                            next(pend, None)
                        next(u)
                        pend = u
                        yield
                next(pend, None)

            def feat_steps(w, tw, f0, evac, blk):
                k = get()
                for j in range(2):
                    for c in range(8):
                        tp = mm(banks[k][:, 256 * j:256 * j + 256], w[:, c, 128 * (f0 + j):128 * (f0 + j) + 128],
                                hT3[:, c, :], c == 0, c == 7, part(th, c), tw, bank_after[k], inc=(c == 7 and j == 1))
                    if j == 1 and blk is not None:
                        release(blk, tp)
                    yield
                put(k, evac(f0, banks[k][:, :].rearrange("p (j n) -> p j n", j=2), tp))

            def attn_a():
                g = rows[:, 0:128]
                tr_ = rc["dt"][1]
                cg, sg = zone(ZY + 256, 256), zone(ZY + 512, 256)
                cg4 = v4(cg, 2, 2)
                sg4 = v4(sg, 2, 2)
                cosr = v4(K("cos64"), 2)
                sinr = v4(K("sin64"), 2)
                for t in range(2):
                    tt(V, cg4[:, t], bc(cosr[:, t:t + 1, :], [128, 2, 64]), v4(g, 2), ALU.mult, tr_, tl_, t_c)
                    for h in range(2):
                        tt(V, sg4[:, t, :, 32 * h:32 * h + 32], bc(sinr[:, t:t + 1, 32 * h:32 * h + 32], [128, 2, 32]),
                           v4(g, 2)[:, :, 32 - 32 * h:64 - 32 * h], ALU.mult)
                l4 = v4(lamd, 4)
                pr = S(128)
                p3 = v4(pr, 2)
                l2 = lamd.rearrange("p (a b d) -> p a b d", a=2, b=2)
                tt(V, p3, l2[:, :, 0, :], l2[:, :, 1, :], ALU.mult)
                sl = S(2)
                tk = V(lambda e: e.tensor_reduce(sl, p3, AX.X, ALU.add))
                tk = act(sl, sl, ACT.Exp, tk)
                lam = lams[l]
                tt(V, lam[:, :], sl[:, 0:1], sl[:, 1:2], ALU.subtract, tk)
                li = 0.8 - 0.6 * math.exp(-0.3 * l)
                ts(V, lam[:, :], lam[:, :], li, None, ALU.add, ALU.bypass)
                sq = zone(ZG, 2048)
                t1 = zone(ZG + 2048, 2048)
                tk = act(sq, xn[:, :], ACT.Square, tqk)
                ss = S(32)
                tk = V(lambda e: e.tensor_reduce(ss, v4(sq, 32), AX.X, ALU.add), tk)
                tk = rsqrt(ss, ss, 1.0 / 64, tk)
                q32 = v4(xn[:, :], 32)
                yield
                tt(V, q32, q32, bc(ss.unsqueeze(2), [128, 32, 64]), ALU.mult, tk, tqk)
                yield
                t14 = t1.rearrange("p (a g d) -> p a g d", a=4, g=8)
                sq4 = sq.rearrange("p (a g d) -> p a g d", a=4, g=8)
                q4 = xn[:, :].rearrange("p (a g d) -> p a g d", a=4, g=8)
                cga = cg.rearrange("p (a d) -> p a d", a=4)
                sga = sg.rearrange("p (a d) -> p a d", a=4)
                for i in range(4):
                    tt(V, t14[:, i], q4[:, i], bc(cga[:, i:i + 1, :], [128, 8, 64]), ALU.mult)
                    for h in range(2):
                        tt(V, sq4[:, i, :, 32 * h:32 * h + 32], q4[:, i, :, 32 - 32 * h:64 - 32 * h],
                           bc(sga[:, i:i + 1, 32 * h:32 * h + 32], [128, 8, 32]), ALU.mult)
                    yield
                tk = tt(V, t1, t1, sq, ALU.add)
                yield N["rope"]
                QT = v4(zone(ZDT, 2048), 8)
                t13 = v4(t1, 2)
                for cp in (0, 2, 1, 3):
                    k = get()
                    for j in range(2):
                        for t in range(2):
                            cc = 2 * cp + j
                            tp = tr(banks[k][:, 256 * j + 128 * t:256 * j + 128 * t + 128],
                                    t13[:, t, 128 * cc:128 * cc + 128], tk, bank_after[k], inc=(j == 1 and t == 1))
                    tq = copy(A if cp % 2 else V, QT[:, 2 * cp:2 * cp + 2, :], v4(banks[k][:, :], 2), tp)
                    put(k, tq)
                    st["qT", cp] = tq
                    yield
                tq = [st["qT", i] for i in range(4)]
                st["qTdone"] = True
                st["rope_done"] = tk
                sc = [zone(ZLT + 1024 + 512 * i, 512) for i in range(2)] + [zone(ZAT + 512 * i, 512) for i in range(4)]
                o = zone(ZY + 1024, 1024).rearrange("p (t h d) -> p t h d", t=2, h=4)
                es, ptr, lastpv, tkt = {}, {}, {}, {}

                def scores(h):
                    es[h] = []
                    for c in range(2):
                        kT = QT[64 * c:64 * c + 64, 4 + h, :]
                        qT = QT[64 * c:64 * c + 64, h, :]
                        A.wait([ptr.get(h - 2)])
                        es[h].append(softmax_pair([st["qT", h // 2], st["qT", 2 + h // 2]], kT, qT, None, 0.125, None, sc[2 * (h % 2) + c], None))

                def combine(h):
                    (e0, r0, te0, _), (e1, r1, te1, _) = es[h]
                    rl = S(2)
                    ts(V, rl, r1, lam[:, 0:1], None, ALU.mult, ALU.bypass)
                    for t in range(2):
                        ts(V, e1[:, t, :], e1[:, t, :], rl[:, t:t + 1], None, ALU.mult, ALU.bypass, te1)
                        ta = stt(e0[:, t, :], e0[:, t, :], r0[:, t:t + 1], e1[:, t, :], ALU.mult, ALU.subtract, te0)
                    tkt[h], ptr[h] = probs_T(e0, ta, sc[4 + h % 2], A, lastpv.get(h - 2))

                def values(h):
                    k, tp = pv(sc[4 + h % 2], tkt[h], lambda kt: vA[:, kt, 128 * h:128 * h + 128], 128, tvA)
                    lastpv[h] = tp
                    st["oa"] = copy(V, o[:, :, h, :], banks[k][:, 0:256].rearrange("p (t d) -> p t d", t=2), tp)
                    put(k, st["oa"])

                for s_ in range(6):
                    if s_ < 4:
                        scores(s_)
                        yield N["sc"]
                    if 1 <= s_ < 5:
                        combine(s_ - 1)
                        yield N["co"]
                    if s_ >= 2:
                        values(s_ - 2)
                        yield N["va"]
                st["free"] = st["oa"]
                yield N["fr"]
                hn = head_norm(o, zone(ZY, 1024), st["oa"], pcol(pl["sg"]), 1.0 - li, None, yaT)
                next(hn)
                yield N["hn"]
                st["ya"] = next(hn)
                st["attn_end"] = True
                yield

            def head_norm(o, tmp, to, gain, fac, mulT, dst, *after):
                o2 = o.rearrange("p t h d -> p (t h d)")
                tk = act(tmp, o2, ACT.Square, to)
                ss = S(8)
                tk = V(lambda e: e.tensor_reduce(ss, v4(tmp, 8), AX.X, ALU.add), tk)
                tk = rsqrt(ss, ss, 1.0 / 128, tk)
                o8 = v4(o2, 8)
                if fac != 1.0:
                    ts(V, ss, ss, fac, None, ALU.mult, ALU.bypass, tk)
                tk = tt(V, o8, o8, bc(ss.unsqueeze(2), [128, 8, 128]), ALU.mult, tk)
                yield
                for hp in range(2):
                    k = get()
                    for j in range(2):
                        for t in range(2):
                            tp = tr(banks[k][:, 256 * j + 128 * t:256 * j + 128 * t + 128], o[:, t, 2 * hp + j, :], tk,
                                    bank_after[k], inc=(j == 1 and t == 1))
                    b = v4(banks[k][:, :], 2)
                    if mulT is None:
                        te = ts(V, dst[:, 2 * hp:2 * hp + 2, :], b, gain, None, ALU.mult, ALU.bypass, tp, *after)
                    else:
                        te = stt(dst[:, 2 * hp:2 * hp + 2, :], b, gain, mulT[:, 2 * hp:2 * hp + 2, :], ALU.mult, ALU.mult, tp, *after)
                    put(k, te)
                yield te

            beta, graw, gsm, ge = (gper[:, o_:o_ + n_] for o_, n_ in ((0, 16), (16, 16), (32, 64), (96, 64)))

            def delta():
                acc = v4(zone(Z1, 3072), 12)
                tmp = v4(zone(Z1 + 3072, 3072), 12)
                TOK = zone(ZTOK, 3072).rearrange("p (g t h d) -> p g t h d", g=3, t=2, h=4)
                cv = pl["cv"]
                tconv = {}
                for g in range(3):
                    while ("cin", g, 2) not in st:
                        yield N["rope"] if "attn_end" in st else 0
                    for f in range(4 * g, 4 * g + 4):
                        tc_ = st["cin", g, 0 if f % 4 < 2 else 2]
                        t0 = act(acc[:, f, :], cin[:, f, 0:256], ACT.Copy, tc_, tpad, scale=pcol(cv + f))
                        for kk in range(1, 5):
                            tk = stt(acc[:, f, :], cin[:, f, kk:kk + 256], pcol(cv + 12 * kk + f), acc[:, f, :],
                                     ALU.mult, ALU.add, t0, tc_)
                        if f % 2 or N["fine"]:
                            yield
                    ag, tg_ = acc[:, 4 * g:4 * g + 4, :], tmp[:, 4 * g:4 * g + 4, :]
                    te = act(tg_, ag, ACT.Tanh, tk)
                    tk = stt(ag, tg_, 1.0, ag, ALU.add, ALU.mult, te)
                    yield N["si"] if g == 2 else 0
                    for t in range(2):
                        k = get()
                        for h in range(4):
                            tp = tr(banks[k][:, 128 * h:128 * h + 128], acc[:, 4 * g + h, 128 * t:128 * t + 128], tk,
                                    bank_after[k], inc=(h == 3))
                        st["tok", g, t] = copy(A, TOK[:, g, t], v4(banks[k][:, :], 4), tp)
                        put(k, st["tok", g, t])
                    yield
                while "proj" not in st:
                    yield N["rope"] if "attn_end" in st else 0
                b3 = v4(beta, 2)
                g3 = v4(graw, 2)
                tk = act(b3, ba[:, :, 0:8], ACT.Tanh, st["ba"], scale=0.5)
                ts(V, b3, b3, 0.5, 0.5, ALU.mult, ALU.add, tk)
                z, nz, sp, ea = v4(S(16), 2), v4(S(16), 2), v4(S(16), 2), S(8)
                dtb = rows[:, 136:144].unsqueeze(1)
                tt(V, z, ba[:, :, 8:16], bc(dtb, [128, 2, 8]), ALU.add)
                ts(V, nz, z, -1.0, None, ALU.mult, ALU.bypass)
                tk = tt(V, nz, nz, z, ALU.max)
                act(sp, nz, ACT.Exp, tk, scale=-1.0)
                tk = act(sp, sp, ACT.Ln, bias=K("ones")[:, 0:1])
                tk = act(ea, rows[:, 128:136], ACT.Exp, rc["dt"][1])
                stt(z, z, 0.0, sp, ALU.max, ALU.add, tk)
                tg = stt(g3, z, -1.0, bc(ea.unsqueeze(1), [128, 2, 8]), ALU.mult, ALU.mult)
                gb = v4(gsm, 2)
                yield N["g"]
                k = get()
                for t in range(2):
                    o = 32 * t
                    for nm, lo, ro_, n in (("triF", 0, 0, 4), ("triB", 4, 4, 4), ("blk", 8, 0, 8), ("half0", 16, 0, 8), ("half1", 24, 0, 8)):
                        tp = mm(banks[k][:, o + lo:o + lo + n], K(nm), g3[:, t, ro_:ro_ + n], True, True, tg, bank_after[k],
                                inc=(t == 1 and nm == "half1"))
                tk = copy(V, gsm, banks[k][:, 0:64], tp)
                put(k, tk)
                tk = tt(V, gb[:, :, 8:16], gb[:, :, 8:16], gb[:, :, 0:8], ALU.subtract)
                tge = act(ge, gsm, ACT.Exp, tk)
                E = v4(ge, 2)
                yield
                ss = S(16)
                sq = zone(Z1 + 3072, 2048)
                tk = act(sq, zone(ZTOK, 2048), ACT.Square)
                tk = V(lambda e: e.tensor_reduce(ss, v4(sq, 16), AX.X, ALU.add), tk)
                tk = rsqrt(ss, ss, 1.0, tk)
                tk = ts(V, ss[:, 0:8], ss[:, 0:8], 128 ** -0.5, None, ALU.mult, ALU.bypass, tk)
                t16 = v4(zone(ZTOK, 2048), 16)
                tk = tt(V, t16, t16, bc(ss.unsqueeze(2), [128, 16, 128]), ALU.mult)
                yield N["kq"]
                while "qTdone" not in st:
                    yield
                kqT = v4(xn[:, :], 4)
                tkq = []
                for h in range(4):
                    k = get()
                    for g in range(2):
                        for t in range(2):
                            tp = tr(banks[k][:, 256 * g + 128 * t:256 * g + 128 * t + 128], TOK[:, 1 - g, t, h, :], tk,
                                    bank_after[k], inc=(g == 1 and t == 1))
                    te = copy(A if h % 2 else V, kqT[:, h, :], banks[k][:, :], tp)
                    put(k, te)
                    tkq.append(te)
                yield
                while "free" not in st:
                    yield
                dT = zone(ZDT, 2048).rearrange("p (i t h d) -> p i t h d", i=2, t=2, h=4)
                tdd = {}
                for i in range(2):
                    tri = K("triF" if i == 0 else "triB")
                    for t in range(2):
                        k = get()
                        for h in range(4):
                            jj = 4 * i + h
                            tp = mm(banks[k][:, 128 * h:128 * h + 128], bc(g3[:, t, jj:jj + 1], [128, 128]), tri, True, True,
                                    tg, bank_after[k], inc=(h == 3))
                        for h in range(4):
                            jj = 4 * i + h
                            tk = stt(dT[:, i, t, h, :], banks[k][:, 128 * h:128 * h + 128], gb[:, t, jj:jj + 1], tri,
                                     ALU.subtract, ALU.mult, tp, st["free"])
                        put(k, tk)
                        te = act(dT[:, i, t], dT[:, i, t], ACT.Exp, tk)
                        tdd[i, t] = tt(V, dT[:, i, t], dT[:, i, t], bc(tri.unsqueeze(1), [128, 4, 128]), ALU.mult, te)
                        yield N["dT"]
                LT = zone(ZLT, 2048).rearrange("p (i t h d) -> p i t h d", i=2, t=2, h=4)
                AT = zone(ZAT, 2048).rearrange("p (i t h d) -> p i t h d", i=2, t=2, h=4)
                X = zone(Z1, 2048).rearrange("p (i t h d) -> p i t h d", i=2, t=2, h=4)
                XT = zone(Z1 + 2048, 2048).rearrange("p (i t h d) -> p i t h d", i=2, t=2, h=4)
                B = zone(Z1 + 4096, 2048).rearrange("p (i t h d) -> p i t h d", i=2, t=2, h=4)
                grp = [(i, t) for i in range(2) for t in range(2)]

                def lv(i, s):
                    return bc(K(("lvF" if i == 0 else "lvB") + str(s)).unsqueeze(1), [128, 4, 128])
                tX, tXT, tB = {}, {}, {}
                while "ya" not in st:
                    yield
                for t in range(2):
                    for hp in range(2):
                        k = get()
                        for j in range(2):
                            h = 2 * hp + j
                            kq = kqT[:, h, :].rearrange("p (g n) -> p g n", g=2)[:, :, 128 * t:128 * t + 128]
                            tp = mm(v4(banks[k][:, 256 * j:256 * j + 256], 2), kqT[:, h, 128 * t:128 * t + 128], kq, True, True,
                                    tkq, bank_after[k], inc=(j == 1))
                        for j in range(2):
                            h = 2 * hp + j
                            for i in range(2):
                                stt(LT[:, i, t, h, :], banks[k][:, 256 * j:256 * j + 128], b3[:, t, 4 * i + h:4 * i + h + 1],
                                    dT[:, i, t, h, :], ALU.mult, ALU.mult, tp)
                            tk = tt(V, dT[:, :, t, h, :], bc(banks[k][:, 256 * j + 128:256 * j + 256].unsqueeze(1), [128, 2, 128]),
                                    dT[:, :, t, h, :], ALU.mult)
                        put(k, tk)
                    tLT = tqkT = tk
                    for i in range(2):
                        tt(V, XT[:, i, t], LT[:, i, t], lv(i, 0), ALU.mult)
                        tXT[i, t] = tt(V, XT[:, i, t], bc(K("ident").unsqueeze(1), [128, 4, 128]), XT[:, i, t], ALU.subtract)
                    yield N["LT"]
                yield N["X"]
                for i, t in grp:
                    k = get()
                    for h in range(4):
                        tp = tr(banks[k][:, 128 * h:128 * h + 128], XT[:, i, t, h, :], tXT[i, t], bank_after[k], inc=(h == 3))
                    tX[i, t] = copy(A, X[:, i, t], v4(banks[k][:, :], 4), tp)
                    put(k, tX[i, t])
                yield
                pB = {}
                for s in range(1, 6):
                    for i, t in grp:
                        ta = tt(G, AT[:, i, t], LT[:, i, t], lv(i, s), ALU.mult, tLT, pB.get((i, t)))
                        k = get()
                        for h in range(4):
                            tp = mm(banks[k][:, 128 * h:128 * h + 128], AT[:, i, t, h, :], X[:, i, t, h, :], True, True, ta,
                                    tX[i, t], bank_after[k], inc=(h == 3))
                        pB[i, t] = tp
                        tB[i, t] = copy(A, B[:, i, t], v4(banks[k][:, :], 4), tp)
                        put(k, tB[i, t])
                    yield
                    for i, t in grp:
                        if s < 5:
                            k = get()
                            for h in range(4):
                                tp = mm(banks[k][:, 128 * h:128 * h + 128], XT[:, i, t, h, :], B[:, i, t, h, :], True, True,
                                        tB[i, t], tXT[i, t], bank_after[k], inc=(h == 3))
                            tX[i, t] = tt(V, X[:, i, t], X[:, i, t], v4(banks[k][:, :], 4), ALU.subtract, tp)
                            put(k, tX[i, t])
                        k = get()
                        for h in range(4):
                            tp = mm(banks[k][:, 128 * h:128 * h + 128], B[:, i, t, h, :], XT[:, i, t, h, :], True, True,
                                    tB[i, t], tXT[i, t], bank_after[k], inc=(h == 3))
                        tXT[i, t] = tt(V, XT[:, i, t], XT[:, i, t], v4(banks[k][:, :], 4), ALU.subtract, tp)
                        put(k, tXT[i, t])
                    yield
                KG, KD, BU, WT = AT, LT, X, B
                ktok, vtok = TOK[:, 1], TOK[:, 2]
                tbu, twt, tkd = {}, {}, {}
                for i, t in grp:
                    egb = bc(E[:, t, 4 * i:4 * i + 4].unsqueeze(2), [128, 4, 128])
                    kdb = bc(E[:, t, 8 + 4 * i:12 + 4 * i].unsqueeze(2), [128, 4, 128])
                    tkg = tt(V, KG[:, i, t], ktok[:, t], egb, ALU.mult, tge, pB[i, t])
                    tkd[i, t] = tt(V, KD[:, i, t], ktok[:, t], kdb, ALU.mult, G.last)
                    k = get()
                    for h in range(4):
                        tp = mm(banks[k][:, 128 * h:128 * h + 128], XT[:, i, t, h, :], vtok[:, t, h, :], True, True,
                                tXT[i, t], st["tok", 2, 1], bank_after[k], inc=(h == 3))
                    tbu[i, t] = tt(V, BU[:, i, t], v4(banks[k][:, :], 4),
                                   bc(b3[:, t, 4 * i:4 * i + 4].unsqueeze(2), [128, 4, 128]), ALU.mult, tp)
                    put(k, tbu[i, t])
                    k = get()
                    for h in range(4):
                        tp = mm(banks[k][:, 128 * h:128 * h + 128], KG[:, i, t, h, :], XT[:, i, t, h, :], True, True, tkg,
                                bank_after[k], inc=(h == 3))
                    twt[i, t] = copy(A, WT[:, i, t], v4(banks[k][:, :], 4), tp)
                    put(k, twt[i, t])
                    yield
                st["XTread"] = (P.sem, P.n)
                ST = zone(ZST, 3072).rearrange("p (i s h d) -> p i s h d", i=2, s=3, h=4)
                tS = {}
                tvn = {}
                tmpd = [zone(ZAT, 512), zone(ZAT + 512, 512)]
                twm = [None, None]
                for s in range(4):
                    for i in range(2):
                        n = s if i == 0 else 3 - s
                        t, p0 = n // 2, 64 * (n % 2)
                        pp = slice(p0, p0 + 64)
                        if s:
                            k = get()
                            for h in range(4):
                                tp = mm(banks[k][pp, 128 * h:128 * h + 128], WT[:, i, t, h, pp], ST[:, i, s - 1, h, :], True, True,
                                        tS[i, s], twt[i, t], bank_after[k], inc=(h == 3))
                            tw3 = v4(tmpd[i][pp, :], 4)
                            tk = tt(V, tw3, v4(banks[k][pp, :], 4),
                                    bc(b3[pp, t, 4 * i:4 * i + 4].unsqueeze(2), [64, 4, 128]), ALU.mult, tp, twt[1, 1])
                            put(k, tk)
                            tvn[i, n] = tt(V, BU[pp, i, t], BU[pp, i, t], tw3, ALU.subtract)
                        else:
                            tvn[i, n] = tbu[i, t]
                        if s < 3:
                            k = get()
                            for h in range(4):
                                tp = mm(banks[k][:, 128 * h:128 * h + 128], KD[pp, i, t, h, :], BU[pp, i, t, h, :], True, True,
                                        tvn[i, n], tkd[i, t], bank_after[k], inc=(h == 3))
                            if s:
                                glb = bc(E[:, t, 16 + 8 * (n % 2) + 4 * i:20 + 8 * (n % 2) + 4 * i].unsqueeze(2), [128, 4, 128])
                                tt(V, ST[:, i, s], ST[:, i, s - 1], glb, ALU.mult)
                                tk = tt(V, ST[:, i, s], ST[:, i, s], v4(banks[k][:, :], 4), ALU.add, tp)
                            else:
                                tk = copy(V, ST[:, i, 0], v4(banks[k][:, :], 4), tp)
                            tS[i, s + 1] = tk
                            put(k, tk)
                    yield N["scan"] if s < N["held"] else 0
                O = zone(ZTOK, 1024).rearrange("p (t h d) -> p t h d", t=2, h=4)
                t5 = zone(ZAT + 1024, 512)
                for t in range(2):
                    k = get()
                    for h in range(4):
                        for i in range(2):
                            tp = mm(banks[k][:, 128 * h:128 * h + 128], dT[:, i, t, h, :], BU[:, i, t, h, :], i == 0, i == 1,
                                    [tvn[i, 2 * t], tvn[i, 2 * t + 1]], tqkT, bank_after[k], inc=(h == 3 and i == 1))
                    to = copy(V, O[:, t], v4(banks[k][:, :], 4), tp)
                    put(k, to)
                    for i in range(2):
                        hs = [h2 for h2 in range(2) if (2 * t + h2 if i == 0 else 3 - 2 * t - h2) > 0]
                        k = get()
                        for h2 in hs:
                            n = 2 * t + h2
                            s = n if i == 0 else 3 - n
                            for h in range(4):
                                pp = slice(64 * h2, 64 * h2 + 64)
                                tp = mm(banks[k][pp, 128 * h:128 * h + 128],
                                        kqT[:, h, 256 + 128 * t + 64 * h2:256 + 128 * t + 64 * h2 + 64],
                                        ST[:, i, s - 1, h, :], True, True, tS[i, s], bank_after[k], inc=(h == 3))
                        pp = slice(64 * hs[0], 64 * hs[-1] + 64)
                        npp = 64 * len(hs)
                        tk = tt(V, v4(t5[pp, :], 4), v4(banks[k][pp, :], 4),
                                bc(E[pp, t, 4 * i:4 * i + 4].unsqueeze(2), [npp, 4, 128]), ALU.mult, tp)
                        put(k, tk)
                        to = tt(V, O[pp, t], O[pp, t], v4(t5[pp, :], 4), ALU.add)
                    yield
                st["o"] = to

            def branch(w, tw, y, ty, f):
                k = get()
                for j in range(2):
                    for c in range(4):
                        tp = mm(banks[k][:, 256 * j:256 * j + 256], w[:, c, 128 * (f + j):128 * (f + j) + 128], y[:, c, :],
                                c == 0, c == 3, tw, ty, bank_after[k], inc=(j == 1 and c == 3))
                return k, tp
            mA = v4(zone(Z1 + 2048, 2048), 8)

            def branch_a():
                ia, wa, twa = take()
                for f in range(0, 8, 2):
                    k, tp = branch(wa, twa, yaT, st["ya"], f)
                    if f == 6:
                        release(ia, tp)
                    yield
                    st["mA"] = stt(mA[:, f:f + 2, :], gT[:, f:f + 2, :], 1.0, v4(banks[k][:, :], 2), ALU.add, ALU.mult, tp,
                                   st["gates"], st["XTread"])
                    put(k, st["mA"])
                yield

            def filler():
                yield from proj_dn()
                yield from gates()
                st["gates_done"] = True
                while "XTread" not in st:
                    yield
                yield from branch_a()
            fl = filler()
            interleave(fl, attn_a(), delta())
            O = zone(ZTOK, 1024).rearrange("p (t h d) -> p t h d", t=2, h=4)
            hn = head_norm(O, zone(ZTOK + 1024, 1024), st["o"], pcol(pl["og"]), 0.5, zT, ybT, st["gates"])
            next(hn)
            for _ in fl:
                pass
            st["yb"] = next(hn)

            gt1 = S(8)
            tm = ts(V, gt1, modT[:, 16:24], 0.5, None, ALU.mult, ALU.bypass, tmod[0])
            dg1 = zone(ZAT + 1024, 1024)
            tdg = diags(dg1, gt1, st["yb"])
            mT = v4(zone(ZLT, 2048), 8)
            ib, wb, twb = take()
            tmpz = [v4(zone(ZAT + 512 * i, 512), 2) for i in range(2)]
            for f in range(0, 8, 2):
                k, tp = branch(wb, twb, ybT, st["yb"], f)
                t2 = tmpz[f // 2 % 2]
                tk = stt(t2, gT[:, 8 + f:10 + f, :], 1.0, v4(banks[k][:, :], 2), ALU.add, ALU.mult, tp)
                put(k, tk)
                tmg = tt(V, mT[:, f:f + 2, :], mA[:, f:f + 2, :], t2, ALU.add)
            release(ib, tp)
            gtB = zone(ZDT, 1024)
            tg = spread(gtB, dg1, tdg)
            t_merged = [tmg, (P.sem, P.n)]
            hs, h1s, wsp, aux = split_mem(l)

            def early():
                A.wait(t_merged)
                V.wait(t_merged)
                for g in range(3):
                    split_at(g)

            gtM = xn[:, 1024:2048]
            used_w = {}
            cut = {}
            held = [None]
            ads = []

            def ada_next(j):
                nonlocal ads
                for q in ads:
                    tmod[0] = ada_pe(q)
                ads = [ada_v(1, j, aux)] if l == 0 and j is not None else []

            def split(g, view):
                if g % 4 == 0:
                    held[0] = take()
                i, w, tw = held[0]
                src = view(w, g % 4)
                hi, lo = wsp[g % 3]
                if len(src.shape) == 3:
                    hi, lo = v4(hi, src.shape[1]), v4(lo, src.shape[1])
                ta = copy(A, hi, src, tw, used_w.get(g - 3))
                tv = tt(V, lo, src, hi, ALU.subtract, ta)
                cut[g] = (hi, lo, tv)
                if g % 4 == 3:
                    release(i, tv)

            def view1(w, q):
                return w[:, :, 128 * q:128 * q + 128]

            def view2(w, q):
                return w[:, q, :]

            def parts(cp, tev, thi, tlo):
                te, tmp = tev[cp]
                d = slice(2 * cp, 2 * cp + 2)
                thi.append(copy(A, hs[0][:, d, :], v4(tmp, 2), te))
                tlo.append(tt(V, hs[1][:, d, :], v4(tmp, 2), hs[0][:, d, :], ALU.subtract, thi[-1], te))

            def split_at(g):
                if g < 32:
                    if g and g % 4 == 0:
                        ada_next(g // 4 - 1)
                    split(g, view1)
                elif g < 64:
                    if g % 4 == 0:
                        q = g // 4 - 8
                        ada_next(7 if q == 0 else 7 + q if q <= 4 else None)
                    split(g, view2)
            tsa = ts(V, sbs[l][:, :], modT[:, 32:40], 1.0, None, ALU.add, ALU.bypass)
            sa2 = sbs[l]
            tsa = tt(V, sa2[:, :], sa2[:, :], pcol(pl["n2"], 8), ALU.mult)
            acc_out(mT, tmg, 2, gtB, None, early, [tg])
            A.wait([G.last])
            D = xn[:, 0:256]
            td = norm_diag(D)
            thi, tlo, tev = [], [], {}
            for g in range(3, 3):
                split_at(g)
            for cp in range(4):
                tmp = aux[:, 512 * (cp % 2):512 * (cp % 2) + 512]
                k, tp = turn(cp, D, td)
                for j in range(2):
                    cc = 2 * cp + j
                    o_, i_ = tmp[:, 256 * j:256 * j + 256], banks[k][:, 256 * j:256 * j + 256]
                    if cp % 2:
                        te = act(o_, i_, ACT.Identity, tp, tsa, tm, V.last, scale=sa2[:, cc:cc + 1], bias=modT[:, 24 + cc:25 + cc])
                    else:
                        te = ts(V, o_, i_, sa2[:, cc:cc + 1], modT[:, 24 + cc:25 + cc], ALU.mult, ALU.add, tp, tsa, tm)
                put(k, te)
                tev[cp] = (te, tmp)
                if cp:
                    parts(cp - 1, tev, thi, tlo)
            parts(3, tev, thi, tlo)
            tsq, th1 = {}, []
            for g in range(32):
                if g % 2 == 0:
                    k = get()
                hi, lo, tv = cut[g]
                o = banks[k][:, 256 * (g % 2):256 * (g % 2) + 256]
                n = 0
                for wpart, hpart, tp_ in ((hi, hs[0], thi), (lo, hs[0], thi), (hi, hs[1], tlo)):
                    for c in range(8):
                        tp = mm(o, wpart[:, c, :], hpart[:, c, :], n == 0, n == 23, tv, tp_[c // 2], bank_after[k], inc=(n == 23))
                        n += 1
                used_w[g] = tp
                split_at(g + 3)
                if g % 2:
                    p_ = g // 2
                    sq = v4(xn[:, 512 * (p_ % 2):512 * (p_ % 2) + 512], 2)
                    b = v4(banks[k][:, :], 2)
                    te = act(sq, b, ACT.Relu, tp, tsq.get(p_ - 2))
                    put(k, te)
                    te = tt(V, sq, sq, sq, ALU.mult, te)
                    d = slice(2 * p_, 2 * p_ + 2)
                    te = copy(A, h1s[0][:, d, :], sq, te)
                    tsq[p_] = tt(V, h1s[1][:, d, :], sq, h1s[0][:, d, :], ALU.subtract, te)
                    th1.append(tsq[p_])
            tdg = diags(xn[:, 0:1024], modT[:, 40:48])
            ks = [get() for _ in range(4)]
            tps = [None] * 4

            def down_(g, t, h, last):
                hi, lo, tv = cut[g]
                f = g - 32
                k = ks[2 * t + h]
                for q, (hp, wp) in enumerate(((0, hi), (0, lo), (1, hi))):
                    tp = mm(banks[k][:, :], h1s[hp][:, f, 128 * t:128 * t + 128], wp[:, 512 * h:512 * h + 512],
                            f == 0 and q == 0, f == 31 and q == 2, tv, th1[f // 2], bank_after[k], inc=(last and q == 2))
                return tp
            for g in range(32, 61):
                for t in range(2):
                    for h in range(2):
                        tp = down_(g, t, h, t == 1 and h == 1)
                used_w[g] = tp
                split_at(g + 3)
                if g == 34:
                    tg = spread(gtM, xn[:, 0:1024], tdg)
            ada_next(None)
            for t in range(2):
                for h in range(2):
                    for g in range(61, 64):
                        tps[2 * t + h] = down_(g, t, h, g == 63)
            out_add(ks, tps, gtM, [tg])
            arena()
            A.wait([V.last])
            V.wait([A.last])

        def acc_out(lhs, tl, nb, gB, hook=None, before=None, toks=[]):
            ks = [get() for _ in range(4)]
            tps = [None] * 4
            for b in range(nb):
                i, w, tw = take()
                end = b == nb - 1
                order = [(t, h, c) for t in range(2) for h in range(2) for c in range(4)] if end else \
                    [(t, h, c) for c in range(4) for t in range(2) for h in range(2)]
                for n, (t, h, c) in enumerate(order):
                    k = ks[2 * t + h]
                    tp = mm(banks[k][:, :], lhs[:, 4 * b + c, 128 * t:128 * t + 128], w[:, c, 512 * h:512 * h + 512],
                            b == 0 and c == 0, end and c == 3, part(tl, 4 * b + c), tw, bank_after[k],
                            inc=(n == 15 or (end and c == 3)))
                    if end and c == 3:
                        tps[2 * t + h] = tp
                release(i, tp)
                if hook is not None:
                    hook(b)
            if before is not None:
                before()
            out_add(ks, tps, gB, toks)

        def out_add(ks, tps, gB, toks):
            for t in range(2):
                for h in range(2):
                    k = ks[2 * t + h]
                    xs = x3[:, t, 512 * h:512 * h + 512]
                    if gB is not None:
                        tmp = xn[:, 0:512]
                        tk = tt(V, tmp, banks[k][:, :], gB[:, 512 * h:512 * h + 512], ALU.mult, tps[2 * t + h], toks)
                        xr[0] = tt(V, xs, xs, tmp, ALU.add)
                    else:
                        tk = xr[0] = tt(V, xs, xs, banks[k][:, :], ALU.add, tps[2 * t + h])
                    put(k, tk)
                    square(t, h, xr[0])

        def square(t, h, tk):
            xsq[0] = act(xn[:, 512:1024], x3[:, t, 512 * h:512 * h + 512], ACT.Square, tk,
                         accum=sq4[:, 2 * t + h:2 * t + h + 1])

        def out_proj(mT, tmg, gB):
            acc_out(mT, tmg, 2, gB)

        def block2(l):
            pl = pc[l]
            nab = zone(11840, 2048).rearrange("p (t h r c) -> p t h r c", t=2, h=4, r=4)
            raw = xn[:, :].rearrange("p (t h r c) -> p t h r c", t=2, h=4, r=4)
            tb = [None]

            def turned(each):
                th = x_hT(xn[:, 0:256], lambda c: pcol(pl["an"] + c), None, each=each)
                SP.wait([V.last, (P.sem, P.n)])
                for h in range(4):
                    for r in range(4):
                        src = bass.AP(tensor=a["na_rpb_2"].tensor, offset=((l * 4 + h) * 15 + 7 - r) * 31 + 15 - 63,
                                      ap=[[1, 64], [31, 4], [1, 64]])
                        tb[0] = l_b.load(SP, raw[64 * (r % 2):64 * (r % 2) + 64, r // 2, h], src)
                return th
            A.wait([V.last])
            ro[0] = 0
            prw("sink", a["swa_sink_2"][l], 6)
            P2 = zone(0, 3648).rearrange("p (t n) -> p t n", t=2)
            cc = [0]
            tpj = []

            def e3(j, t, b, tp):
                n = b.shape[-1]
                tpj.append(copy(A if t else V, P2[:, t, 512 * (j + 1):512 * (j + 1) + n], b, tp))
                return tpj[-1]
            th = lin3(f"b{l}", turned, [512, 512, 288], e3)
            n3 = zone(11840, 2048).rearrange("p (a c) -> p a c", a=32)
            kf = []
            for q in range(4):
                k = get()
                kf.append((k, mm(banks[k][:, :], K2("flip"), xn[:, 512 * q:512 * q + 512], True, True, tb, t_c2, bank_after[k],
                                 inc=True)))
            i, w, tw = take()
            tpz = []

            def e(t, b, tp):
                tpz.append(copy(A, P2[:, t, 0:512], b, tp))
                return tpz[-1]
            tmp = zone(16960, 1024)
            ss = S(4)
            for t in range(2):
                tk = act(tmp[:, 0:256], P2[:, t, 768:1024], ACT.Square, tpj, V.last, accum=ss[:, t:t + 1])
                tk = act(tmp[:, 0:128], P2[:, t, 1024:1152], ACT.Square, accum=ss[:, 2 + t:3 + t])
            tp = lin_tok(hT3, th, w, tw, 512, 8, e)
            release(i, tp)
            rsqrt(ss[:, 0:2], ss[:, 0:2], 1.0 / 256, tk)
            tk = rsqrt(ss[:, 2:4], ss[:, 2:4], 1.0 / 128)
            for t in range(2):
                ts(V, P2[:, t, 768:1024], P2[:, t, 768:1024], ss[:, t:t + 1], None, ALU.mult, ALU.bypass, tk)
                tn = ts(V, P2[:, t, 1024:1152], P2[:, t, 1024:1152], ss[:, 2 + t:3 + t], None, ALU.mult, ALU.bypass)
            mq = zone(3648, 1152).rearrange("p (t h d) -> p t h d", t=2, h=6)
            mk = zone(4800, 1152).rearrange("p (t h d) -> p t h d", t=2, h=6)
            mv = zone(5952, 768).rearrange("p (t h d) -> p t h d", t=2, h=6)
            ta, tb_ = zone(16960, 512), zone(17472, 512)

            def rot(dst, src, n, d, cs, sn, *after):
                a_, b_ = v4(ta[:, 0:n * d], n), v4(tb_[:, 0:n * d], n)
                hd = d // 2
                tt(V, a_, src, bc(cs, [128, n, d]), ALU.mult, *after)
                for h in range(2):
                    tt(V, b_[:, :, hd * h:hd * h + hd], src[:, :, hd - hd * h:2 * hd - hd * h],
                       bc(sn[:, :, hd * h:hd * h + hd], [128, n, hd]), ALU.mult)
                return dst(a_, b_)
            c32, s32 = v4(K2("cos32"), 2), v4(K2("sin32"), 2)
            c64, s64 = v4(K("cos64"), 2), v4(K("sin64"), 2)
            cro = zone(15936, 1024).rearrange("p (t n) -> p t n", t=2)
            for t in range(2):
                kr = P2[:, t, 1152:1184].unsqueeze(1)
                rot(lambda x_, y_: tt(V, mk[:, t, :, 64:96], bc(x_, [128, 6, 32]), bc(y_, [128, 6, 32]), ALU.add), kr, 1, 32,
                    c32[:, t:t + 1, :], s32[:, t:t + 1, :], t_c2, tpj)

                def put_c(x_, y_, t=t):
                    o = cro[:, t, 0:384].rearrange("p (g v d) -> p v g d", g=3, v=2)
                    xq = x_[:, 0:6, :].rearrange("p (v g) d -> p v g d", v=2)
                    yq = y_[:, 0:6, :].rearrange("p (v g) d -> p v g d", v=2)
                    tt(V, o, xq, yq, ALU.add)
                    return tt(V, v4(cro[:, t, 384:512], 2), x_[:, 6:8, :], y_[:, 6:8, :], ALU.add)
                trc = rot(put_c, v4(P2[:, t, 1184:1696], 8), 8, 64, c64[:, t:t + 1, :], s64[:, t:t + 1, :])
            for q in range(4):
                k, tp = kf[q]
                tk = tt(V, n3[:, 8 * q:8 * q + 8, :], v4(banks[k][:, :], 8), bc(K2("na01").unsqueeze(1), [128, 8, 64]), ALU.mult, tp)
                put(k, tk)
            tnab = tt(V, n3, n3, bc(K2("naneg").unsqueeze(1), [128, 32, 64]), ALU.add)
            cqT = v4(zone(22072, 768), 3)
            tcq = []
            for cp in range(2):
                k = get()
                for j in range(2 if cp == 0 else 1):
                    for t in range(2):
                        c0 = 768 + 128 * (2 * cp + j)
                        tp = tr(banks[k][:, 256 * j + 128 * t:256 * j + 128 * t + 128], P2[:, t, c0:c0 + 128], tn, bank_after[k],
                                inc=True)
                for j in range(2 if cp == 0 else 1):
                    g = pcol(pl["qn"] + j) if cp == 0 else pcol(pl["kn"])
                    te = act(cqT[:, 2 * cp + j, :], banks[k][:, 256 * j:256 * j + 256], ACT.Copy, tp, scale=g)
                put(k, te)
            tcq = te
            i, w, tw = take()
            for t in range(2):
                for s in range(2):
                    k = get()
                    for c in range(2):
                        tp = mm(banks[k][:, 0:288], cqT[:, c, 128 * t:128 * t + 128], w[:, c, 288 * s:288 * s + 288], c == 0, c == 1,
                                tcq, tw, bank_after[k], inc=(c == 1))
                    te = copy(A, mq[:, t, 3 * s:3 * s + 3, :], v4(banks[k][:, 0:288], 3), tp)
                    put(k, te)
            release(i, tp)
            tmq = te
            i, w, tw = take()
            for t in range(2):
                for s in range(2):
                    k = get()
                    tp = mm(banks[k][:, 0:384], cqT[:, 2, 128 * t:128 * t + 128], w[:, 0, 384 * s:384 * s + 384], True, True,
                            tcq, tw, bank_after[k], inc=True)
                    b = v4(banks[k][:, 0:384], 3)
                    copy(V, mk[:, t, 3 * s:3 * s + 3, 0:64], b[:, :, 0:64], tp)
                    te = copy(V, mv[:, t, 3 * s:3 * s + 3, :], b[:, :, 64:128], tp)
                    put(k, te)
            release(i, tp)
            for t in range(2):
                tk = rot(lambda x_, y_: tt(V, mq[:, t, :, 64:96], x_, y_, ALU.add), mq[:, t, :, 64:96], 6, 32,
                         c32[:, t:t + 1, :], s32[:, t:t + 1, :], tmq, t_c2)
            mT = zone(6720, 3072).rearrange("p (h n) -> p h n", h=6)
            cT = v4(zone(9792, 1024), 4)
            aT = v4(zone(10816, 1024), 4)
            tT = []
            n_ = [0]
            for dst, src in ((aT, P2[:, :, 0:512]), (cT, cro)):
                for cp in range(2):
                    k = get()
                    for j in range(2):
                        for t in range(2):
                            c0 = 128 * (2 * cp + j)
                            tp = tr(banks[k][:, 256 * j + 128 * t:256 * j + 128 * t + 128], src[:, t, c0:c0 + 128], trc, tpz,
                                    bank_after[k], inc=(j == 1 and t == 1))
                    te = copy(A if cp % 2 else V, dst[:, 2 * cp:2 * cp + 2, :], v4(banks[k][:, :], 2), tp)
                    put(k, te)
                    tT.append(te)
            for h in range(6):
                k = get()
                for g, src in ((0, mq), (1, mk)):
                    for t in range(2):
                        tp = tr(banks[k][0:96, 256 * g + 128 * t:256 * g + 128 * t + 128], src[:, t, h, :], tk, tmq, bank_after[k],
                                inc=(g == 1 and t == 1))
                te = copy(A if h % 2 else V, mT[0:96, h, :], banks[k][0:96, :], tp)
                put(k, te)
                tT.append(te)
            oc = zone(13888, 2048).rearrange("p (t n) -> p t n", t=2)
            swa = v4(K2("swa"), 2)
            units = []
            for h in range(4):
                pp = slice(64 * (h % 2), 64 * (h % 2) + 64)
                units.append(dict(q=aT[pp, h // 2, :], k=aT[pp, 2 + h // 2, :], bias=nab[:, :, h].rearrange("p t r c -> p t (r c)"),
                                  scale=0.125, sink=None, v=lambda kt, h=h: P2[:, kt, 512 + 64 * h:576 + 64 * h], o=64 * h))
            for h in range(6):
                units.append(dict(q=mT[0:96, h, 0:256], k=mT[0:96, h, 256:512], bias=None, scale=96 ** -0.5, sink=None,
                                  v=lambda kt, h=h: mv[:, kt, h, :], o=256 + 64 * h))
            for h in range(6):
                kv, g = h // 3, h % 3
                pp = slice(64 * kv, 64 * kv + 64)
                units.append(dict(q=cT[pp, g, :], k=cT[pp, 3, :], bias=swa, scale=0.125, sink=rows[:, h:h + 1],
                                  v=lambda kt, kv=kv: P2[:, kt, 1696 + 64 * kv:1760 + 64 * kv], o=640 + 64 * h))
            sc = [zone(19000 + 512 * i, 512) for i in range(6)]
            grp = ((0, 256), (256, 384), (640, 384))
            gth, gtok = [], {}

            def g_square(g, to):
                o0, n = grp[g]
                gss = S(2)
                for t in range(2):
                    tk = act(tmp[:, 0:n], oc[:, t, o0:o0 + n], ACT.Square, to, accum=gss[:, t:t + 1])
                return gss, tk

            def g_scale(g, st_):
                o0, n = grp[g]
                gss, tk = st_
                tk = rsqrt(gss, gss, 1.0 / n, tk)
                for t in range(2):
                    tk = ts(V, oc[:, t, o0:o0 + n], oc[:, t, o0:o0 + n], gss[:, t:t + 1], None, ALU.mult, ALU.bypass)
                return tk

            def g_turn(cp, tk):
                k = get()
                for j in range(2):
                    for t in range(2):
                        cc = 2 * cp + j
                        tp = tr(banks[k][:, 256 * j + 128 * t:256 * j + 128 * t + 128], oc[:, t, 128 * cc:128 * cc + 128], tk,
                                bank_after[k], inc=(j == 1 and t == 1))
                for j in range(2):
                    cc = 2 * cp + j
                    i = banks[k][:, 256 * j:256 * j + 256]
                    te = act(hT3[:, cc, :], i, ACT.Copy, tp, scale=pcol(pl["gn"] + cc)) if cp % 2 else \
                        ts(V, hT3[:, cc, :], i, pcol(pl["gn"] + cc), None, ALU.mult, ALU.bypass, tp)
                put(k, te)
                gth.append(te)

            def group_step(q, to):
                for g, q0 in ((0, 3), (1, 9)):
                    if q == q0:
                        gtok[g] = g_square(g, to)
                    if q == q0 + 1:
                        gtok[g] = g_scale(g, gtok[g])
                    if q == q0 + 3:
                        g_turn(g, gtok[g])
            res = {}
            V.wait([rc["sink"][1]])
            A.wait([rc["sink"][1]])
            for s in range(len(units) + 2):
                if s < len(units):
                    u = units[s]
                    b = s % 2
                    e3, r, te, tr2 = softmax_pair([tT, res.get(("T", s - 2))], u["k"], u["q"], u["bias"], u["scale"], sc[b], sc[2 + b], u["sink"])
                    if s >= 2:
                        pass
                    res[s] = (e3, r, te, tr2)
                if 1 <= s <= len(units):
                    q = s - 1
                    e3, r, te, tr2 = res[q]
                    tk, ptr = probs_T(e3, te, sc[4 + q % 2], A, res.get(("P", q - 2)))
                    A.wait([ptr])
                    res["T", q] = ptr
                    res["tk", q] = tk
                if s >= 2:
                    q = s - 2
                    u = units[q]
                    e3, r, te, tr2 = res[q]
                    k, tp = pv(sc[4 + q % 2], res["tk", q], u["v"], 64, [te, tpj, tpz])
                    res["P", q] = tp
                    to = tt(V, oc[:, :, u["o"]:u["o"] + 64], v4(banks[k][:, 0:128], 2), bc(r.unsqueeze(2), [128, 2, 64]), ALU.mult, tp, tr2)
                    put(k, to)
                    group_step(q, to)
            tg2 = g_scale(2, g_square(2, to))
            for cp in (2, 3):
                g_turn(cp, tg2)
            out_proj(hT3, gth, None)

            used["more", l] = [(P.sem, P.n), V.last, A.last]
            issue()
            th = x_hT(zone(22528, 256), lambda c: pcol(pl["fn"] + c), None)
            for t in range(2):
                txn = ts(V, xn[:, 1024 * t:1024 * t + 1024], x3[:, t, :], rstd[:, t:t + 1], None, ALU.mult, ALU.bypass, xsq[0])
            i, w, tw = take()
            k = get()
            for t in range(2):
                for c in range(8):
                    tp = mm(banks[k][:, 16 * t:16 * t + 16], hT3[:, c, 128 * t:128 * t + 128], w[:, c, :], c == 0, c == 7,
                            part(th, c), tw, bank_after[k], inc=(c == 7))
            release(i, tp)
            aff = zone(17408, 32).rearrange("p (t n) -> p t n", t=2)
            sel = zone(17440, 32).rearrange("p (t n) -> p t n", t=2)
            lg = v4(banks[k][:, 0:32], 2)
            mx, smv = S(2), S(2)
            V(lambda e: e.tensor_reduce(mx, lg, AX.X, ALU.max), tp)
            tk = tt(V, aff, lg, bc(mx.unsqueeze(2), [128, 2, 16]), ALU.subtract)
            put(k, tk)
            tk = act(aff, aff, ACT.Exp, tk)
            V(lambda e: e.tensor_reduce(smv, aff, AX.X, ALU.add), tk)
            V(lambda e: e.reciprocal(smv, smv))
            taff = tt(V, aff, aff, bc(smv.unsqueeze(2), [128, 2, 16]), ALU.mult)
            k = get()
            for t in range(2):
                tp = tr(banks[k][0:16, 128 * t:128 * t + 128], aff[:, t, :], taff, bank_after[k], inc=True)
            w0 = zone(17472, 256)[0:16, :]
            w1 = zone(17728, 256)[0:16, :]
            m8 = zone(17984, 8)[0:16, :]
            tk = copy(V, w0, banks[k][0:16, 0:256], tp)
            put(k, tk)
            ws = [w0, w1]
            for r in range(4):
                s_, d_ = ws[r % 2], ws[1 - r % 2]
                V(lambda e: e.max(m8, s_))
                V(lambda e: e.match_replace(d_, m8, s_, -1.0))
            tk = ts(V, w1, w0, 0.0, None, ALU.is_lt, ALU.bypass)
            k = get()
            for t in range(2):
                tp = tr(banks[k][:, 16 * t:16 * t + 16], w1[:, 128 * t:128 * t + 128], tk, bank_after[k], inc=True)
            tsel = copy(V, sel, v4(banks[k][:, 0:32], 2), tp)
            put(k, tsel)
            k = get()
            mm(banks[k][:, 0:16], K2("triA"), sel[:, 0, :], True, True, tsel, bank_after[k])
            mm(banks[k][:, 16:32], K("ones"), sel[:, 0, :], True, False)
            tp = mm(banks[k][:, 16:32], K2("triA"), sel[:, 1, :], False, True, inc=True)
            pm = S(32)
            pm3 = v4(pm, 2)
            tk = tt(V, pm3, v4(banks[k][:, 0:32], 2), sel, ALU.mult, tp)
            put(k, tk)
            ts(V, pm, pm, -1.0, None, ALU.add, ALU.bypass)
            Pm = zone(0, 1024).rearrange("p (t e s) -> p t e s", t=2, e=16)
            PA = zone(1024, 4096).rearrange("p (t e r s) -> p t e r s", t=2, e=16, r=4)
            for t in range(2):
                tPm = tt(V, Pm[:, t], bc(K2("iota").unsqueeze(1), [128, 16, 32]), bc(pm3[:, t, :].unsqueeze(2), [128, 16, 32]), ALU.is_equal)
            xs = v4(zone(9216, 4096), 8)
            txs = {}

            def gather(c, e0, n, k, o):
                for t in range(2):
                    tp = mm(banks[k][:, o:o + 32 * n], xn[:, 1024 * t + 128 * c:1024 * t + 128 * c + 128],
                            Pm[:, t, e0:e0 + n].rearrange("p e s -> p (e s)"), t == 0, t == 1, tPm, txn, bank_after[k], inc=(t == 1))
                return tp

            def gathered(c, e0, n, k, o, q, tp):
                g = pcol(pl["fn"] + c)
                dst, src = xs[:, c, 32 * e0:32 * e0 + 32 * n], banks[k][:, o:o + 32 * n]
                if q is A:
                    return act(dst, src, ACT.Copy, tp, scale=g)
                return ts(V, dst, src, g, None, ALU.mult, ALU.bypass, tp)
            for h in range(2):
                k = get()
                for c in range(4 * h, 4 * h + 4):
                    tp = gather(c, 0, 4, k, 128 * (c % 4))
                for c in range(4 * h, 4 * h + 4):
                    te = gathered(c, 0, 4, k, 128 * (c % 4), A if h else V, tp)
                put(k, te)
                txs[0, h] = te
            PW = zone(5120, 4096).rearrange("p (g n) -> p g n", g=16)
            tpw = []

            def rest():
                for t in range(2):
                    for r in range(4):
                        tPA = tt(V, PA[:, t, :, r, :], Pm[:, t], bc(aff[:, t, :].unsqueeze(2), [128, 16, 32]), ALU.mult)
                for c in range(8):
                    k = get()
                    txs[1, c % 2] = gathered(c, 4, 12, k, 0, A if c % 2 else V, gather(c, 4, 12, k, 0))
                    put(k, txs[1, c % 2])
                for gp in range(8):
                    k = get()
                    for j in range(2):
                        for t in range(2):
                            src = PA[:, t, 2 * gp + j].rearrange("p r s -> p (r s)")
                            tp = tr(banks[k][:, 256 * j + 128 * t:256 * j + 128 * t + 128], src, tPA, bank_after[k],
                                    inc=(j == 1 and t == 1))
                    te = copy(A if gp % 2 else V, PW[:, 2 * gp:2 * gp + 2, :], v4(banks[k][:, :], 2), tp)
                    put(k, te)
                    tpw.append(te)
            hid = [zone(13312 + 256 * b, 256).rearrange("p (c b s) -> p c b s", c=4, b=2) for b in range(2)]
            sg = [zone(13824 + 256 * b, 256).rearrange("p (c s) -> p c s", c=4) for b in range(2)]
            gs = [zone(14336 + 512 * b, 512) for b in range(2)]
            Ys = [v4(zone(15360 + 1024 * b, 1024), 2) for b in range(2)]
            thid, tdn, ttr, tY, tsc = {}, {}, {}, {}, {}
            acc4 = []

            def gate_up(e_):
                k = get()
                for s_ in range(4):
                    i, w, tw = take()
                    for c2 in range(2):
                        for q in range(4):
                            tp = mm(banks[k][32 * q:32 * q + 32, :], xs[:, 2 * s_ + c2, 32 * e_:32 * e_ + 32],
                                    w[:, 2 * (q // 2) + c2, 512 * (q % 2):512 * (q % 2) + 512], s_ == 0 and c2 == 0,
                                    s_ == 3 and c2 == 1, tw, [txs[e_ > 3, 0], txs[e_ > 3, 1]], bank_after[k], inc=(c2 == 1 and q == 3))
                    release(i, tp)
                tk = copy(A, gs[e_ % 2], banks[k][:, :], tp, ttr.get(e_ - 2))
                put(k, tk)
                return tk

            def hidden(e_, tk):
                k = get()
                for c in range(4):
                    tp = tr(banks[k][:, 128 * c:128 * c + 128], gs[e_ % 2][:, 128 * c:128 * c + 128], tk, bank_after[k], inc=(c == 3))
                ttr[e_] = tp
                b4 = v4(banks[k][:, :], 4)
                g_, u_, s_ = b4[:, :, 0:64], b4[:, :, 64:128], sg[e_ % 2]
                te = act(s_, g_, ACT.Tanh, tp, scale=0.5)
                stt(s_, s_, 1.0, g_, ALU.add, ALU.mult, te)
                thid[e_] = stt(hid[e_ % 2].rearrange("p c b s -> p c (b s)"), s_, 0.5, u_, ALU.mult, ALU.mult, tdn.get(e_ - 2))
                put(k, thid[e_])

            def down(q):
                yk = [get(), get()]
                for b in range(2):
                    i, w, tw = take()
                    for hf in range(2):
                        for j in range(4):
                            tp = mm(banks[yk[hf]][32 * j:32 * j + 32, :], hid[q % 2][:, j, b, :], w[:, j, 512 * hf:512 * hf + 512],
                                    b == 0, b == 1, tw, thid[q], bank_after[yk[hf]], inc=(hf == 1 and j == 3))
                    release(i, tp)
                tdn[q] = tp
                tY[q] = []
                for hf in range(2):
                    te = copy(A if hf else V, Ys[q % 2][:, hf, :], banks[yk[hf]][:, :], tp, tsc.get(q - 2))
                    put(yk[hf], te)
                    tY[q].append(te)

            def scatter(q):
                for t in range(2):
                    for hf in range(2):
                        k = acc4[t][hf]
                        tp = mm(banks[k][:, :], PW[:, q, 128 * t:128 * t + 128], Ys[q % 2][:, hf, :], q == 0, q == 15,
                                tpw, tY[q], bank_after[k], inc=(t == 1 and hf == 1))
                tsc[q] = tp

            for s_ in range(18):
                if s_ < 16:
                    tk = gate_up(s_)
                if 2 <= s_:
                    scatter(s_ - 2)
                if 1 <= s_ <= 16:
                    down(s_ - 1)
                if s_ < 16:
                    hidden(s_, tk)
                if s_ == 0:
                    rest()
                    acc4 += [[get(), get()], [get(), get()]]
            for t in range(2):
                for hf in range(2):
                    k = acc4[t][hf]
                    xs_ = x3[:, t, 512 * hf:512 * hf + 512]
                    xr[0] = tt(V, xs_, xs_, banks[k][:, :], ALU.add, tsc[15])
                    put(k, xr[0])
                    square(t, hf, xr[0])

        l_b = Landing()
        for t in range(2):
            for h in range(2):
                square(t, h, t_x)
        for l in range(2):
            block1(l)
        A.wait([V.last, (P.sem, P.n)])
        l_c2 = Landing()
        c2t = ar
        t_c2 = l_c2.load(A, ar[:, C2B:AR], a["c2"])
        for l in range(2):
            block2(l)
        fg = zone(0, 1024)
        A.wait([V.last, (P.sem, P.n)])
        tf = l_r.load(A, fg, a["final_norm_2"].partition_broadcast(128))
        tk = normed()
        l_o = Landing()
        for t in range(2):
            tk = tt(V, xn[:, 1024 * t:1024 * t + 1024], xn[:, 1024 * t:1024 * t + 1024], fg, ALU.mult, tf)
        to = l_o.load(SP, out[0].rearrange("(t p) d -> p t d", p=128), xn[:, :].rearrange("p (t d) -> p t d", t=2), tk)
        SP.wait([to])
        assert nxt[0] == len(blocks)


_INS = ['x', 'c', 'ada_w', 'ada_b', 'norm1_g', 'norm2_g', 'w_in', 'dn_conv', 'dn_A_log', 'dn_dt_bias', 'dn_out_gain',
        'qk_norm_gain', 'diff_lambda', 'diff_subln_gain', 'w_branch_a', 'w_branch_b', 'w_out', 'w_mlp1', 'w_mlp2',
        'attn_norm_2', 'w_in_2', 'na_rpb_2', 'mla_q_norm_2', 'mla_w_uq_2', 'mla_kv_norm_2', 'mla_w_ukv_2', 'swa_sink_2',
        'group_norm_2', 'w_out_2', 'ffn_norm_2', 'w_router_2', 'w_gate_2', 'w_up_2', 'w_down_2', 'final_norm_2']


def kernel(**inputs):
    import numpy as _np
    import concourse.bacc as _bacc
    from concourse import mybir as _mybir
    from concourse.bass_utils import run_bass_kernel_spmd as _run

    nc = _bacc.Bacc("TRN2", target_bir_lowering=False, num_devices=1)
    (o1, c1), (o2, c2) = const_arrays()
    arrays, aps = {}, {}
    for name in _INS:
        v = _np.ascontiguousarray(inputs[name])
        arrays[f"in_{name}_dram"] = v
        aps[name] = nc.dram_tensor(f"in_{name}_dram", v.shape, _mybir.dt.from_np(v.dtype), kind="ExternalInput").ap()
    for name, v in (("c1", c1), ("c2", c2)):
        arrays[f"in_{name}_dram"] = v
        aps[name] = nc.dram_tensor(f"in_{name}_dram", v.shape, _mybir.dt.from_np(v.dtype), kind="ExternalInput").ap()
    out = nc.dram_tensor("out_0_dram", (1, 256, 1024), F32, kind="ExternalOutput").ap()
    program(nc, aps, o1, o2, out)
    r = _run(nc, [arrays], core_ids=[0])
    return r.results[0]["out_0_dram"]
```
